# Optimizing a Trainium2 kernel written in Bass

```python
import math
import jax, jax.numpy as jnp
from jax import lax
import numpy as np

D_MODEL = 1024
BATCH = 1
SEQ = 512
DEPTH = 2

HEAD_DIM = 64
BLOCK = 128
A_HEADS = 8
A_KV = 2
WINDOW = 128
B_HEADS = 8
B_KV = 2
GRID_W = 64
C_WIDTH = 512
C_GROUPS = 4
C_GROUP_DIM = C_WIDTH // C_GROUPS
CHUNK = 128
N_BRANCH = 3
BRANCH_WIDTH = 512
ROPE_THETA = 10000.0
MEM_LEN = 256
X_HEADS = 4
X_HEAD_DIM = 128
X_WIDTH = X_HEADS * X_HEAD_DIM
D_FF = 2816
CONV_W = 3
ALPHA = (2 * DEPTH) ** 0.25
BETA = (8 * DEPTH) ** -0.25
LN_EPS = 1e-5
RMS_EPS = 1e-6

A_Q_W = A_HEADS * HEAD_DIM
A_KV_W = A_KV * HEAD_DIM
B_Q_W = B_HEADS * HEAD_DIM
B_KV_W = B_KV * HEAD_DIM
IN_SIZES = (A_Q_W, A_KV_W, A_KV_W, B_Q_W, B_KV_W, B_KV_W, 2 * C_WIDTH, N_BRANCH * D_MODEL)
D_IN = sum(IN_SIZES)


def _split_points(sizes):
    pts, acc = [], 0
    for s in sizes[:-1]:
        acc += s
        pts.append(acc)
    return pts

def layer_norm(x, g, b):
    xf = x.astype(jnp.float32)
    mu = jnp.mean(xf, axis=-1, keepdims=True)
    var = jnp.mean(jnp.square(xf - mu), axis=-1, keepdims=True)
    y = (xf - mu) * lax.rsqrt(var + LN_EPS) * g.astype(jnp.float32) + b.astype(jnp.float32)
    return y.astype(x.dtype)

def rms_norm(x, g):
    xf = x.astype(jnp.float32)
    y = xf * lax.rsqrt(jnp.mean(jnp.square(xf), axis=-1, keepdims=True) + RMS_EPS)
    return (y * g.astype(jnp.float32)).astype(x.dtype)

def rope(x, pos, theta):
    d = x.shape[-1]
    half = d // 2
    inv = theta ** (-jnp.arange(half, dtype=jnp.float32) * (2.0 / d))
    ang = pos.astype(jnp.float32)[:, None] * inv[None, :]
    cos = jnp.cos(ang)[:, None, :]
    sin = jnp.sin(ang)[:, None, :]
    x1 = x[..., :half].astype(jnp.float32)
    x2 = x[..., half:].astype(jnp.float32)
    out = jnp.concatenate([x1 * cos - x2 * sin, x2 * cos + x1 * sin], axis=-1)
    return out.astype(x.dtype)

def window_attention(q, k, v, sink):
    B, S, H, D = q.shape
    KV = k.shape[2]
    G = H // KV
    nb = S // BLOCK
    qb = q.reshape(B, nb, BLOCK, KV, G, D)
    pad = ((0, 0), (BLOCK, BLOCK), (0, 0), (0, 0))
    kp = jnp.pad(k, pad).reshape(B, nb + 2, BLOCK, KV, D)
    vp = jnp.pad(v, pad).reshape(B, nb + 2, BLOCK, KV, D)
    kw = jnp.concatenate([kp[:, :-2], kp[:, 1:-1], kp[:, 2:]], axis=2)
    vw = jnp.concatenate([vp[:, :-2], vp[:, 1:-1], vp[:, 2:]], axis=2)
    s = jnp.einsum('bnqkgd,bnskd->bnkgqs', qb, kw).astype(jnp.float32) / math.sqrt(D)
    blk = jnp.arange(nb, dtype=jnp.int32)[:, None]
    qpos = blk * BLOCK + jnp.arange(BLOCK, dtype=jnp.int32)[None, :]
    kpos = (blk - 1) * BLOCK + jnp.arange(3 * BLOCK, dtype=jnp.int32)[None, :]
    dist = jnp.abs(qpos[:, :, None] - kpos[:, None, :])
    valid = (dist <= WINDOW) & (kpos[:, None, :] >= 0) & (kpos[:, None, :] < S)
    s = jnp.where(valid[None, :, None, None], s, -jnp.inf)
    sink_l = jnp.broadcast_to(sink.astype(jnp.float32).reshape(KV, G)[None, None, :, :, None, None],
                              s.shape[:-1] + (1,))
    p = jax.nn.softmax(jnp.concatenate([s, sink_l], axis=-1), axis=-1)[..., :-1]
    o = jnp.einsum('bnkgqs,bnskd->bnqkgd', p.astype(v.dtype), vw)
    return o.reshape(B, S, H * D)

def dense_block_attention(q, k, v):
    B, S, H, D = q.shape
    KV = k.shape[2]
    G = H // KV
    nb = S // BLOCK
    scale = 1.0 / math.sqrt(D)
    qb = q.reshape(B, nb, BLOCK, KV, G, D).transpose(1, 0, 2, 3, 4, 5)

    def one_block(qblk):
        s = jnp.einsum('bqkgd,bskd->bkgqs', qblk, k).astype(jnp.float32) * scale
        p = jax.nn.softmax(s, axis=-1)
        return jnp.einsum('bkgqs,bskd->bqkgd', p.astype(v.dtype), v)

    o = lax.map(one_block, qb)
    return o.transpose(1, 0, 2, 3, 4, 5).reshape(B, S, H * D)

def spatial_gating(u, v, ln_g, ln_b, w_s, b_s):
    B, S, _ = v.shape
    nc = S // CHUNK
    vc = layer_norm(v, ln_g, ln_b).reshape(B, nc, CHUNK, C_GROUPS, C_GROUP_DIM)
    mixed = jnp.einsum('gij,bnjgc->bnigc', w_s, vc) + b_s.T[None, None, :, :, None]
    return u * mixed.reshape(B, S, C_WIDTH)

def hybrid_mixer(x, pos, row, col, w_in, b_gate, a_sink, b_q_gain, b_k_gain,
                 c_ln_g, c_ln_b, c_ws, c_bs, w_branch, w_mix_out):
    B, S, _ = x.shape
    proj = x @ w_in
    aq, ak, av, bq, bk, bv, cz, gate = jnp.split(proj, _split_points(IN_SIZES), axis=-1)
    aq = rope(aq.reshape(B, S, A_HEADS, HEAD_DIM), pos, ROPE_THETA)
    ak = rope(ak.reshape(B, S, A_KV, HEAD_DIM), pos, ROPE_THETA)
    av = av.reshape(B, S, A_KV, HEAD_DIM)
    out_a = window_attention(aq, ak, av, a_sink)
    half = HEAD_DIM // 2
    bq = rms_norm(bq.reshape(B, S, B_HEADS, HEAD_DIM), b_q_gain)
    bk = rms_norm(bk.reshape(B, S, B_KV, HEAD_DIM), b_k_gain)
    bq = jnp.concatenate([rope(bq[..., :half], row, ROPE_THETA), rope(bq[..., half:], col, ROPE_THETA)], axis=-1)
    bk = jnp.concatenate([rope(bk[..., :half], row, ROPE_THETA), rope(bk[..., half:], col, ROPE_THETA)], axis=-1)
    bv = bv.reshape(B, S, B_KV, HEAD_DIM)
    out_b = dense_block_attention(bq, bk, bv)
    u, v = jnp.split(jax.nn.gelu(cz, approximate=False), 2, axis=-1)
    out_c = spatial_gating(u, v, c_ln_g, c_ln_b, c_ws, c_bs)
    branches = jnp.stack([out_a, out_b, out_c], axis=2)
    gates = jax.nn.sigmoid(gate + b_gate).reshape(B, S, N_BRANCH, D_MODEL)
    merged = (jnp.einsum('bsnc,ncd->bsnd', branches, w_branch) * gates).sum(axis=2)
    return merged @ w_mix_out

def memory_cross_attention(x, mem, wq, wkv, wo):
    B, S, _ = x.shape
    M = mem.shape[1]
    q = (x @ wq).reshape(B, S, X_HEADS, X_HEAD_DIM)
    k, v = jnp.split(mem @ wkv, 2, axis=-1)
    k = k.reshape(B, M, X_HEADS, X_HEAD_DIM)
    v = v.reshape(B, M, X_HEADS, X_HEAD_DIM)
    s = jnp.einsum('bqhd,bmhd->bhqm', q, k).astype(jnp.float32) / math.sqrt(X_HEAD_DIM)
    p = jax.nn.softmax(s, axis=-1)
    o = jnp.einsum('bhqm,bmhd->bqhd', p.astype(v.dtype), v)
    return o.reshape(B, S, X_WIDTH) @ wo

def conv_ffn(x, w_up, conv_k, conv_b, w_down):
    S = x.shape[1]
    h = x @ w_up
    r = CONV_W // 2
    hp = jnp.pad(h, ((0, 0), (r, r), (0, 0)))
    h = sum(hp[:, j:j + S] * conv_k[j] for j in range(CONV_W)) + conv_b
    a, b = jnp.split(h, 2, axis=-1)
    return (jax.nn.gelu(a, approximate=False) * b) @ w_down

def first_inputs(seed: int = 0) -> dict:
    key = jax.random.key(seed)
    ks = jax.random.split(key, 26)

    def nrm(k, shape, scale):
        return jax.random.normal(k, shape, dtype=jnp.float32) * scale

    L = DEPTH
    return {
        "x": nrm(ks[0], (BATCH, SEQ, D_MODEL), 1.0),
        "mem": nrm(ks[1], (BATCH, MEM_LEN, D_MODEL), 1.0),
        "w_in": nrm(ks[2], (L, D_MODEL, D_IN), D_MODEL ** -0.5),
        "b_gate": nrm(ks[3], (L, N_BRANCH * D_MODEL), 0.1),
        "a_sink": nrm(ks[4], (L, A_HEADS), 1.0),
        "b_q_gain": 1.0 + nrm(ks[5], (L, HEAD_DIM), 0.02),
        "b_k_gain": 1.0 + nrm(ks[6], (L, HEAD_DIM), 0.02),
        "c_ln_g": 1.0 + nrm(ks[7], (L, C_WIDTH), 0.02),
        "c_ln_b": nrm(ks[8], (L, C_WIDTH), 0.02),
        "c_ws": nrm(ks[9], (L, C_GROUPS, CHUNK, CHUNK), CHUNK ** -0.5),
        "c_bs": 1.0 + nrm(ks[10], (L, C_GROUPS, CHUNK), 0.02),
        "w_branch": nrm(ks[11], (L, N_BRANCH, BRANCH_WIDTH, D_MODEL), BRANCH_WIDTH ** -0.5),
        "w_mix_out": nrm(ks[12], (L, D_MODEL, D_MODEL), BETA * D_MODEL ** -0.5),
        "ln1_g": 1.0 + nrm(ks[13], (L, D_MODEL), 0.02),
        "ln1_b": nrm(ks[14], (L, D_MODEL), 0.02),
        "x_wq": nrm(ks[15], (L, D_MODEL, X_WIDTH), D_MODEL ** -0.5),
        "x_wkv": nrm(ks[16], (L, D_MODEL, 2 * X_WIDTH), D_MODEL ** -0.5),
        "x_wo": nrm(ks[17], (L, X_WIDTH, D_MODEL), BETA * X_WIDTH ** -0.5),
        "ln2_g": 1.0 + nrm(ks[18], (L, D_MODEL), 0.02),
        "ln2_b": nrm(ks[19], (L, D_MODEL), 0.02),
        "f_w_up": nrm(ks[20], (L, D_MODEL, 2 * D_FF), D_MODEL ** -0.5),
        "f_conv_k": nrm(ks[21], (L, CONV_W, 2 * D_FF), CONV_W ** -0.5),
        "f_conv_b": nrm(ks[22], (L, 2 * D_FF), 0.02),
        "f_w_down": nrm(ks[23], (L, D_FF, D_MODEL), BETA * D_FF ** -0.5),
        "ln3_g": 1.0 + nrm(ks[24], (L, D_MODEL), 0.02),
        "ln3_b": nrm(ks[25], (L, D_MODEL), 0.02),
    }

def first_block(x, mem, w_in, b_gate, a_sink, b_q_gain, b_k_gain, c_ln_g, c_ln_b, c_ws, c_bs,
              w_branch, w_mix_out, ln1_g, ln1_b, x_wq, x_wkv, x_wo, ln2_g, ln2_b,
              f_w_up, f_conv_k, f_conv_b, f_w_down, ln3_g, ln3_b):
    seq = x.shape[1]
    rows = seq // GRID_W
    pos = jnp.arange(seq, dtype=jnp.int32)
    row = jnp.repeat(jnp.arange(rows, dtype=jnp.int32), GRID_W)
    col = jnp.tile(jnp.arange(GRID_W, dtype=jnp.int32), rows)
    for l in range(DEPTH):
        h = hybrid_mixer(x, pos, row, col, w_in[l], b_gate[l], a_sink[l], b_q_gain[l], b_k_gain[l],
                         c_ln_g[l], c_ln_b[l], c_ws[l], c_bs[l], w_branch[l], w_mix_out[l])
        x = layer_norm(ALPHA * x + h, ln1_g[l], ln1_b[l])
        h = memory_cross_attention(x, mem, x_wq[l], x_wkv[l], x_wo[l])
        x = layer_norm(ALPHA * x + h, ln2_g[l], ln2_b[l])
        h = conv_ffn(x, f_w_up[l], f_conv_k[l], f_conv_b[l], f_w_down[l])
        x = layer_norm(ALPHA * x + h, ln3_g[l], ln3_b[l])
    return x


N_EVEN = (DEPTH + 1) // 2
N_ODD = DEPTH // 2
EPS = 1e-6

A_HEADS_2 = 4
A_WIDTH = D_MODEL // 2
HEAD_DIM_2 = A_WIDTH // A_HEADS_2
IDX_HEADS = 16
IDX_DIM = 64
TOPK_MAX = 256
Q_BLOCK = 128
ROPE_THETA_2 = 500000.0

POOL_WINDOWS = (2, 4, 8, 16)
B_WIDTH = D_MODEL - A_WIDTH
POOL_GROUP = B_WIDTH // len(POOL_WINDOWS)

AB_SIZES = (A_WIDTH, A_WIDTH, A_WIDTH, B_WIDTH, IDX_HEADS * IDX_DIM, IDX_HEADS, IDX_DIM)
IN_AB = sum(AB_SIZES)
AB_SPLITS = [int(s) for s in np.cumsum(AB_SIZES)[:-1]]

D_CONV = D_MODEL
CONV_WIDTH = 31

C_HEADS = 4
C_HEAD_DIM = D_MODEL // C_HEADS

D_FF_2 = -(-8 * D_MODEL // (3 * 256)) * 256


def rmsnorm(x, g):
    xf = x.astype(jnp.float32)
    y = xf * lax.rsqrt(jnp.mean(xf * xf, axis=-1, keepdims=True) + EPS)
    return (y * g.astype(jnp.float32)).astype(x.dtype)

def layernorm(x, g, b):
    xf = x.astype(jnp.float32)
    mu = jnp.mean(xf, axis=-1, keepdims=True)
    var = jnp.mean(jnp.square(xf - mu), axis=-1, keepdims=True)
    y = (xf - mu) * lax.rsqrt(var + EPS)
    return (y * g.astype(jnp.float32) + b.astype(jnp.float32)).astype(x.dtype)

def rope_partial(x, pos):
    d = x.shape[-1]
    rot = d // 4
    half = rot // 2
    inv = ROPE_THETA_2 ** (-jnp.arange(half, dtype=jnp.float32) * 2.0 / rot)
    ang = pos.astype(jnp.float32)[:, None] * inv[None, :]
    cos = jnp.cos(ang)[:, None, :]
    sin = jnp.sin(ang)[:, None, :]
    xf = x.astype(jnp.float32)
    x1, x2, rest = xf[..., :half], xf[..., half:rot], xf[..., rot:]
    out = jnp.concatenate([x1 * cos - x2 * sin, x2 * cos + x1 * sin, rest], axis=-1)
    return out.astype(x.dtype)

def dsa_attention(q, k, v, iq, iw, ik):
    bsz, t_len = q.shape[0], q.shape[1]
    topk = min(TOPK_MAX, t_len // 4)
    n_blocks = t_len // Q_BLOCK
    key_pos = jnp.arange(t_len)
    bidx = jnp.arange(bsz)[:, None, None]
    scale = HEAD_DIM_2 ** -0.5

    def block(i):
        start = i * Q_BLOCK
        qb = lax.dynamic_slice_in_dim(q, start, Q_BLOCK, axis=1)
        iqb = lax.dynamic_slice_in_dim(iq, start, Q_BLOCK, axis=1)
        iwb = lax.dynamic_slice_in_dim(iw, start, Q_BLOCK, axis=1)
        qpos = start + jnp.arange(Q_BLOCK)
        s = jnp.einsum('bqhd,bsd->bqhs', iqb, ik).astype(jnp.float32)
        scores = jnp.einsum('bqhs,bqh->bqs', jax.nn.relu(s), iwb.astype(jnp.float32))
        causal = key_pos[None, :] <= qpos[:, None]
        scores = jnp.where(causal[None], scores, -jnp.inf)
        _, idx = lax.top_k(scores, topk)
        valid = idx <= qpos[None, :, None]
        ks = k[bidx, idx]
        vs = v[bidx, idx]
        logits = jnp.einsum('bqhd,bqkhd->bhqk', qb, ks).astype(jnp.float32) * scale
        logits = jnp.where(valid[:, None], logits, -jnp.inf)
        p = jax.nn.softmax(logits, axis=-1).astype(v.dtype)
        return jnp.einsum('bhqk,bqkhd->bqhd', p, vs)

    out = lax.map(block, jnp.arange(n_blocks))
    return jnp.transpose(out, (1, 0, 2, 3, 4)).reshape(q.shape)

def multiscale_pool(u, pool_w):
    t_len = u.shape[1]
    uf = u.astype(jnp.float32)
    cs = jnp.cumsum(uf, axis=1)
    t = jnp.arange(t_len)
    outs = []
    for g, w in enumerate(POOL_WINDOWS):
        sl = slice(g * POOL_GROUP, (g + 1) * POOL_GROUP)
        c = cs[..., sl]
        shifted = jnp.pad(c, ((0, 0), (w, 0), (0, 0)))[:, :t_len]
        cnt = jnp.minimum(t + 1, w).astype(jnp.float32)[None, :, None]
        outs.append((c - shifted) / cnt - uf[..., sl])
    pooled = jnp.stack(outs, axis=2).astype(u.dtype)
    y = jnp.einsum('btgc,gcd->btgd', pooled, pool_w)
    return y.reshape(u.shape)

def mixer_ab(xn, w_in, q_gain, k_gain, pool_w, pool_scale, w_out):
    bsz, t_len, _ = xn.shape
    proj = xn @ w_in
    q, k, v, u, iq, iw, ik = jnp.split(proj, AB_SPLITS, axis=-1)
    pos = jnp.arange(t_len)
    q = rope_partial(rmsnorm(q.reshape(bsz, t_len, A_HEADS_2, HEAD_DIM_2), q_gain), pos)
    k = rope_partial(rmsnorm(k.reshape(bsz, t_len, A_HEADS_2, HEAD_DIM_2), k_gain), pos)
    v = v.reshape(bsz, t_len, A_HEADS_2, HEAD_DIM_2)
    iq = rope_partial(iq.reshape(bsz, t_len, IDX_HEADS, IDX_DIM), pos)
    ik = rope_partial(ik.reshape(bsz, t_len, 1, IDX_DIM), pos)[:, :, 0]
    iw = iw * (IDX_HEADS ** -0.5 * IDX_DIM ** -0.5)
    a = dsa_attention(q, k, v, iq, iw, ik).reshape(bsz, t_len, A_WIDTH)
    b = multiscale_pool(u, pool_w) * pool_scale
    return jnp.concatenate([a, b], axis=-1) @ w_out

def conv_module(xn, w_in, b_in, dw_w, dw_b, ln_g, ln_b, w_out):
    h = xn @ w_in + b_in
    a, gate = jnp.split(h, 2, axis=-1)
    h = a * jax.nn.sigmoid(gate)
    h = lax.conv_general_dilated(
        h, dw_w[:, None, :], window_strides=(1,), padding=[(CONV_WIDTH - 1, 0)],
        dimension_numbers=('NWC', 'WIO', 'NWC'), feature_group_count=D_CONV) + dw_b
    h = jax.nn.silu(layernorm(h, ln_g, ln_b))
    return h @ w_out

def cross_attn(hn, memn, wq, wk, wv, q_gain, k_gain, wo):
    bsz, t_len, _ = hn.shape
    m_len = memn.shape[1]
    q = rmsnorm((hn @ wq).reshape(bsz, t_len, C_HEADS, C_HEAD_DIM), q_gain)
    k = rmsnorm((memn @ wk).reshape(bsz, m_len, C_HEADS, C_HEAD_DIM), k_gain)
    v = (memn @ wv).reshape(bsz, m_len, C_HEADS, C_HEAD_DIM)
    logits = jnp.einsum('bthd,bmhd->bhtm', q, k).astype(jnp.float32) * C_HEAD_DIM ** -0.5
    p = jax.nn.softmax(logits, axis=-1).astype(v.dtype)
    o = jnp.einsum('bhtm,bmhd->bthd', p, v).reshape(bsz, t_len, D_MODEL)
    return o @ wo

def swiglu(xn, w_gate, w_up, w_down):
    return (jax.nn.silu(xn @ w_gate) * (xn @ w_up)) @ w_down

def second_inputs(seed: int = 0) -> dict:
    key = jax.random.key(seed)
    ks = iter(jax.random.split(key, 40))

    def dense(shape, fan_in):
        return jax.random.normal(next(ks), shape, jnp.float32) * fan_in ** -0.5

    def gain(shape):
        return 1.0 + 0.05 * jax.random.normal(next(ks), shape, jnp.float32)

    def bias(shape):
        return 0.02 * jax.random.normal(next(ks), shape, jnp.float32)

    return {
        'x': jax.random.normal(next(ks), (BATCH, SEQ, D_MODEL), jnp.float32),
        'mem': jax.random.normal(next(ks), (BATCH, MEM_LEN, D_MODEL), jnp.float32),
        'norm_mix': gain((DEPTH, D_MODEL)),
        'norm_cross': gain((DEPTH, D_MODEL)),
        'norm_mem': gain((DEPTH, D_MODEL)),
        'norm_ffn': gain((DEPTH, D_MODEL)),
        'w_in_ab': dense((N_EVEN, D_MODEL, IN_AB), D_MODEL),
        'a_q_norm': gain((N_EVEN, HEAD_DIM_2)),
        'a_k_norm': gain((N_EVEN, HEAD_DIM_2)),
        'pool_w': dense((N_EVEN, len(POOL_WINDOWS), POOL_GROUP, POOL_GROUP), POOL_GROUP),
        'pool_scale': gain((N_EVEN, B_WIDTH)),
        'w_out_ab': dense((N_EVEN, D_MODEL, D_MODEL), D_MODEL),
        'conv_w_in': dense((N_ODD, D_MODEL, 2 * D_CONV), D_MODEL),
        'conv_b_in': bias((N_ODD, 2 * D_CONV)),
        'conv_dw_w': dense((N_ODD, CONV_WIDTH, D_CONV), CONV_WIDTH),
        'conv_dw_b': bias((N_ODD, D_CONV)),
        'conv_ln_g': gain((N_ODD, D_CONV)),
        'conv_ln_b': bias((N_ODD, D_CONV)),
        'conv_w_out': dense((N_ODD, D_CONV, D_MODEL), D_CONV),
        'cross_wq': dense((DEPTH, D_MODEL, D_MODEL), D_MODEL),
        'cross_wk': dense((DEPTH, D_MODEL, D_MODEL), D_MODEL),
        'cross_wv': dense((DEPTH, D_MODEL, D_MODEL), D_MODEL),
        'cross_q_norm': gain((DEPTH, C_HEAD_DIM)),
        'cross_k_norm': gain((DEPTH, C_HEAD_DIM)),
        'cross_wo': dense((DEPTH, D_MODEL, D_MODEL), D_MODEL),
        'ffn_w_gate': dense((DEPTH, D_MODEL, D_FF_2), D_MODEL),
        'ffn_w_up': dense((DEPTH, D_MODEL, D_FF_2), D_MODEL),
        'ffn_w_down': dense((DEPTH, D_FF_2, D_MODEL), D_FF_2),
    }

def second_block(x, mem, norm_mix, norm_cross, norm_mem, norm_ffn, w_in_ab, a_q_norm, a_k_norm,
              pool_w, pool_scale, w_out_ab, conv_w_in, conv_b_in, conv_dw_w, conv_dw_b,
              conv_ln_g, conv_ln_b, conv_w_out, cross_wq, cross_wk, cross_wv, cross_q_norm,
              cross_k_norm, cross_wo, ffn_w_gate, ffn_w_up, ffn_w_down):
    h = x
    for l in range(DEPTH):
        xn = rmsnorm(h, norm_mix[l])
        if l % 2 == 0:
            e = l // 2
            h = h + mixer_ab(xn, w_in_ab[e], a_q_norm[e], a_k_norm[e], pool_w[e],
                             pool_scale[e], w_out_ab[e])
        else:
            o = l // 2
            h = h + conv_module(xn, conv_w_in[o], conv_b_in[o], conv_dw_w[o], conv_dw_b[o],
                                conv_ln_g[o], conv_ln_b[o], conv_w_out[o])
        h = h + cross_attn(rmsnorm(h, norm_cross[l]), rmsnorm(mem, norm_mem[l]),
                           cross_wq[l], cross_wk[l], cross_wv[l], cross_q_norm[l],
                           cross_k_norm[l], cross_wo[l])
        h = h + swiglu(rmsnorm(h, norm_ffn[l]), ffn_w_gate[l], ffn_w_up[l], ffn_w_down[l])
    return h


def setup_inputs(seed=0):
    out = dict(first_inputs(seed))
    for name, value in second_inputs(seed + 1).items():
        if name != "x":
            out[name + "_2"] = value
    return out


def reference(
    x, mem, w_in, b_gate, a_sink, b_q_gain, b_k_gain, c_ln_g, c_ln_b, c_ws, c_bs, w_branch,
    w_mix_out, ln1_g, ln1_b, x_wq, x_wkv, x_wo, ln2_g, ln2_b, f_w_up, f_conv_k, f_conv_b,
    f_w_down, ln3_g, ln3_b, mem_2, norm_mix_2, norm_cross_2, norm_mem_2, norm_ffn_2, w_in_ab_2,
    a_q_norm_2, a_k_norm_2, pool_w_2, pool_scale_2, w_out_ab_2, conv_w_in_2, conv_b_in_2,
    conv_dw_w_2, conv_dw_b_2, conv_ln_g_2, conv_ln_b_2, conv_w_out_2, cross_wq_2, cross_wk_2,
    cross_wv_2, cross_q_norm_2, cross_k_norm_2, cross_wo_2, ffn_w_gate_2, ffn_w_up_2,
    ffn_w_down_2,
):
    x = first_block(
        x, mem, w_in, b_gate, a_sink, b_q_gain, b_k_gain, c_ln_g, c_ln_b, c_ws, c_bs, w_branch,
        w_mix_out, ln1_g, ln1_b, x_wq, x_wkv, x_wo, ln2_g, ln2_b, f_w_up, f_conv_k, f_conv_b,
        f_w_down, ln3_g, ln3_b,
    )
    return second_block(
        x, mem_2, norm_mix_2, norm_cross_2, norm_mem_2, norm_ffn_2, w_in_ab_2, a_q_norm_2,
        a_k_norm_2, pool_w_2, pool_scale_2, w_out_ab_2, conv_w_in_2, conv_b_in_2, conv_dw_w_2,
        conv_dw_b_2, conv_ln_g_2, conv_ln_b_2, conv_w_out_2, cross_wq_2, cross_wk_2, cross_wv_2,
        cross_q_norm_2, cross_k_norm_2, cross_wo_2, ffn_w_gate_2, ffn_w_up_2, ffn_w_down_2,
    )


_drawn_inputs = setup_inputs


def setup_inputs(seed=0):
    import zlib

    import numpy as np

    out = dict(_drawn_inputs(seed))
    spreads = {}
    factors = {'b_gate': 3.674,
     'a_sink': 8.0,
     'b_q_gain': 8.0,
     'b_k_gain': 8.0,
     'c_ln_g': 7.98,
     'c_ln_b': 7.997,
     'c_bs': 8.0,
     'f_conv_b': 4.037,
     'norm_cross_2': 8.0,
     'norm_mem_2': 5.796,
     'a_q_norm_2': 8.0,
     'a_k_norm_2': 8.0,
     'conv_b_in_2': 5.536,
     'conv_dw_b_2': 3.269,
     'conv_ln_b_2': 6.31,
     'cross_q_norm_2': 8.0,
     'cross_k_norm_2': 8.0}
    for name, (base, spread) in spreads.items():
        noise = np.random.default_rng([zlib.crc32(name.encode()), seed]).standard_normal(out[name].shape)
        drawn = base * np.exp(spread * noise) if base else spread * noise
        out[name] = __import__('jax').numpy.asarray(drawn.astype(out[name].dtype))
    for name, factor in factors.items():
        out[name] = (out[name] * factor).astype(out[name].dtype)
    return out
```

```python
from contextlib import ExitStack

import numpy as np
import concourse.bass as bass
from concourse import mybir

F32 = mybir.dt.float32
F32R = mybir.dt.float32r
ALU = mybir.AluOpType
ACT = mybir.ActivationFunctionType
AX = mybir.AxisListType

S = 512
D = 1024
NT = 4
DEPTH = 2
ALPHA = (2 * DEPTH) ** 0.25
LN_EPS = 1e-5
RMS_EPS = 1e-6
BIG = -1.0e30
GONE = -3.0e38

CST = {}
PAR = {}


def _columns(table, entries):
    at = 0
    for name, n in entries:
        table[name] = (at, n)
        at += n
    return at


NCST = _columns(CST, [
    ("ident", 128), ("band", 384), ("causal", 128), ("cosA", 128), ("sinA", 128), ("cosB", 128), ("sinB", 128),
    ("cosq", 64), ("sinq", 64), ("cosi", 32), ("sini", 32), ("ones", 128), ("pw", 16), ("invc", 64),
])
NPAR = _columns(PAR, [
    ("b_gate", 48), ("conv_k", 264), ("conv_b", 88), ("pool_scale", 4), ("cv_bin", 16), ("dw_w", 248), ("dw_b", 8),
    ("cln_g", 8), ("cln_b", 8), ("n_mix", 16), ("n_cross", 16), ("n_mem", 16), ("n_ffn", 16),
])
POOL_W = (2, 4, 8, 16)


class Lane:

    def __init__(self, sem):
        self.sem, self.n, self.seen, self.queue = sem, 0, {}, []

    def __call__(self, make, *waits, sig=True, sem=None, by=1):
        need = {}
        stack = list(waits)
        while stack:
            w = stack.pop()
            if isinstance(w, list):
                stack += w
            elif w is not None:
                need[w[0]] = max(need.get(w[0], 0), w[1])
        for s, v in need.items():
            if self.seen.get(s, 0) < v:
                self.seen[s] = v
                self.queue.append((None, s, v))
        if sem is not None:
            sem[1] += by
            self.queue.append((make, sem[0], by))
            return (sem[0], sem[1])
        if sig:
            self.n += 1
        self.queue.append((make, self.sem if sig else None, 1))
        return (self.sem, self.n) if sig else None

    def last(self):
        return (self.sem, self.n)

    def play(self, eng, sems):
        for make, s, v in self.queue:
            if make is None:
                eng.wait_ge(sems[s], v)
            else:
                i = make(eng)
                if s is not None:
                    i.then_inc(sems[s], v)


def drive(*gens):
    live = [[g, r] for g, r in gens]
    while live:
        for item in list(live):
            for _ in range(item[1]):
                try:
                    next(item[0])
                except StopIteration:
                    live.remove(item)
                    break


def unit_shape(desc):
    nk, pieces = desc[1], desc[2]
    return nk, sum(p[3] - p[2] for p in pieces)


class Program:
    def __init__(self, nc, ins, out, plan, stage=None, dumps=None):
        self.nc, self.ins, self.out, self.plan = nc, ins, out, plan
        self.stage, self.dumps = stage, dumps
        self.units = []
        self.nsem = 0
        self.T, self.V, self.A, self.G, self.Y = (Lane(self.newsem()) for _ in range(5))
        self.ctx = ExitStack()
        sb = lambda n, s, d=F32: self.ctx.enter_context(nc.sbuf_tensor(n, s, d))
        self.x = sb("x", [128, NT, D])
        self.xh, self.xl = sb("xh", [128, 8, S], F32R), sb("xl", [128, 8, S], F32R)
        self.ah, self.al = sb("ah", [128, 12, S], F32R), sb("al", [128, 12, S], F32R)
        self.NR = 3
        self.wr = sb("wr", [128, self.NR, 1024])
        self.wh, self.wl = sb("wh", [128, self.NR, 1024], F32R), sb("wl", [128, self.NR, 1024], F32R)
        self.gb = sb("gb", [128, 2, D])
        self.cst, self.par = sb("cst", [128, NCST]), sb("par", [128, NPAR])
        self.st = sb("st", [128, 320])
        self.NU = 14700
        self.ar = sb("ar", [128, self.NU])
        self.bk = [self.ctx.enter_context(nc.psum_tensor(f"bk{i}", [128, 512], F32)) for i in range(8)]
        self.free = [(i, None) for i in range(8)]
        self.wr_sem = [[self.newsem(), 0] for _ in range(self.NR)]
        self.wr_free = [None] * self.NR
        self.w_free = [None] * self.NR
        self.w_ready = {}
        self.w_dma = self.w_split = 0
        self.nuse = 0
        self.io = [self.newsem(), 0]
        self.stores = []

    def newsem(self):
        self.nsem += 1
        return self.nsem - 1

    def c(self, name):
        a, n = CST[name]
        return self.cst[:, a:a + n]

    def p(self, name, i=0, n=None):
        a, m = PAR[name]
        return self.par[:, a + i:a + (m if n is None else i + n)]

    def u(self, a, n):
        assert a + n <= self.NU, (a, n)
        return self.ar[:, a:a + n]

    def snap(self):
        return [x.last() for x in (self.T, self.V, self.A, self.G)]

    def bank(self):
        i, toks = self.free.pop(0)
        return i, self.bk[i], toks

    def give(self, i, *toks):
        self.free.append((i, list(toks)))

    def load(self, dst, src, *waits, eng=None):
        s = [self.newsem(), 0]
        return (eng or self.Y)(lambda e: e.dma_start(dst, src), *waits, sem=s, by=16)

    def dump(self, name, ap, *waits):
        if self.dumps is not None and name in self.dumps:
            d = self.dumps[name]
            self.stores.append(self.load(d, ap, *waits))

    def tt(self, lane, out, a, b, op, *w):
        return lane(lambda e: e.tensor_tensor(out, a, b, op), *w)

    def ts(self, lane, out, a, s1, s2, o1, o2, *w):
        if s2 is None:
            return lane(lambda e: e.tensor_scalar(out, a, s1, None, o1), *w)
        return lane(lambda e: e.tensor_scalar(out, a, s1, s2, o1, o2), *w)

    def stt(self, out, a, s, b, o1, o2, *w):
        return self.V(lambda e: e.scalar_tensor_tensor(out, a, s, b, o1, o2), *w)

    def cp(self, lane, out, a, *w):
        if lane is self.A:
            return lane(lambda e: e.activation(out, a, ACT.Copy), *w)
        return lane(lambda e: e.tensor_copy(out, a), *w)

    def act(self, out, a, f, *w, bias=0.0, scale=1.0, acc=None):
        if acc is not None:
            return self.A(lambda e: e.activation(out, a, f, bias=bias, scale=scale, accum_out=acc), *w)
        return self.A(lambda e: e.activation(out, a, f, bias=bias, scale=scale), *w)

    def acopy(self, out, a, scale, *w):
        return self.A(lambda e: e.activation(out, a, ACT.Copy, scale=scale), *w)

    def mm(self, out, l, r, start, stop, *w, sig=False):
        return self.T(lambda e: e.matmul(out, l, r, start=start, stop=stop), *w, sig=sig)

    def tr(self, out, a, *w, sig=False):
        ident = self.c("ident")
        return self.T(lambda e: e.transpose(out, a, ident), *w, sig=sig)

    def split(self, h, l, src, *w, scale=None):
        hf = h.bitcast(F32)
        if scale is None:
            a = self.cp(self.A, h, src, *w)
            return [a, self.tt(self.V, l, src, hf, ALU.subtract, a, *w)]
        a = self.acopy(h, src, scale, *w)
        return [a, self.stt(l, src, scale, hf, ALU.mult, ALU.subtract, a, *w)]

    def w_prefetch(self, i):
        plan = self.plan if self.plan is not None else self.units
        n = len(plan)
        while self.w_split < min(i + self.NR, n):
            self._w_load(min(self.w_split + 1, n))
            j, r = self.w_split, self.w_split % self.NR
            nk, cols = unit_shape(plan[j])
            gain = plan[j][3]
            got = (self.wr_sem[r][0], 16 * (j // self.NR + 1))
            if gain is None:
                m = nk * cols
                toks = self.split(self.wh[:, r, 0:m], self.wl[:, r, 0:m], self.wr[:, r, 0:m], got, self.w_free[r])
            else:
                toks = []
                for k in range(nk):
                    g = self.p(gain[0], gain[1] + k, 1)
                    a = k * cols
                    toks += self.split(self.wh[:, r, a:a + cols], self.wl[:, r, a:a + cols],
                                       self.wr[:, r, a:a + cols], got, self.w_free[r], self.t_par, scale=g)
            self.w_ready[j] = toks
            self.wr_free[r] = toks
            self.w_split += 1
        self._w_load(min(self.w_split + self.NR, n))

    def _w_load(self, upto):
        while self.w_dma < upto:
            j, r = self.w_dma, self.w_dma % self.NR
            if j >= self.w_split + self.NR:
                break
            nk, cols = unit_shape((self.plan or self.units)[j])
            m = nk * cols
            dst = self.wr[:, r, 0:m]
            src = None if self.plan is None else self.ins["wpk"][j, :, 0:m]
            self.Y(lambda e, dst=dst, src=src: e.dma_start(dst, src), self.wr_free[r], sem=self.wr_sem[r], by=16)
            self.w_dma += 1

    def w_use(self, desc):
        i = self.nuse
        self.nuse += 1
        if self.plan is None:
            self.units.append(desc)
        else:
            assert self.plan[i] == desc
        self.w_prefetch(i)
        r = i % self.NR
        nk, cols = unit_shape(desc)
        view = lambda t: t[:, r, 0:nk * cols].rearrange("p (k c) -> p k c", k=nk)
        return view(self.wh), view(self.wl), self.w_ready[i], r

    def gemm(self, nk, pieces, act, toks, orient, nout, evac, gain=None, per=None, width=None):
        ah, al, base = act
        cols = sum(p[3] - p[2] for p in pieces)
        per = per or max(1, 1024 // cols)
        width = width or S
        banks = [self.bank() for _ in range(nout)]
        first = set()
        for k0 in range(0, nk, per):
            n = min(per, nk - k0)
            h, l, wt, r = self.w_use((k0, n, tuple(pieces), None if gain is None else (gain[0], gain[1] + k0)))
            for o in range(nout):
                i, bk, bt = banks[o]
                for kk in range(n):
                    k = k0 + kk
                    if orient == "F":
                        a = slice(o * 128, o * 128 + 128)
                        xh, xl = ah[:, base + k, 0:width], al[:, base + k, 0:width]
                        seq = [(h[:, kk, a], xh), (h[:, kk, a], xl), (l[:, kk, a], xh)]
                        ap = bk[:, 0:width]
                    else:
                        a = slice(o * 128, o * 128 + 128)
                        xh, xl = ah[:, base + k, a], al[:, base + k, a]
                        seq = [(xh, h[:, kk, :]), (xh, l[:, kk, :]), (xl, h[:, kk, :])]
                        ap = bk[:, 0:cols]
                    for q, (lw, rw) in enumerate(seq):
                        st = o not in first
                        first.add(o)
                        end = k == nk - 1 and q == 2
                        sig = (kk == n - 1 and q == 2) and (end or o == nout - 1)
                        t = self.mm(ap, lw, rw, st, end, wt, toks, bt if st else None, sig=sig)
                if k0 + n == nk:
                    evac(o, i, ap, t)
            self.w_free[r] = t
            yield

    def turn(self, src, n, toks, dst):
        for j in range(0, n, 4):
            m = min(4, n - j)
            i, bk, bt = self.bank()
            for q in range(m):
                t = self.tr(bk[:, q * 128:q * 128 + 128], src[:, (j + q) * 128:(j + q + 1) * 128],
                            toks, bt, self.t_cst, sig=(q == m - 1))
            dst(j, m, i, bk[:, 0:m * 128].rearrange("p (j c) -> p j c", j=m), t)

    def turn_split(self, src, n, toks, hi, lo, base, t, keep, *w):
        def dst(j, m, i, v, tok):
            a = slice(t * 128, t * 128 + 128)
            got = self.split(hi[:, base + j:base + j + m, a], lo[:, base + j:base + j + m, a], v, tok, *w)
            self.give(i, got[1])
            keep.extend(got)
        self.turn(src, n, toks, dst)

    def rstd(self, out, var, scale, eps, *w):
        g = self.ts(self.G, out, var, scale, eps, ALU.mult, ALU.add, *w)
        n = out.shape[-1]
        pw = self.c("pw")[:, 0:n]
        return self.tt(self.G, out, out, pw, ALU.pow, g, self.t_cst)

    def residual(self, nk, pieces, act, toks, norm, extra=None, first=True, fin=True, scale=True):
        for hf in range(2):
            def evac(t, i, ap, tok, hf=hf):
                xs = self.x[:, t, hf * 512:hf * 512 + 512]
                w = [tok, self.t_x[t], self.t_xr]
                if scale and first:
                    r = self.stt(xs, xs, ALPHA, ap, ALU.mult, ALU.add, *w)
                else:
                    r = self.tt(self.V, xs, xs, ap, ALU.add, *w)
                self.give(i, r)
                if hf == 1:
                    self.t_x[t] = [r]
                    if fin:
                        norm(t, r)
            yield from self.gemm(nk, pieces(hf), act, toks, "T", 4, evac)

    def ln_chain(self, t, r, tg):
        x = self.x[:, t, :]
        st = self.st[:, t * 16:t * 16 + 12]
        mv = self.st[:, t * 16 + 12:t * 16 + 14]
        rs = self.st[:, t * 16 + 14:t * 16 + 15]
        a = self.V(lambda e: e.bn_stats(st[:, 0:6], x[:, 0:512]), r)
        b = self.V(lambda e: e.bn_stats(st[:, 6:12], x[:, 512:1024]), r)
        m = self.V(lambda e: e.bn_aggr(mv, st), a, b, self.t_ln[t])
        g = self.rstd(rs, mv[:, 1:2], 1.0, LN_EPS, m)
        c = self.stt(x, x, mv[:, 0:1], self.gb[:, 0, :], ALU.subtract, ALU.mult, m, tg)
        d = self.stt(x, x, rs, self.gb[:, 1, :], ALU.mult, ALU.add, c, g, tg)
        self.t_x[t] = [d]
        self.t_ln[t] = [d, g]
        return d

    def rms_chain(self, t, r):
        s, x = self.gb[:, t % 2, :], self.x[:, t, :]
        ss, rs = self.st[:, t * 16:t * 16 + 1], self.st[:, t * 16 + 14:t * 16 + 15]
        a = self.act(s, x, ACT.Square, r, self.t_gb[t % 2], self.t_ln[t], acc=ss)
        g = self.rstd(rs, ss, 1.0 / D, RMS_EPS, a)
        b = self.acopy(s, x, rs, g, a)
        self.t_ln[t] = [b, g]
        return b

    def rope(self, src, dst, nh, g, half, cos, sin, tmp, *w):
        sh = [128, nh, g, half]
        v = lambda a: a.rearrange("p h (g w f) -> p h g w f", g=g, w=2)
        bc = lambda a: a.rearrange("p (g f) -> p g f", g=g).unsqueeze(1).broadcast_to(sh)
        x1, x2 = v(src)[:, :, :, 0, :], v(src)[:, :, :, 1, :]
        d1, d2 = v(dst)[:, :, :, 0, :], v(dst)[:, :, :, 1, :]
        n = nh * g * half
        t = [tmp[:, q * n:(q + 1) * n].rearrange("p (h g f) -> p h g f", h=nh, g=g) for q in range(4)]
        c, s = bc(cos), bc(sin)
        a = self.tt(self.V, t[0], x1, c, ALU.mult, *w)
        b = self.tt(self.V, t[1], x2, s, ALU.mult, *w)
        p = self.tt(self.V, d1, t[0], t[1], ALU.subtract, a, b, *w)
        a = self.tt(self.G, t[2], x2, c, ALU.mult, *w)
        b = self.tt(self.G, t[3], x1, s, ALU.mult, *w)
        return [p, self.tt(self.G, d2, t[2], t[3], ALU.add, a, b, *w)]

    def head_norm(self, src, nh, hd, gains, sq, col, *w):
        ss = self.st[:, 64 + col:64 + col + nh]
        a = self.act(sq, src, ACT.Square, *w)
        v = src.rearrange("p (h d) -> p h d", h=nh)
        b = self.V(lambda e: e.tensor_reduce(ss, sq.rearrange("p (h d) -> p h d", h=nh), AX.X, ALU.add), a, *w)
        g = self.rstd(ss, ss, 1.0 / hd, RMS_EPS, b)
        c = self.tt(self.V, v, v, ss.unsqueeze(2).broadcast_to([128, nh, hd]), ALU.mult, g, b)
        out = []
        for h0, n, gain in gains:
            out.append(self.tt(self.G, v[:, h0:h0 + n, :], v[:, h0:h0 + n, :],
                               gain.unsqueeze(1).broadcast_to([128, n, hd]), ALU.mult, c, *w))
        return out

    def attend(self, nh, dv, qk, keys, val, scale, ready, hold, pbuf, ptbuf, obuf, put, mask=None, sink=None):
        per = 512 // dv
        items = [(t, h) for t in range(NT) for h in range(nh)]
        n = len(items)
        nm, sm = self.st[:, 128:160], self.st[:, 160:192]
        e8 = self.st[:, 192:200]
        p_free, pt_free, o_free = [hold] * 2, [hold] * 2, [hold] * 2
        P, PT, O = {}, {}, {}
        no = 0
        later = []
        for i in range(n + 3):
            if i < n:
                t, h = items[i]
                k0, k1 = keys(t)
                w = (k1 - k0) * 128
                b, bk, bt = self.bank()
                prs = qk(h, t, k0, k1)
                for q, (lw, rw) in enumerate(prs):
                    s = self.mm(bk[:, 0:w], lw, rw, q == 0, q == len(prs) - 1, ready, bt, sig=(q == len(prs) - 1))
                pb = pbuf[:, (i % 2) * 512:(i % 2) * 512 + w]
                ci = (t * nh + h) % 32
                m_, s_ = nm[:, ci:ci + 1], sm[:, ci:ci + 1]
                if mask is not None:
                    mk = mask(t, k0, k1)
                    init = sink[:, h:h + 1] if sink is not None else -3.0e38
                    a = self.V(lambda e, pb=pb, bk=bk, w=w, mk=mk, m_=m_, init=init: e.tensor_tensor_reduce(
                        pb, bk[:, 0:w], mk, scale, init, ALU.add, ALU.max, m_), s, p_free[i % 2], ready)
                    self.give(b, a)
                    a = self.ts(self.V, m_, m_, -1.0, None, ALU.mult, None, a)
                    e_ = self.act(pb, pb, ACT.Exp, a, bias=m_, acc=s_)
                else:
                    a = self.V(lambda e, bk=bk, w=w, m_=m_: e.tensor_reduce(m_, bk[:, 0:w], AX.X, ALU.max), s, hold)
                    a = self.ts(self.V, m_, m_, -scale, None, ALU.mult, None, a)
                    e_ = self.act(pb, bk[:, 0:w], ACT.Exp, a, p_free[i % 2], bias=m_, scale=scale, acc=s_)
                    self.give(b, e_)
                P[i] = (e_, pb, k0, k1)
            if 1 <= i <= n:
                j = i - 1
                e_, pb, k0, k1 = P.pop(j)
                w = (k1 - k0) * 128
                b, bk, bt = self.bank()
                for q in range(k1 - k0):
                    tk = self.tr(bk[:, q * 128:q * 128 + 128], pb[:, q * 128:q * 128 + 128], e_, bt, self.t_cst,
                                 sig=(q == k1 - k0 - 1))
                p_free[j % 2] = [tk]
                pt = ptbuf[:, (j % 2) * 512:(j % 2) * 512 + w]
                c = self.cp(self.A if j % 2 else self.V, pt, bk[:, 0:w], tk, pt_free[j % 2])
                self.give(b, c)
                PT[j] = (c, pt, k0, k1, e_)
            for f in later:
                f()
            later = []
            if 2 <= i <= n + 1:
                j = i - 2
                t, h = items[j]
                c, pt, k0, k1, e_ = PT.pop(j)
                if h % per == 0:
                    O[t, h // per] = self.bank() + ([],)
                b, bk, bt, es = O[t, h // per]
                es.append(e_)
                col = (h % per) * dv
                for q in range(k1 - k0):
                    tk = self.mm(bk[:, col:col + dv], pt[:, q * 128:q * 128 + 128], val(h, k0 + q), q == 0,
                                 q == k1 - k0 - 1, c, bt, ready, sig=(q == k1 - k0 - 1))
                pt_free[j % 2] = [tk]
                if h % per == per - 1:
                    c0 = t * nh + h - per + 1
                    c0 %= 32
                    sv = sm[:, c0:c0 + per]
                    w2 = es
                    if sink is not None:
                        a = self.tt(self.V, e8, sink, nm[:, c0:c0 + per], ALU.add, es, ready)
                        a = self.act(e8, e8, ACT.Exp, a)
                        w2 = [self.tt(self.V, sv, sv, e8, ALU.add, a, es)]
                    a = self.V(lambda e, sv=sv: e.reciprocal(sv, sv), w2)
                    ob = obuf[:, (no % 2) * 512:(no % 2) * 512 + 512]
                    r = self.tt(self.V, ob.rearrange("p (h d) -> p h d", h=per),
                                bk[:, :].rearrange("p (h d) -> p h d", h=per),
                                sv.unsqueeze(2).broadcast_to([128, per, dv]), ALU.mult, a, tk, o_free[no % 2])
                    self.give(b, r)

                    def fin(t=t, c=h // per, ob=ob, r=r, k=no % 2):
                        put(t, c, ob, [r])
                        o_free[k] = [self.T.last()]
                    later.append(fin)
                    no += 1
            yield

    def build(self):
        ins, V, A, G, T = self.ins, self.V, self.A, self.G, self.T
        self.t_cst = self.load(self.cst[:, :], ins["cst"])
        self.t_par = self.load(self.par[:, :], ins["par"])
        self.t_gb = [None, None]
        self.t_ln = [None] * NT
        t = self.load(self.x[:, :, :], ins["x"].rearrange("(t p) d -> p t d", p=128))
        self.t_x = [[t] for _ in range(NT)]
        self.t_xr = None
        self.t_xT = []
        arena = None
        for q in range(2):
            raw = self.u(q * 2048, 2048)
            tok = self.load(raw, ins["xT"][:, q * 2048:(q + 1) * 2048])
            self.t_xT += self.split(self.xh[:, q * 4:q * 4 + 4, :], self.xl[:, q * 4:q * 4 + 4, :],
                                    raw.rearrange("p (k s) -> p k s", k=4), tok)
        self.free_ar = self.snap()
        for l in range(DEPTH):
            self.mixer1(l)
            if self.stage == f"mix{l}":
                return self.finish()
            self.cross1(l)
            if self.stage == f"cross{l}":
                return self.finish()
            self.ffn1(l)
            if self.stage == f"ffn{l}":
                return self.finish()
        for l in range(DEPTH):
            if l == 0:
                self.mixer2()
            else:
                self.convmod()
            if self.stage == f"mix2{l}":
                return self.finish()
            self.cross2(l)
            if self.stage == f"cross2{l}":
                return self.finish()
            self.ffn2(l)
            if self.stage == f"ffn2{l}":
                return self.finish()
        return self.finish()

    def finish(self):
        for t in range(NT):
            self.stores.append(self.load(self.out[t * 128:(t + 1) * 128, :], self.x[:, t, :], self.t_x[t]))
        self.Y(None if False else (lambda e: e.nop()), self.stores, sig=False)

    def cols(self, name, idx, a, b):
        return ((name, idx, a, b),)

    def load_gb(self, g, b, l, *w):
        a = self.load(self.gb[:, 0, :], self.ins[g][l:l + 1, :].broadcast_to([128, D]), *w)
        return [a, self.load(self.gb[:, 1, :], self.ins[b][l:l + 1, :].broadcast_to([128, D]), *w)]

    def turn_x(self, ln=None, rms=False, then_xT=True):
        keep = []
        for t in range(NT):
            if rms:
                d = self.rms_chain(t, self.t_x[t])
                src = self.gb[:, t % 2, :]
            else:
                d = self.t_x[t]
                src = self.x[:, t, :]
            self.turn_split(src, 8, [d], self.xh, self.xl, 0, t, keep, self.x_free)
            if rms:
                self.t_gb[t % 2] = [T_ for T_ in [self.T.last()]]
            yield
        self.t_xr = [self.T.last()]
        self.t_xT = keep

    def mixer1(self, l):
        V, A, G, T = self.V, self.A, self.G, self.T
        ins = self.ins
        xa = (self.xh, self.xl, 0)
        vA, vB = self.u(0, 512), self.u(512, 512)
        qkA, qkB = self.u(1024, 2560), self.u(3584, 2560)
        qT, kT = self.u(6144, 2048), self.u(8192, 1024)
        pb, ptb, ob = self.u(9216, 1024), self.u(10240, 1024), self.u(11264, 1024)
        ro, tmp, kd = self.u(12288, 640), self.u(12928, 1280), self.u(14208, 256)
        sink = self.st[:, 200:208]
        hold = self.free_ar
        tg = self.load_gb("ln1_g", "ln1_b", l, self.gb_free())
        gq, gk = self.u(14464, 64), self.u(14528, 64)
        tgain = [self.load(gq, ins["b_q_gain"][l:l + 1, :].broadcast_to([128, 64]), hold),
                 self.load(gk, ins["b_k_gain"][l:l + 1, :].broadcast_to([128, 64]), hold)]
        tsink = self.load(sink, ins["a_sink"][l:l + 1, :].broadcast_to([128, 8]), hold)
        t3 = lambda a: a.rearrange("p (t c) -> p t c", t=NT)
        qk3 = {"A": t3(qkA), "B": t3(qkB)}
        v3 = {"A": t3(vA), "B": t3(vB)}
        got = {"A": [], "B": []}

        def proj(br, c0):
            def e1(t, i, ap, tok):
                r = self.cp(A if t % 2 else V, qk3[br][:, t, 0:512], ap, tok, hold)
                self.give(i, r)
                got[br].append(r)

            def e2(t, i, ap, tok):
                ln = A if t % 2 else V
                r = self.cp(ln, qk3[br][:, t, 512:640], ap[:, 0:128], tok, hold)
                r2 = self.cp(ln, v3[br][:, t, :], ap[:, 128:256], tok, hold)
                self.give(i, r, r2)
                got[br].extend([r, r2])
            yield from self.gemm(8, self.cols("w_in", l, c0, c0 + 512), xa, self.t_xT, "T", 4, e1)
            yield from self.gemm(8, self.cols("w_in", l, c0 + 512, c0 + 768), xa, self.t_xT, "T", 4, e2)

        qT3, kT3 = qT.rearrange("p (j s) -> p j s", j=4), kT.rearrange("p (j s) -> p j s", j=2)
        qkT = {}

        def prologue(br, free_q):
            out, prev = [], hold
            for t in range(NT):
                src = qk3[br][:, t, :]
                w = [got[br]]
                if br == "B":
                    w = self.head_norm(src, 10, 64, [(0, 8, gq), (8, 2, gk)], ob[:, 0:640], t * 10, got[br], tgain,
                                       free_q, prev)
                cos, sin = self.c("cos" + br)[:, t * 32:t * 32 + 32], self.c("sin" + br)[:, t * 32:t * 32 + 32]
                r = self.rope(src.rearrange("p (h d) -> p h d", h=10), ro.rearrange("p (h d) -> p h d", h=10), 10,
                              1 if br == "A" else 2, 32 if br == "A" else 16, cos, sin, tmp, w, prev, self.t_cst)
                kv = ro[:, 512:640].rearrange("p (k d) -> p k d", k=2)
                k2 = self.cp(G, kd.rearrange("p (k w d) -> p k w d", k=2, w=2),
                             kv.unsqueeze(2).broadcast_to([128, 2, 2, 64]), r, prev)

                def put(dst3):
                    def f(j, m, i, v, tok):
                        c = self.cp(A if t % 2 else V, dst3[:, j:j + m, t * 128:t * 128 + 128], v, tok, free_q)
                        self.give(i, c)
                        out.append(c)
                    return f
                self.turn(ro[:, 0:512], 4, r, put(qT3))
                self.turn(kd, 2, [k2], put(kT3))
                prev = [T.last()]
                yield
            qkT[br] = out

        def branch(br, free_q):
            n = 0 if br == "A" else 1
            keep = []

            def qk(h, t, k0, k1):
                a = slice((h % 2) * 64, (h % 2) * 64 + 64)
                return [(qT3[a, h // 2, t * 128:t * 128 + 128], kT3[a, h // 4, k0 * 128:k1 * 128])]

            def val(h, k):
                return v3[br][:, k, (h // 4) * 64:(h // 4) * 64 + 64]

            def put(t, c, o, toks):
                self.turn_split(o, 4, toks, self.ah, self.al, 4 * n, t, keep, self.a_free)
            if br == "A":
                keys = lambda t: (max(0, t - 1), min(NT, t + 2))
                mask = lambda t, k0, k1: self.c("band")[:, (k0 - t + 1) * 128:(k1 - t + 1) * 128]
                sk = sink
            else:
                keys = lambda t: (0, NT)
                mask = sk = None
            ready = [qkT[br], got[br], tsink, self.t_cst]
            yield from self.attend(8, 64, qk, keys, val, 0.125, ready, free_q, pb, ptb, ob, put, mask, sk)
            self.t_br[n] = keep

        self.t_br = [None] * 3
        drive((proj("A", 0), 1))
        drive((self.chain(lambda: prologue("A", hold), lambda: branch("A", hold)), 2), (proj("B", 768), 1))
        freeA = self.snap()
        if self.stage == "qk":
            self.dump("qkT", self.u(6144, 3072), freeA)

        uT, vc = self.u(1024, 2048).rearrange("p (k s) -> p k s", k=4), self.u(3072, 2048).rearrange(
            "p (t c) -> p t c", t=NT)
        t_u, t_v = [], []
        cz = {}

        def proj_c():
            def eu(o, i, ap, tok):
                r = self.act(uT[:, o, :], ap, ACT.Gelu, tok, cz["free"])
                self.give(i, r)
                t_u.append(r)

            def ev(t, i, ap, tok):
                r = self.act(vc[:, t, :], ap, ACT.Gelu, tok, cz["free"])
                self.give(i, r)
                t_v.append(r)
            yield from self.gemm(8, self.cols("w_in", l, 1536, 2048), xa, self.t_xT, "F", 4, eu)
            yield from self.gemm(8, self.cols("w_in", l, 2048, 2560), xa, self.t_xT, "T", 4, ev)

        drive((prologue("B", freeA), 1))
        cz["free"] = [freeA, self.snap()]
        drive((branch("B", freeA), 2), (proj_c(), 1))
        freeB = self.snap()
        lg, lb, bs = self.u(6144, 512), self.u(6656, 512), self.u(7168, 512)
        wsT = self.u(7680, 512)
        tp = [self.load(lg, ins["c_ln_g"][l:l + 1, :].broadcast_to([128, 512]), freeB),
              self.load(lb, ins["c_ln_b"][l:l + 1, :].broadcast_to([128, 512]), freeB),
              self.load(bs, ins["c_bs"][l:l + 1, :].broadcast_to([128, 512]), freeB),
              self.load(wsT, ins["wsT"][l, :, :], freeB)]
        vn = []
        for t in range(NT):
            st, mv, rs = (self.st[:, 64 + t * 16 + a:64 + t * 16 + b] for a, b in ((0, 6), (6, 8), (8, 9)))
            x = vc[:, t, :]
            a = V(lambda e, st=st, x=x: e.bn_stats(st, x), t_v, freeB)
            a = V(lambda e, st=st, mv=mv: e.bn_aggr(mv, st), a)
            g = self.rstd(rs, mv[:, 1:2], 1.0, LN_EPS, a)
            c = self.stt(x, x, mv[:, 0:1], lg, ALU.subtract, ALU.mult, a, tp)
            vn.append(self.stt(x, x, rs, lb, ALU.mult, ALU.add, c, g, tp))
        keep = []
        mt = [self.u(8192, 512), self.u(8704, 512)]
        mt_free = [freeB, freeB]
        for g in range(4):
            i, bk, bt = self.bank()
            for n in range(NT):
                tok = self.mm(bk[:, n * 128:n * 128 + 128], vc[:, n, g * 128:g * 128 + 128],
                              wsT[:, g * 128:g * 128 + 128], True, True, vn, tp, bt, sig=(n == 3))
            m = mt[g % 2]
            r = self.tt(V, m.rearrange("p (n i) -> p n i", n=4), bk[:, :].rearrange("p (n i) -> p n i", n=4),
                        bs[:, g * 128:g * 128 + 128].unsqueeze(1).broadcast_to([128, 4, 128]), ALU.add, tok, tp,
                        mt_free[g % 2])
            self.give(i, r)
            r = self.tt(V, m, m, uT[:, g, :], ALU.mult, r, t_u)
            s = self.split(self.ah[:, 8 + g, :], self.al[:, 8 + g, :], m, r, self.a_free)
            mt_free[g % 2] = s
            keep += s
        self.t_br[2] = keep
        mg = self.u(9216, 4096).rearrange("p (k s) -> p k s", k=8)
        sg = self.u(0, 1024)
        sgs = [self.u(5120, 512), self.u(5632, 512), self.u(6144, 512), self.u(6656, 512)]
        tms = [self.u(13312, 512), self.u(13824, 512)]
        freeC = self.snap()
        hb = self.st[:, 208:232]
        thb = self.ts(V, hb, self.p("b_gate", l * 24, 24), 0.5, None, ALU.mult, None, self.t_par, freeC)
        sg_free, tm_free = [freeC] * 4, [freeC] * 2
        t_mg = [None] * 8
        nt = 0
        gone = []
        for n in range(3):
            for mgp in range(2):
                t_sg = [None] * 4

                def eg(o, i, ap, tok):
                    m = mgp * 4 + o
                    r = self.act(sgs[o], ap, ACT.Tanh, tok, thb, sg_free[o], bias=hb[:, n * 8 + m:n * 8 + m + 1],
                                 scale=0.5)
                    self.give(i, r)
                    t_sg[o] = r

                def eb(o, i, ap, tok):
                    nonlocal nt
                    m = mgp * 4 + o
                    if n == 0:
                        r = self.stt(mg[:, m, :], sgs[o], 1.0, ap, ALU.add, ALU.mult, tok, t_sg[o], freeC)
                        self.give(i, r)
                        sg_free[o] = [r]
                    else:
                        tm = tms[nt % 2]
                        r = self.stt(tm, sgs[o], 1.0, ap, ALU.add, ALU.mult, tok, t_sg[o], tm_free[nt % 2])
                        self.give(i, r)
                        sg_free[o] = [r]
                        r = self.tt(G, mg[:, m, :], mg[:, m, :], tm, ALU.add, r, t_mg[m])
                        tm_free[nt % 2] = [r]
                        nt += 1
                    t_mg[m] = [r]
                c0 = 2560 + n * 1024 + mgp * 512
                drive((self.gemm(8, self.cols("w_in", l, c0, c0 + 512), xa, self.t_xT, "F", 4, eg), 1))
                drive((self.gemm(4, self.cols("w_branch", (l, n), mgp * 512, mgp * 512 + 512),
                                 (self.ah, self.al, 4 * n), self.t_br[n], "F", 4, eb), 1))
        self.a_free = [T.last()]
        xfree = [T.last()]
        tm_ = []
        for m in range(8):
            tm_ += self.split(self.xh[:, m, :], self.xl[:, m, :], mg[:, m, :], t_mg[m], xfree,
                              scale=self.c("pw")[:, 15:16])
        self.dump("mg", self.u(9216, 4096), tm_)
        self.free_ar = self.snap()
        drive((self.residual(8, lambda hf: self.cols("w_mix_out", l, hf * 512, hf * 512 + 512), xa, tm_,
                             lambda t, r: self.ln_chain(t, r, tg)), 1))
        self.x_free = [T.last()]
        self.gb_done = list(self.t_x)
        drive((self.turn_x(), 1))

    def chain(self, *fs):
        for f in fs:
            yield from f()

    def gb_free(self):
        return [list(self.t_x), self.t_gb[0], self.t_gb[1]]

    def mem_operand(self, name, at, *w):
        raw = self.u(at, 2048)
        tok = self.load(raw, self.ins[name], *w)
        return self.split(self.ah[:, 0:8, 0:256], self.al[:, 0:8, 0:256],
                          raw.rearrange("p (k s) -> p k s", k=8), tok, self.a_free)

    def cross1(self, l):
        V, A, T = self.V, self.A, self.T
        hold = self.free_ar
        tg = self.load_gb("ln2_g", "ln2_b", l, self.gb_free())
        kT = self.u(2048, 1024).rearrange("p (h s) -> p h s", h=4)
        vm = self.u(3072, 1024).rearrange("p (t c) -> p t c", t=2)
        qT = self.u(4096, 2048).rearrange("p (h s) -> p h s", h=4)
        pb, ptb, ob = self.u(6144, 1024), self.u(7168, 1024), self.u(8192, 1024)
        tm = self.mem_operand("memT", 0, hold)
        ma = (self.ah, self.al, 0)
        t_k, t_v, t_q = [], [], []

        def ek(o, i, ap, tok):
            r = self.cp(A if o % 2 else V, kT[:, o, :], ap, tok, hold)
            self.give(i, r)
            t_k.append(r)

        def ev(t, i, ap, tok):
            r = self.cp(A if t % 2 else V, vm[:, t, :], ap, tok, hold)
            self.give(i, r)
            t_v.append(r)

        def eq(o, i, ap, tok):
            r = self.cp(A if o % 2 else V, qT[:, o, :], ap, tok, hold)
            self.give(i, r)
            t_q.append(r)
        drive((self.gemm(8, self.cols("x_wkv", l, 0, 512), ma, tm, "F", 4, ek, width=256), 1))
        drive((self.gemm(8, self.cols("x_wkv", l, 512, 1024), ma, tm, "T", 2, ev), 1))
        self.a_free = [T.last()]
        drive((self.gemm(8, self.cols("x_wq", l, 0, 512), (self.xh, self.xl, 0), self.t_xT, "F", 4, eq), 1))
        keep = []

        def put(t, c, o, toks):
            self.turn_split(o, 4, toks, self.ah, self.al, 0, t, keep, self.a_free)
        drive((self.attend(
            4, 128, lambda h, t, k0, k1: [(qT[:, h, t * 128:t * 128 + 128], kT[:, h, :])], lambda t: (0, 2),
            lambda h, k: vm[:, k, h * 128:h * 128 + 128], 128 ** -0.5, [t_k, t_v, t_q], hold, pb, ptb, ob, put), 1))
        self.free_ar = self.snap()
        drive((self.residual(4, lambda hf: self.cols("x_wo", l, hf * 512, hf * 512 + 512), (self.ah, self.al, 0),
                             keep, lambda t, r: self.ln_chain(t, r, tg)), 1))
        self.x_free = [T.last()]
        self.a_free = [T.last()]
        drive((self.turn_x(), 1))

    def ffn1(self, l):
        V, A, G, T = self.V, self.A, self.G, self.T
        hold = self.free_ar
        tg = self.load_gb("ln3_g", "ln3_b", l, self.gb_free())
        xa = (self.xh, self.xl, 0)
        FT = 22
        ck = lambda j, m: self.p("conv_k", l * 132 + j * 44 + m, 1)
        cb = lambda m: self.p("conv_b", l * 44 + m, 1)
        bufs = [self.u(q * 512, 512) for q in range(8)]
        b_free = [hold] * 8
        nb = 0
        last = l == DEPTH - 1
        for half, (m0, m1) in enumerate(((0, 12), (12, 22))):
            keep = []
            for m in range(m0, m1, 2):
                res = {}

                def ev(o, i, ap, tok):
                    nonlocal nb
                    f = m + o % 2 + (FT if o >= 2 else 0)
                    s = nb % 8
                    nb += 1
                    b = bufs[s]
                    r = self.act(b, ap, ACT.Identity, tok, b_free[s], self.t_par, bias=cb(f), scale=ck(1, f))
                    r = self.stt(b[:, 1:512], ap[:, 0:511], ck(0, f), b[:, 1:512], ALU.mult, ALU.add, r)
                    r = self.stt(b[:, 0:511], ap[:, 1:512], ck(2, f), b[:, 0:511], ALU.mult, ALU.add, r)
                    self.give(i, r)
                    if o < 2:
                        r = self.act(b, b, ACT.Gelu, r)
                        res[o] = (r, b, s)
                    else:
                        ra, ba, sa = res[o - 2]
                        r = self.tt(V, ba, ba, b, ALU.mult, ra, r)
                        b_free[s] = [r]
                        k = m - m0 + o - 2
                        w = self.split(self.ah[:, k, :], self.al[:, k, :], ba, r, self.a_free)
                        b_free[sa] = w
                        keep.extend(w)
                pieces = (("f_w_up", l, m * 128, m * 128 + 256), ("f_w_up", l, (m + FT) * 128, (m + FT) * 128 + 256))
                drive((self.gemm(8, pieces, xa, self.t_xT, "F", 4, ev), 1))
            self.x_free = [T.last()]
            nk = m1 - m0
            drive((self.residual(nk, lambda hf: (("f_w_down", (l, m0), hf * 512, hf * 512 + 512),),
                                 (self.ah, self.al, 0), keep, lambda t, r: self.ln_chain(t, r, tg),
                                 first=half == 0, fin=half == 1), 1))
            self.a_free = [T.last()]
        self.free_ar = self.snap()
        if last:
            self.t_gb = [list(self.t_x), list(self.t_x)]
            drive((self.turn_x(rms=True), 1))
        else:
            drive((self.turn_x(), 1))

    def mixer2(self):
        V, A, G, T = self.V, self.A, self.G, self.T
        ins = self.ins
        xa = (self.xh, self.xl, 0)
        hold = self.free_ar
        gain = ("n_mix", 0)
        iqT = self.u(0, 4096).rearrange("p (j s) -> p j s", j=8)
        ikT = self.u(4096, 512)
        iq = self.u(4608, 2048).rearrange("p (t c) -> p t c", t=NT)
        sc = self.u(6656, 2048).rearrange("p (t s) -> p t s", t=NT)
        iw = self.u(8704, 64).rearrange("p (t c) -> p t c", t=NT)
        ik = self.u(8768, 256).rearrange("p (t c) -> p t c", t=NT)
        ikd = self.u(9024, 128)
        tmp = self.u(9152, 512)
        rl = [self.u(9664 + 512 * q, 512) for q in range(3)]
        t_ik, t_iw = [], []

        def ei(t, i, ap, tok):
            r = self.ts(V, iw[:, t, :], ap[:, 0:16], 1.0 / 32.0, None, ALU.mult, None, tok, hold)
            r2 = self.cp(V, ik[:, t, :], ap[:, 16:80], tok, hold)
            self.give(i, r2)
            t_iw.append(r)
            t_ik.append(r2)
        drive((self.gemm(8, self.cols("w_in_ab_2", 0, 3072, 3152), xa, self.t_xT, "T", 4, ei, gain=gain, per=8), 1))

        def partial(src, nh, hd, half, cs, t, prev, toks):
            rot = 2 * half
            cos = self.c("cos" + cs)[:, t * half:t * half + half]
            sin = self.c("sin" + cs)[:, t * half:t * half + half]
            v = src.rearrange("p (h d) -> p h d", h=nh)[:, :, 0:rot]
            return self.rope(v, v, nh, 1, half, cos, sin, tmp, toks, prev, self.t_cst)

        def rope_in_place(src, nh, half, cs, t, prev, toks):
            cos = self.c("cos" + cs)[:, t * half:t * half + half]
            sin = self.c("sin" + cs)[:, t * half:t * half + half]
            v = src.rearrange("p (h d) -> p h d", h=nh)
            x1, x2 = v[:, :, 0:half], v[:, :, half:2 * half]
            n = nh * half
            q = [tmp[:, a * n:(a + 1) * n].rearrange("p (h f) -> p h f", h=nh) for a in range(4)]
            c = cos.unsqueeze(1).broadcast_to([128, nh, half])
            s = sin.unsqueeze(1).broadcast_to([128, nh, half])
            a0 = self.tt(V, q[0], x1, c, ALU.mult, toks, prev, self.t_cst)
            a1 = self.tt(V, q[1], x2, s, ALU.mult, toks, prev, self.t_cst)
            a2 = self.tt(V, q[2], x2, c, ALU.mult, toks, prev, self.t_cst)
            a3 = self.tt(V, q[3], x1, s, ALU.mult, toks, prev, self.t_cst)
            r1 = self.tt(V, x1, q[0], q[1], ALU.subtract, a0, a1, a3)
            r2 = self.tt(V, x2, q[2], q[3], ALU.add, a2, a3, r1)
            return [r1, r2]

        t_ikT = []
        prev = hold
        for t in range(NT):
            r = rope_in_place(ik[:, t, :], 1, 8, "i", t, prev, t_ik)
            d = self.cp(V, ikd.rearrange("p (w d) -> p w d", w=2), ik[:, t, :].unsqueeze(1).broadcast_to([128, 2, 64]),
                        r, prev)
            prev = [d]

            def dst(j, m, i, v, tok, t=t):
                c = self.cp(A, ikT[:, t * 128:t * 128 + 128], v[:, 0, :], tok, hold)
                self.give(i, c)
                t_ikT.append(c)
            self.turn(ikd, 1, [d], dst)
            prev = [d, T.last()]
        t_iqT = []
        for cg in range(2):
            t_iq = {}

            def eq(t, i, ap, tok):
                r = self.cp(A, iq[:, t, :], ap, tok, hold)
                self.give(i, r)
                t_iq[t] = r
            drive((self.gemm(8, self.cols("w_in_ab_2", 0, 2048 + cg * 512, 2560 + cg * 512), xa, self.t_xT, "T", 4,
                             eq, gain=gain), 1))
            for t in range(NT):
                r = rope_in_place(iq[:, t, :], 8, 8, "i", t, prev, t_iq[t])
                prev = r

                def dst(j, m, i, v, tok, t=t):
                    c = self.cp(A if t % 2 else V, iqT[:, cg * 4 + j:cg * 4 + j + m, t * 128:t * 128 + 128], v, tok,
                                hold)
                    self.give(i, c)
                    t_iqT.append(c)
                self.turn(iq[:, t, :], 4, r, dst)
            hold = [hold, T.last()]
        t_sc = {}
        top = self.st[:, 232:240]

        def index_scores():
            n = 0
            rf = [hold] * 3
            for t in range(NT):
                w = (t + 1) * 128
                prev = None
                for h in range(16):
                    a = slice((h % 2) * 64, (h % 2) * 64 + 64)
                    i, bk, bt = self.bank()
                    tok = self.mm(bk[:, 0:w], iqT[a, h // 2, t * 128:t * 128 + 128], ikT[a, 0:w], True, True,
                                  t_iqT, t_ikT, bt, sig=True)
                    r = rl[n % 3][:, 0:w]
                    c = self.act(r, bk[:, 0:w], ACT.Relu, tok, rf[n % 3])
                    self.give(i, c)
                    s = sc[:, t, 0:w]
                    wv = iw[:, t, h:h + 1]
                    if h == 0:
                        prev = self.ts(V, s, r, wv, None, ALU.mult, None, c, t_iw, hold)
                    else:
                        prev = self.stt(s, r, wv, s, ALU.mult, ALU.add, c, prev)
                    rf[n % 3] = [prev]
                    n += 1
                    if h % 2:
                        yield
                d = sc[:, t, t * 128:w]
                prev = self.tt(V, d, d, self.c("causal"), ALU.add, prev, self.t_cst)
                t_sc[t] = prev
                yield

        def choose():
            prev = None
            for t in range(1, NT):
                w = (t + 1) * 128
                s = sc[:, t, 0:w]
                prev = [prev, t_sc[t]]
                for _ in range(16):
                    a = V(lambda e, s=s: e.max(top, s), prev)
                    prev = V(lambda e, s=s: e.match_replace(s, top, s, GONE), a)
                    yield
                t_sc[t] = self.ts(V, s, s, -2.0e38, BIG, ALU.is_gt, ALU.mult, prev)
                yield
        drive((index_scores(), 1))
        freeI = self.snap()
        qT = self.u(0, 2048).rearrange("p (h s) -> p h s", h=4)
        kT = self.u(2048, 2048).rearrange("p (h s) -> p h s", h=4)
        vt = self.u(4096, 2048).rearrange("p (t c) -> p t c", t=NT)
        raw = self.u(8704, 2048).rearrange("p (t c) -> p t c", t=NT)
        sq = self.u(10752, 512)
        tmp = self.u(11264, 512)
        gq = [self.u(11776, 128), self.u(11904, 128)]
        pbf, ptb, obf = self.u(8704, 1024), self.u(9728, 1024), self.u(12032, 1024)
        tgain = [self.load(gq[0], ins["a_q_norm_2"].broadcast_to([128, 128]), freeI),
                 self.load(gq[1], ins["a_k_norm_2"].broadcast_to([128, 128]), freeI)]
        t_qk = []
        t_vt = []

        def project():
            rfree = freeI
            for which in range(2):
                t_r = {}

                def er(t, i, ap, tok):
                    r = self.cp(A, raw[:, t, :], ap, tok, rfree)
                    self.give(i, r)
                    t_r[t] = r
                yield from self.gemm(8, self.cols("w_in_ab_2", 0, which * 512, which * 512 + 512), xa, self.t_xT,
                                     "T", 4, er, gain=gain)
                pv = None
                for t in range(NT):
                    w = self.head_norm(raw[:, t, :], 4, 128, [(0, 4, gq[which])], sq, t * 4, t_r[t], tgain, freeI, pv)
                    w = rope_in_place(raw[:, t, :], 4, 16, "q", t, freeI, w)
                    pv = w
                    dd = qT if which == 0 else kT

                    def dst(j, m, i, v, tok, t=t):
                        c = self.cp(A, dd[:, j:j + m, t * 128:t * 128 + 128], v, tok, freeI)
                        self.give(i, c)
                        t_qk.append(c)
                    self.turn(raw[:, t, :], 4, w, dst)
                    yield
                rfree = [T.last()]

            def ev(t, i, ap, tok):
                r = self.cp(A, vt[:, t, :], ap, tok, freeI)
                self.give(i, r)
                t_vt.append(r)
            yield from self.gemm(8, self.cols("w_in_ab_2", 0, 1024, 1536), xa, self.t_xT, "T", 4, ev, gain=gain)
            yield from pool_branch()

        def pool_branch():
            uT = [self.u(13056, 528), self.u(13584, 528)]
            pw = self.u(14112, 128)
            ub = self.u(10752, 512)
            t_u = []
            uall = raw

            def eu(o, i, ap, tok):
                r = self.cp(A, uall[:, o, :], ap, tok, T_raw)
                self.give(i, r)
                t_u.append(r)
            T_raw = [T.last(), V.last()]
            yield from self.gemm(8, self.cols("w_in_ab_2", 0, 1536, 2048), xa, self.t_xT, "F", 4, eu, gain=gain)
            keep = []
            prev = [freeI, V.last(), T.last(), A.last()]
            z0 = V(lambda e: e.memset(uT[0][:, 0:16], 0.0), prev)
            z1 = V(lambda e: e.memset(uT[1][:, 0:16], 0.0), prev)
            zz = [z0, z1]
            tp = prev
            for g, win in enumerate(POOL_W):
                tw = self.load(pw, ins["pool_w_2"][g, :, :], tp)
                u = uall[:, g, :]
                cur = self.cp(V, uT[0][:, 16:528], u, t_u, zz, prev)
                src, k, sh = 0, 0, 1
                while sh < win:
                    s_, d_ = uT[k % 2], uT[(k + 1) % 2]
                    cur = self.tt(V, d_[:, 16:528], s_[:, 16:528], s_[:, 16 - sh:528 - sh], ALU.add, cur)
                    sh *= 2
                    k += 1
                s_ = uT[k % 2]
                po = ub
                r = self.tt(V, s_[:, 16:32], s_[:, 16:32], self.c("invc")[:, g * 16:g * 16 + 16], ALU.mult, cur,
                            self.t_cst)
                r1 = self.tt(V, po[:, 0:16], s_[:, 16:32], u[:, 0:16], ALU.subtract, r, prev)
                r2 = self.stt(po[:, 16:512], s_[:, 32:528], 1.0 / win, u[:, 16:512], ALU.mult, ALU.subtract, cur,
                              prev)
                i, bk, bt = self.bank()
                tok = self.mm(bk[:, :], pw, po, True, True, r1, r2, tw, bt, sig=True)
                prev = [tok, r1, r2]
                tp = [tok]
                rr = self.ts(V, uT[(k + 1) % 2][:, 16:528], bk[:, :], self.p("pool_scale", g, 1), None, ALU.mult,
                             None, tok, self.t_par)
                self.give(i, rr)
                sp = self.split(self.ah[:, 4 + g, :], self.al[:, 4 + g, :], uT[(k + 1) % 2][:, 16:528], rr,
                                self.a_free)
                prev = prev + sp
                keep += sp
                yield
            self.t_pool = keep
        drive((project(), 1), (choose(), 2))
        if self.stage == "dsa":
            self.dump("sc", self.u(6656, 2048), self.snap())
            self.dump("qT", self.u(0, 4096), self.snap())
        freeP = self.snap()
        keep = []

        def put(t, c, o, toks):
            self.turn_split(o, 4, toks, self.ah, self.al, 0, t, keep, self.a_free)

        def mask(t, k0, k1):
            return self.c("causal") if t == 0 else sc[:, t, 0:(t + 1) * 128]
        drive((self.attend(
            4, 128, lambda h, t, k0, k1: [(qT[:, h, t * 128:t * 128 + 128], kT[:, h, 0:k1 * 128])],
            lambda t: (0, t + 1), lambda h, k: vt[:, k, h * 128:h * 128 + 128], 128 ** -0.5,
            [t_qk, t_vt, list(t_sc.values())], freeP, pbf, ptb, obf, put, mask), 1))
        self.free_ar = self.snap()
        self.resid2(8, lambda hf: self.cols("w_out_ab_2", 0, hf * 512, hf * 512 + 512), (self.ah, self.al, 0),
                    [keep, self.t_pool])

    def resid2(self, nk, pieces, act, toks, first=True, fin=True):
        drive((self.residual(nk, pieces, act, toks, lambda t, r: None, scale=False), 1))
        self.a_free = [self.T.last()]
        if fin:
            self.x_free = [self.T.last()]
            drive((self.turn_x(rms=True), 1))

    def convmod(self):
        V, A, G, T = self.V, self.A, self.G, self.T
        xa = (self.xh, self.xl, 0)
        hold = self.free_ar
        hT = self.u(0, 8 * 542).rearrange("p (k s) -> p k s", k=8)
        y = self.u(4336, 4096).rearrange("p (k s) -> p k s", k=8)
        th = [self.u(8432 + 512 * q, 512) for q in range(4)]
        gain = ("n_mix", 8)
        hb = self.st[:, 64:72]
        thb = self.ts(V, hb, self.p("cv_bin", 8, 8), 0.5, None, ALU.mult, None, self.t_par, hold)
        z = V(lambda e: e.memset(hT[:, :, 0:30], 0.0), hold)
        th_free = [hold] * 4
        t_h = {}
        res = {}
        n = [0]
        t_y = {}
        steps = []

        def conv(m):
            r = self.ts(V, y[:, m, :], hT[:, m, 30:542], self.p("dw_w", m * 31 + 30, 1), self.p("dw_b", m, 1),
                        ALU.mult, ALU.add, t_h[m], z, hold)
            for j in range(30):
                r = self.stt(y[:, m, :], hT[:, m, j:j + 512], self.p("dw_w", m * 31 + j, 1), y[:, m, :], ALU.mult,
                             ALU.add, r)
                if j % 6 == 5:
                    yield
            t_y[m] = r

        def proj():
            for m in range(0, 8, 2):
                def ev(o, i, ap, tok):
                    if o < 2:
                        s = n[0] % 4
                        n[0] += 1
                        r = self.act(th[s], ap, ACT.Tanh, tok, thb, th_free[s], bias=hb[:, m + o:m + o + 1],
                                     scale=0.5)
                        self.give(i, r)
                        r = self.ts(V, th[s], th[s], 0.5, 0.5, ALU.mult, ALU.add, r)
                        res[o] = (r, s)
                    else:
                        r0, s = res[o - 2]
                        f = m + o - 2
                        r = self.stt(hT[:, f, 30:542], ap, self.p("cv_bin", f, 1), th[s], ALU.add, ALU.mult, tok, r0,
                                     hold)
                        self.give(i, r)
                        th_free[s] = [r]
                        t_h[f] = r
                pieces = (("conv_w_in_2", 0, 1024 + m * 128, 1024 + m * 128 + 256),
                          ("conv_w_in_2", 0, m * 128, m * 128 + 256))
                yield from self.gemm(8, pieces, xa, self.t_xT, "F", 4, ev, gain=gain)

        def convs():
            for m in range(8):
                while m not in t_h:
                    yield
                yield from conv(m)
        drive((proj(), 1), (convs(), 2))
        ones = self.c("ones")
        ib, mb, bt = self.bank()
        for m in range(8):
            tok = self.mm(mb[:, :], ones, y[:, m, :], m == 0, m == 7, t_y[m], bt, self.t_cst, sig=(m == 7))
        mu, rs = self.u(8432, 512), self.u(8944, 512)
        hold2 = self.snap()
        a = self.ts(V, mu, mb[:, :], 1.0 / D, None, ALU.mult, None, tok, hold2)
        self.give(ib, a)
        iv, vb, bt = self.bank()
        sq = [self.u(9456, 512), self.u(9968, 512)]
        sf = [hold2, hold2]
        t_d = {}
        for m in range(8):
            d = self.tt(V, y[:, m, :], y[:, m, :], mu, ALU.subtract, a, t_y[m], tok)
            t_d[m] = d
            q = self.act(sq[m % 2], y[:, m, :], ACT.Square, d, sf[m % 2])
            tok2 = self.mm(vb[:, :], ones, sq[m % 2], m == 0, m == 7, q, bt, sig=True)
            sf[m % 2] = [tok2]
        r = self.ts(V, rs, vb[:, :], 1.0 / D, RMS_EPS, ALU.mult, ALU.add, tok2, hold2)
        self.give(iv, r)
        q = self.tt(G, rs, rs, self.c("pw")[:, 0:1].broadcast_to([128, 512]), ALU.pow, r, self.t_cst)
        keep = []
        for m in range(8):
            ym = y[:, m, :]
            d = self.tt(V, ym, ym, rs, ALU.mult, q, t_d[m], tok2)
            e = self.act(ym, ym, ACT.Silu, d, self.t_par, bias=self.p("cln_b", m, 1), scale=self.p("cln_g", m, 1))
            keep += self.split(self.ah[:, m, :], self.al[:, m, :], ym, e, self.a_free)
        self.free_ar = self.snap()
        self.resid2(8, lambda hf: self.cols("conv_w_out_2", 0, hf * 512, hf * 512 + 512), (self.ah, self.al, 0), keep)

    def cross2(self, l):
        V, A, G, T = self.V, self.A, self.G, self.T
        ins = self.ins
        hold = self.free_ar
        qT = self.u(0, 4096).rearrange("p (j s) -> p j s", j=8)
        kT = self.u(4096, 2048).rearrange("p (j s) -> p j s", j=8)
        vm = self.u(6144, 2048).rearrange("p (t c) -> p t c", t=2)
        raw = self.u(8192, 2048).rearrange("p (t c) -> p t c", t=4)
        sq = self.u(10240, 512)
        gq = [self.u(10752, 256), self.u(11008, 256)]
        mrow = self.u(11264, 1024)
        pb, ptb, ob = self.u(11264, 1024), self.u(12288, 1024), self.u(13312, 1024)
        tgain = [self.load(gq[0], ins["cross_q_norm_2"][l:l + 1, :].broadcast_to([128, 256]), hold),
                 self.load(gq[1], ins["cross_k_norm_2"][l:l + 1, :].broadcast_to([128, 256]), hold)]
        tm = self.mem_operand("mem_2T", 8192, hold)
        rs = self.st[:, 64:66]
        fr = hold
        w = []
        for t in range(2):
            k = self.load(mrow, ins["mem_2"][t * 128:t * 128 + 128, :], fr)
            s = self.act(mrow, mrow, ACT.Square, k, acc=rs[:, t:t + 1])
            fr = [s]
            w.append(s)
        t_rs = self.rstd(rs, rs, 1.0 / D, RMS_EPS, w)
        ma = (self.ah, self.al, 0)
        t_k, t_v, t_q = [], [], []
        rfree = [tm, hold]
        for cg in range(2):
            t_r = {}

            def er(t, i, ap, tok):
                r = self.ts(V, raw[:, t, :], ap, rs[:, t:t + 1], None, ALU.mult, None, tok, t_rs, rfree)
                self.give(i, r)
                t_r[t] = r
            drive((self.gemm(8, self.cols("cross_wk_2", l, cg * 512, cg * 512 + 512), ma, tm, "T", 2, er,
                             gain=("n_mem", l * 8)), 1))
            pv = None
            for t in range(2):
                wv = self.head_norm(raw[:, t, :], 2, 256, [(0, 2, gq[1])], sq, 2 + t * 2, t_r[t], tgain, hold, pv)
                pv = wv

                def dst(j, m, i, v, tok, t=t):
                    c = self.cp(A, kT[:, cg * 4 + j:cg * 4 + j + m, t * 128:t * 128 + 128], v, tok, hold)
                    self.give(i, c)
                    t_k.append(c)
                self.turn(raw[:, t, :], 4, wv, dst)
            rfree = [T.last()]
        for cg in range(2):
            def ev(t, i, ap, tok):
                r = self.ts(V, vm[:, t, cg * 512:cg * 512 + 512], ap, rs[:, t:t + 1], None, ALU.mult, None, tok,
                            t_rs, hold)
                self.give(i, r)
                t_v.append(r)
            drive((self.gemm(8, self.cols("cross_wv_2", l, cg * 512, cg * 512 + 512), ma, tm, "T", 2, ev,
                             gain=("n_mem", l * 8)), 1))
        self.a_free = [T.last()]
        for cg in range(2):
            t_r = {}

            def er(t, i, ap, tok):
                r = self.cp(A, raw[:, t, :], ap, tok, rfree)
                self.give(i, r)
                t_r[t] = r
            drive((self.gemm(8, self.cols("cross_wq_2", l, cg * 512, cg * 512 + 512), (self.xh, self.xl, 0),
                             self.t_xT, "T", 4, er, gain=("n_cross", l * 8)), 1))
            pv = None
            for t in range(NT):
                wv = self.head_norm(raw[:, t, :], 2, 256, [(0, 2, gq[0])], sq, 8 + t * 2, t_r[t], tgain, hold, pv)
                pv = wv

                def dst(j, m, i, v, tok, t=t):
                    c = self.cp(A, qT[:, cg * 4 + j:cg * 4 + j + m, t * 128:t * 128 + 128], v, tok, hold)
                    self.give(i, c)
                    t_q.append(c)
                self.turn(raw[:, t, :], 4, wv, dst)
            rfree = [T.last()]
        freeP = self.snap()
        keep = []

        def put(t, c, o, toks):
            self.turn_split(o, 4, toks, self.ah, self.al, 4 * c, t, keep, self.a_free)
        drive((self.attend(
            4, 256, lambda h, t, k0, k1: [(qT[:, 2 * h + q, t * 128:t * 128 + 128], kT[:, 2 * h + q, :])
                                          for q in range(2)],
            lambda t: (0, 2), lambda h, k: vm[:, k, h * 256:h * 256 + 256], 256 ** -0.5, [t_k, t_v, t_q], freeP,
            pb, ptb, ob, put), 1))
        self.free_ar = self.snap()
        self.resid2(8, lambda hf: self.cols("cross_wo_2", l, hf * 512, hf * 512 + 512), (self.ah, self.al, 0), keep)

    def ffn2(self, l):
        V, A, G, T = self.V, self.A, self.G, self.T
        hold = self.free_ar
        xa = (self.xh, self.xl, 0)
        bufs = [self.u(q * 512, 512) for q in range(6)]
        b_free = [hold] * 6
        nb = 0
        for half, (m0, m1) in enumerate(((0, 12), (12, 22))):
            keep = []
            for m in range(m0, m1, 2):
                res = {}

                def ev(o, i, ap, tok):
                    nonlocal nb
                    if o < 2:
                        s = nb % 6
                        nb += 1
                        r = self.act(bufs[s], ap, ACT.Silu, tok, b_free[s])
                        self.give(i, r)
                        res[o] = (r, s)
                    else:
                        r0, s = res[o - 2]
                        r = self.tt(V, bufs[s], bufs[s], ap, ALU.mult, tok, r0)
                        self.give(i, r)
                        k = m - m0 + o - 2
                        w = self.split(self.ah[:, k, :], self.al[:, k, :], bufs[s], r, self.a_free)
                        b_free[s] = w
                        keep.extend(w)
                pieces = (("ffn_w_gate_2", l, m * 128, m * 128 + 256), ("ffn_w_up_2", l, m * 128, m * 128 + 256))
                drive((self.gemm(8, pieces, xa, self.t_xT, "F", 4, ev, gain=("n_ffn", l * 8)), 1))
            self.x_free = [T.last()]
            drive((self.residual(m1 - m0, lambda hf: (("ffn_w_down_2", (l, m0), hf * 512, hf * 512 + 512),),
                                 (self.ah, self.al, 0), keep, lambda t, r: None, scale=False), 1))
            self.a_free = [T.last()]
        self.free_ar = self.snap()
        if l < DEPTH - 1:
            drive((self.turn_x(rms=True), 1))

    def emit(self):
        nc = self.nc
        sems = [self.ctx.enter_context(nc.semaphore(f"s{i}")) for i in range(self.nsem)]
        block = self.ctx.enter_context(nc.Block())
        for name, lane in (("tensor", self.T), ("vector", self.V), ("scalar", self.A), ("gpsimd", self.G),
                           ("sync", self.Y)):
            reg = {"tensor": block.tensor, "vector": block.vector, "scalar": block.scalar,
                   "gpsimd": block.gpsimd, "sync": block.sync}[name]
            reg(lambda eng, lane=lane: lane.play(eng, sems))
        self.ctx.close()


def new_program(nc, ins, out, plan, stage=None, dumps=None):
    p = Program(nc, ins, out, plan, stage, dumps)
    p.a_free = None
    p.x_free = None
    p.build()
    return p


def tables():
    c = np.zeros((128, NCST), np.float32)

    def put(name, a):
        at, n = CST[name]
        c[:, at:at + n] = a
    put("ident", np.eye(128))
    put("ones", 1.0)
    i, j = np.arange(128)[:, None], np.arange(384)[None, :]
    put("band", np.where((j >= i) & (j <= i + 256), 0.0, BIG))
    put("causal", np.where(np.arange(128)[None, :] <= i, 0.0, BIG))

    def angles(pos, half, theta, d):
        inv = np.float32(theta) ** (-np.arange(half, dtype=np.float32) * np.float32(2.0 / d))
        return pos.astype(np.float32)[:, None] * inv[None, :].astype(np.float32)

    def table(cn, sn, ang):
        n = ang.shape[1]
        for name, f in ((cn, np.cos), (sn, np.sin)):
            put(name, f(ang).astype(np.float32).reshape(NT, 128, n).transpose(1, 0, 2).reshape(128, NT * n))
    pos = np.arange(S)
    table("cosA", "sinA", angles(pos, 32, 10000.0, 64))
    table("cosB", "sinB", np.concatenate([angles(pos // 64, 16, 10000.0, 32), angles(pos % 64, 16, 10000.0, 32)], 1))
    table("cosq", "sinq", angles(pos, 16, 500000.0, 32))
    table("cosi", "sini", angles(pos, 8, 500000.0, 16))
    pw = np.full((128, 16), -0.5)
    pw[:, 15] = 0.5
    put("pw", pw)
    t = np.arange(16)
    put("invc", np.concatenate([1.0 / np.minimum(t + 1, w) for w in POOL_W])[None, :])
    return c


_SHAPES = {"x": (S, D), "mem_2": (256, D), "xT": (128, 8 * S), "memT": (128, 2048), "mem_2T": (128, 2048),
           "c_bs": (2, 512), "wsT": (2, 128, 512), "pool_w_2": (4, 128, 128), "par": (128, NPAR),
           "cst": (128, NCST), "a_sink": (2, 8), "b_q_gain": (2, 64), "b_k_gain": (2, 64), "c_ln_g": (2, 512),
           "c_ln_b": (2, 512), "a_q_norm_2": (1, 128), "a_k_norm_2": (1, 128), "cross_q_norm_2": (2, 256),
           "cross_k_norm_2": (2, 256), "ln1_g": (2, D), "ln1_b": (2, D), "ln2_g": (2, D), "ln2_b": (2, D),
           "ln3_g": (2, D), "ln3_b": (2, D)}


def the_plan(nc, stage=None):
    ins = {k: nc.dram_tensor("p_" + k, v, F32, kind="ExternalInput").ap() for k, v in _SHAPES.items()}
    out = nc.dram_tensor("p_out", (S, D), F32, kind="ExternalOutput").ap()
    p = new_program(nc, ins, out, None, stage)
    p.ctx.close()
    return p.units


_INS = ["ln1_g", "ln1_b", "ln2_g", "ln2_b", "ln3_g", "ln3_b", "a_sink", "b_q_gain", "b_k_gain", "c_ln_g", "c_ln_b",
        "a_q_norm_2", "a_k_norm_2", "cross_q_norm_2", "cross_k_norm_2"]


def lay_out(inputs, plan):
    g = {k: np.asarray(v) for k, v in inputs.items()}
    a = {k: np.ascontiguousarray(g[k]) for k in _INS}
    a["x"] = np.ascontiguousarray(g["x"][0])
    a["mem_2"] = np.ascontiguousarray(g["mem_2"][0])

    def feature_major(m):
        n = m.shape[0]
        return np.ascontiguousarray(m.T.reshape(8, 128, n).transpose(1, 0, 2).reshape(128, 8 * n))
    a["xT"] = feature_major(g["x"][0])
    a["memT"] = feature_major(g["mem"][0])
    a["mem_2T"] = feature_major(g["mem_2"][0])
    a["c_bs"] = np.ascontiguousarray(g["c_bs"].reshape(2, 512))
    a["wsT"] = np.ascontiguousarray(g["c_ws"].transpose(0, 3, 1, 2).reshape(2, 128, 512))
    a["pool_w_2"] = np.ascontiguousarray(g["pool_w_2"][0])
    par = np.zeros((128, NPAR), np.float32)

    def put(name, m):
        at, n = PAR[name]
        par[:, at:at + n] = m

    def cols(m):
        m = m.reshape(-1, 128)
        return m.T
    put("b_gate", cols(g["b_gate"]))
    put("conv_k", cols(g["f_conv_k"]))
    put("conv_b", cols(g["f_conv_b"]))
    put("pool_scale", cols(g["pool_scale_2"]))
    put("cv_bin", cols(g["conv_b_in_2"]))
    put("dw_w", g["conv_dw_w_2"][0].reshape(31, 8, 128).transpose(2, 1, 0).reshape(128, 248))
    put("dw_b", cols(g["conv_dw_b_2"]))
    put("cln_g", cols(g["conv_ln_g_2"]))
    put("cln_b", cols(g["conv_ln_b_2"]))
    for n, k in (("n_mix", "norm_mix_2"), ("n_cross", "norm_cross_2"), ("n_mem", "norm_mem_2"), ("n_ffn", "norm_ffn_2")):
        put(n, cols(g[k]))
    a["par"] = par
    a["cst"] = tables()
    pk = np.zeros((len(plan), 128, 1024), np.float32)
    for j, (k0, nk, pieces, _) in enumerate(plan):
        at = 0
        width = sum(p[3] - p[2] for p in pieces)
        dst = pk[j, :, 0:nk * width].reshape(128, nk, width)
        for name, idx, c0, c1 in pieces:
            w, r0 = g[name], 0
            if isinstance(idx, tuple):
                if "down" in name:
                    w, r0 = w[idx[0]], idx[1] * 128
                else:
                    w = w[idx[0]][idx[1]]
            else:
                w = w[idx]
            r = r0 + k0 * 128
            dst[:, :, at:at + c1 - c0] = w[r:r + nk * 128, c0:c1].reshape(nk, 128, c1 - c0).transpose(1, 0, 2)
            at += c1 - c0
    a["wpk"] = pk
    return a


def kernel(**inputs):
    import concourse.bacc as _bacc
    from concourse import mybir as _mybir
    from concourse.bass_utils import run_bass_kernel_spmd as _run

    plan = the_plan(_bacc.Bacc("TRN2", target_bir_lowering=False, num_devices=1))
    arrays = lay_out(inputs, plan)
    nc = _bacc.Bacc("TRN2", target_bir_lowering=False, num_devices=1)
    ins = {k: nc.dram_tensor("in_" + k, v.shape, _mybir.dt.float32, kind="ExternalInput").ap()
           for k, v in arrays.items()}
    out = nc.dram_tensor("out_0", (S, D), _mybir.dt.float32, kind="ExternalOutput").ap()
    new_program(nc, ins, out, plan).emit()
    r = _run(nc, [{"in_" + k: v for k, v in arrays.items()}], core_ids=[0])
    return r.results[0]["out_0"].reshape(1, S, D)
```

```python
from contextlib import ExitStack

import numpy as np
import concourse.bass as bass
from concourse import mybir

F32 = mybir.dt.float32
F32R = mybir.dt.float32r
ALU = mybir.AluOpType
ACT = mybir.ActivationFunctionType
AX = mybir.AxisListType

S = 512
D = 1024
NT = 4
DEPTH = 2
ALPHA = (2 * DEPTH) ** 0.25
LN_EPS = 1e-5
RMS_EPS = 1e-6
BIG = -1.0e30
GONE = -3.0e38

CST = {}
PAR = {}


def _columns(table, entries):
    at = 0
    for name, n in entries:
        table[name] = (at, n)
        at += n
    return at


NCST = _columns(CST, [
    ("ident", 128), ("band", 384), ("causal", 128), ("cosA", 128), ("sinA", 128), ("cosB", 128), ("sinB", 128),
    ("cosq", 64), ("sinq", 64), ("cosi", 32), ("sini", 32), ("ones", 128), ("pw", 16), ("invc", 64),
])
NPAR = _columns(PAR, [
    ("b_gate", 48), ("conv_k", 264), ("conv_b", 88), ("pool_scale", 4), ("cv_bin", 16), ("dw_w", 248), ("dw_b", 8),
    ("cln_g", 8), ("cln_b", 8), ("n_mix", 16), ("n_cross", 16), ("n_mem", 16), ("n_ffn", 16),
])
POOL_W = (2, 4, 8, 16)


class Lane:

    def __init__(self, sem):
        self.sem, self.n, self.seen, self.queue = sem, 0, {}, []

    def __call__(self, make, *waits, sig=True, sem=None, by=1):
        need = {}
        stack = list(waits)
        while stack:
            w = stack.pop()
            if isinstance(w, list):
                stack += w
            elif w is not None:
                need[w[0]] = max(need.get(w[0], 0), w[1])
        for s, v in need.items():
            if self.seen.get(s, 0) < v:
                self.seen[s] = v
                self.queue.append((None, s, v))
        if sem is not None:
            sem[1] += by
            self.queue.append((make, sem[0], by))
            return (sem[0], sem[1])
        if sig:
            self.n += 1
        self.queue.append((make, self.sem if sig else None, 1))
        return (self.sem, self.n) if sig else None

    def last(self):
        return (self.sem, self.n)

    def play(self, eng, sems):
        for make, s, v in self.queue:
            if make is None:
                eng.wait_ge(sems[s], v)
            else:
                i = make(eng)
                if s is not None:
                    i.then_inc(sems[s], v)


def drive(*gens):
    live = [[g, r] for g, r in gens]
    while live:
        for item in list(live):
            for _ in range(item[1]):
                try:
                    next(item[0])
                except StopIteration:
                    live.remove(item)
                    break


def unit_shape(desc):
    nk, pieces = desc[1], desc[2]
    return nk, sum(p[3] - p[2] for p in pieces)


class Program:
    def __init__(self, nc, ins, out, plan, stage=None, dumps=None):
        self.nc, self.ins, self.out, self.plan = nc, ins, out, plan
        self.stage, self.dumps = stage, dumps
        self.park = nc.dram_tensor("park", (S, D), F32, kind="Internal").ap()
        self.units = []
        self.marks, self.npe = [], 0
        self.nsem = 0
        self.T, self.V, self.A, self.G, self.Y = (Lane(self.newsem()) for _ in range(5))
        self.ctx = ExitStack()
        sb = lambda n, s, d=F32: self.ctx.enter_context(nc.sbuf_tensor(n, s, d))
        self.x = sb("x", [128, NT, D])
        self.xh, self.xl = sb("xh", [128, 8, S], F32R), sb("xl", [128, 8, S], F32R)
        self.ah, self.al = sb("ah", [128, 12, S], F32R), sb("al", [128, 12, S], F32R)
        self.NR = 3
        self.wr = sb("wr", [128, self.NR, 1024])
        self.wh, self.wl = sb("wh", [128, self.NR, 1024], F32R), sb("wl", [128, self.NR, 1024], F32R)
        self.gb = sb("gb", [128, 2, D])
        self.cst, self.par = sb("cst", [128, NCST]), sb("par", [128, NPAR])
        self.st = sb("st", [128, 320])
        self.NU = 14700
        self.ar = sb("ar", [128, self.NU])
        self.bk = [self.ctx.enter_context(nc.psum_tensor(f"bk{i}", [128, 512], F32)) for i in range(8)]
        self.free = [(i, None) for i in range(8)]
        self.wr_sem = [[self.newsem(), 0] for _ in range(self.NR)]
        self.wr_free = [None] * self.NR
        self.w_free = [None] * self.NR
        self.w_ready = {}
        self.w_dma = self.w_split = 0
        self.nuse = self.w_rel = 0
        self.look = 2
        self.pending = []
        self.io = [self.newsem(), 0]
        self.stores = []

    def newsem(self):
        self.nsem += 1
        return self.nsem - 1

    def c(self, name):
        a, n = CST[name]
        return self.cst[:, a:a + n]

    def p(self, name, i=0, n=None):
        a, m = PAR[name]
        return self.par[:, a + i:a + (m if n is None else i + n)]

    def u(self, a, n):
        assert a + n <= self.NU, (a, n)
        return self.ar[:, a:a + n]

    def snap(self):
        return [x.last() for x in (self.T, self.V, self.A, self.G)]

    def bank(self):
        i, toks = self.free.pop(0)
        return i, self.bk[i], toks

    def give(self, i, *toks):
        self.free.append((i, list(toks)))

    def load(self, dst, src, *waits, eng=None):
        s = [self.newsem(), 0]
        return (eng or self.Y)(lambda e: e.dma_start(dst, src), *waits, sem=s, by=16)

    def dump(self, name, ap, *waits):
        if self.dumps is not None and name in self.dumps:
            d = self.dumps[name]
            self.stores.append(self.load(d, ap, *waits))

    def tt(self, lane, out, a, b, op, *w):
        return lane(lambda e: e.tensor_tensor(out, a, b, op), *w)

    def ts(self, lane, out, a, s1, s2, o1, o2, *w):
        if s2 is None:
            return lane(lambda e: e.tensor_scalar(out, a, s1, None, o1), *w)
        return lane(lambda e: e.tensor_scalar(out, a, s1, s2, o1, o2), *w)

    def stt(self, out, a, s, b, o1, o2, *w):
        return self.V(lambda e: e.scalar_tensor_tensor(out, a, s, b, o1, o2), *w)

    def cp(self, lane, out, a, *w):
        if lane is self.A:
            return lane(lambda e: e.activation(out, a, ACT.Copy), *w)
        return lane(lambda e: e.tensor_copy(out, a), *w)

    def act(self, out, a, f, *w, bias=0.0, scale=1.0, acc=None):
        if acc is not None:
            return self.A(lambda e: e.activation(out, a, f, bias=bias, scale=scale, accum_out=acc), *w)
        return self.A(lambda e: e.activation(out, a, f, bias=bias, scale=scale), *w)

    def acopy(self, out, a, scale, *w):
        return self.A(lambda e: e.activation(out, a, ACT.Copy, scale=scale), *w)

    def mark(self, name):
        self.marks.append((name, self.npe))

    def mm(self, out, l, r, start, stop, *w, sig=False):
        self.npe += 1 if l.dtype == F32R else 2
        return self.T(lambda e: e.matmul(out, l, r, start=start, stop=stop), *w, sig=sig)

    def tr(self, out, a, *w, sig=False):
        self.npe += 1
        ident = self.c("ident")
        return self.T(lambda e: e.transpose(out, a, ident), *w, sig=sig)

    def split(self, h, l, src, *w, scale=None):
        hf = h.bitcast(F32)
        if scale is None:
            a = self.cp(self.A, h, src, *w)
            return [a, self.tt(self.V, l, src, hf, ALU.subtract, a, *w)]
        a = self.acopy(h, src, scale, *w)
        return [a, self.stt(l, src, scale, hf, ALU.mult, ALU.subtract, a, *w)]

    def w_prefetch(self, i):
        plan = self.plan if self.plan is not None else self.units
        n = len(plan)
        while self.w_split < min(i + 1 + self.look, self.w_rel + self.NR, n):
            self._w_load(min(self.w_split + 1, n))
            j, r = self.w_split, self.w_split % self.NR
            nk, cols = unit_shape(plan[j])
            gain = plan[j][3]
            got = (self.wr_sem[r][0], 16 * (j // self.NR + 1))
            if gain is None:
                m = nk * cols
                toks = self.split(self.wh[:, r, 0:m], self.wl[:, r, 0:m], self.wr[:, r, 0:m], got, self.w_free[r])
            else:
                toks = []
                for k in range(nk):
                    g = self.p(gain[0], gain[1] + k, 1)
                    a = k * cols
                    toks += self.split(self.wh[:, r, a:a + cols], self.wl[:, r, a:a + cols],
                                       self.wr[:, r, a:a + cols], got, self.w_free[r], self.t_par, scale=g)
            self.w_ready[j] = toks
            self.wr_free[r] = toks
            self.w_split += 1
        self._w_load(min(self.w_split + self.NR, n))

    def _w_load(self, upto):
        upto = min(upto, len(self.plan or self.units))
        while self.w_dma < upto:
            j, r = self.w_dma, self.w_dma % self.NR
            if j >= self.w_split + self.NR:
                break
            nk, cols = unit_shape((self.plan or self.units)[j])
            m = nk * cols
            dst = self.wr[:, r, 0:m]
            src = None if self.plan is None else self.ins["wpk"][j, :, 0:m]
            self.Y(lambda e, dst=dst, src=src: e.dma_start(dst, src), self.wr_free[r], sem=self.wr_sem[r], by=16)
            self.w_dma += 1

    def w_use(self, desc):
        i = self.nuse
        self.nuse += 1
        if self.plan is None:
            self.units.append(desc)
        else:
            assert self.plan[i] == desc
        self.w_prefetch(i)
        r = i % self.NR
        nk, cols = unit_shape(desc)
        view = lambda t: t[:, r, 0:nk * cols].rearrange("p (k c) -> p k c", k=nk)
        return view(self.wh), view(self.wl), self.w_ready[i], i

    def w_done(self, i, tok):
        assert i == self.w_rel
        self.w_rel += 1
        self.w_free[i % self.NR] = tok

    def gemm(self, nk, pieces, act, toks, orient, nout, evac, gain=None, per=None, width=None, pair=False,
             hooks=None):
        ah, al, base = act
        cols = sum(p[3] - p[2] for p in pieces)
        per = per or max(1, 1024 // cols)
        width = width or S
        nu = -(-nk // per)
        banks = [self.bank() for _ in range(nout)]
        outs = list(range(nout))
        steps, q = [], min(self.NR, nu)
        if pair:
            for half in range(2):
                for u in range(q):
                    steps.append((u, outs, half) if orient == "F" else (u, outs[2 * half:2 * half + 2], None))
                if half == 0:
                    steps.append(None)
            steps += [(u, outs, None) for u in range(q, nu)]
        elif hooks is not None:
            steps += [(u, outs, None) for u in range(nu - q)]
            for half in range(2):
                for u in range(nu - q, nu):
                    steps.append((u, outs[2 * half:2 * half + 2], None))
        else:
            steps = [(u, outs, None) for u in range(nu)]
        last = {}
        for j, s in enumerate(steps):
            if s is not None:
                last[s[0]] = j
        first, units = set(), {}
        for j, s in enumerate(steps):
            if s is None:
                self.flush()
                continue
            u, os_, half = s
            k0 = u * per
            n = min(per, nk - k0)
            if u not in units:
                units[u] = self.w_use((k0, n, tuple(pieces), None if gain is None else (gain[0], gain[1] + k0)))
            h, l, wt, ui = units[u]
            c0, c1 = (0, width) if half is None else (half * 256, half * 256 + 256)
            for o in os_:
                i, bk, bt = banks[o]
                at = toks
                if isinstance(toks, dict):
                    tiles = [o] if orient == "T" else range(c0 // 128, c1 // 128)
                    at = [toks[t] for t in tiles]
                for kk in range(n):
                    k = k0 + kk
                    kb = base[k] if isinstance(base, list) else base + k
                    a = slice(o * 128, o * 128 + 128)
                    if orient == "F":
                        xh, xl = ah[:, kb, c0:c1], al[:, kb, c0:c1]
                        seq = [(h[:, kk, a], xh), (h[:, kk, a], xl), (l[:, kk, a], xh)]
                        ap, whole = bk[:, c0:c1], bk[:, 0:width]
                    else:
                        xh, xl = ah[:, kb, a], al[:, kb, a]
                        seq = [(xh, h[:, kk, :]), (xh, l[:, kk, :]), (xl, h[:, kk, :])]
                        ap = whole = bk[:, 0:cols]
                    for q, (lw, rw) in enumerate(seq):
                        st = o not in first
                        first.add(o)
                        end = k == nk - 1 and q == 2 and half != 0
                        sig = (kk == n - 1 and q == 2) and (end or o == os_[-1])
                        t = self.mm(ap, lw, rw, st, end, wt, at, bt if st else None, sig=sig)
                if k0 + n == nk and half != 0:
                    evac(o, i, whole, t)
            if last[u] == j:
                self.w_done(ui, t)
                self.w_prefetch(ui)
            if hooks is not None:
                f = hooks.get(j - len(steps))
                if f is not None:
                    f()
            yield

    def turn(self, src, n, toks, dst):
        for j in range(0, n, 4):
            m = min(4, n - j)
            i, bk, bt = self.bank()
            for q in range(m):
                t = self.tr(bk[:, q * 128:q * 128 + 128], src[:, (j + q) * 128:(j + q + 1) * 128],
                            toks, bt, self.t_cst, sig=(q == m - 1))
            dst(j, m, i, bk[:, 0:m * 128].rearrange("p (j c) -> p j c", j=m), t)

    def turn_split(self, src, n, toks, hi, lo, base, t, keep, *w):
        def dst(j, m, i, v, tok):
            a = slice(t * 128, t * 128 + 128)
            got = self.split(hi[:, base + j:base + j + m, a], lo[:, base + j:base + j + m, a], v, tok, *w)
            self.give(i, got[1])
            keep.extend(got)
        self.turn(src, n, toks, dst)

    def rstd(self, out, var, scale, eps, *w):
        g = self.ts(self.G, out, var, scale, eps, ALU.mult, ALU.add, *w)
        n = out.shape[-1]
        pw = self.c("pw")[:, 0:n]
        return self.tt(self.G, out, out, pw, ALU.pow, g, self.t_cst)

    def residual(self, nk, pieces, act, toks, norm=None, pre=None, scale=False):
        def turn(t, got):
            def f():
                self.turn_split(got[t][0], 8, got[t][1], self.xh, self.xl, 0, t, keep[t])
                if got[t][2] is not None:
                    self.t_xn[got[t][2]] = [self.T.last()]
                self.t_xr = [self.T.last()]
            return f
        keep = {t: [] for t in range(NT)}
        got, tok_r = {}, {}
        for hf in range(2):
            def evac(t, i, ap, tok, hf=hf):
                xs = self.x[:, t, hf * 512:hf * 512 + 512]
                w = [tok, self.t_x[t], self.t_xr]
                if scale:
                    r = self.stt(xs, xs, ALPHA, ap, ALU.mult, ALU.add, *w)
                else:
                    r = self.tt(self.V, xs, xs, ap, ALU.add, *w)
                self.give(i, r)
                tok_r.setdefault(t, []).append(r)
                if hf == 0:
                    if pre is not None:
                        pre(t, r)
                    return
                self.t_x[t] = list(tok_r[t])
                if norm is not None and t < 2:
                    got[t] = norm(t, self.t_x[t])
            hooks = None
            if norm is not None and hf == 1:
                hooks = {-2: lambda: turn(0, got)()}
            yield from self.gemm(nk, pieces(hf), act, toks, "T", 4, evac, hooks=hooks)
        if norm is not None:
            turn(1, got)()
            got[2] = norm(2, self.t_x[2])
            got[3] = norm(3, self.t_x[3])
            self.t_xT = keep
            self.pending += [turn(2, got), turn(3, got)]
            self.mark(' next')

    def flush(self):
        for f in self.pending:
            f()
        self.pending = []

    def ln_pre(self, t, r):
        st = self.st[:, t * 16:t * 16 + 12]
        x = self.x[:, t, :]
        self.t_pre[t] = self.V(lambda e: e.bn_stats(st[:, 0:6], x[:, 0:512]), r, self.t_ln[t])

    def ln_turn(self, tg):
        def norm(t, r):
            d = self.ln_chain(t, r, tg)
            return self.x[:, t, :], [d], None
        return norm

    def rms_turn(self, slots, tg=None):
        def norm(t, r):
            if tg is not None:
                r = [self.ln_chain(t, r, tg)]
            s, x = slots[t % 2], self.x[:, t, :]
            ss, rs = self.st[:, 240 + t:241 + t], self.st[:, 244 + t:245 + t]
            a = self.act(s, x, ACT.Square, r, self.t_xn[t % 2], self.t_rms[t], acc=ss)
            g = self.rstd(rs, ss, 1.0 / D, RMS_EPS, a)
            b = self.acopy(s, x, rs, g, a)
            self.t_rms[t] = [b, g]
            self.t_x[t] = [self.t_x[t], b]
            return s, [b], t % 2
        return norm

    def xn_slots(self):
        return [self.gb[:, 0, :], self.gb[:, 1, :]]

    def ln_chain(self, t, r, tg):
        x = self.x[:, t, :]
        st = self.st[:, t * 16:t * 16 + 12]
        mv = self.st[:, t * 16 + 12:t * 16 + 14]
        rs = self.st[:, t * 16 + 14:t * 16 + 15]
        a = self.t_pre[t]
        b = self.V(lambda e: e.bn_stats(st[:, 6:12], x[:, 512:1024]), r)
        m = self.V(lambda e: e.bn_aggr(mv, st), a, b, self.t_ln[t])
        g = self.rstd(rs, mv[:, 1:2], 1.0, LN_EPS, m)
        c = self.stt(x, x, mv[:, 0:1], self.gb[:, 0, :], ALU.subtract, ALU.mult, m, tg)
        d = self.stt(x, x, rs, self.gb[:, 1, :], ALU.mult, ALU.add, c, g, tg)
        self.t_x[t] = [d]
        self.t_ln[t] = [d, g]
        return d

    def rope(self, src, dst, nh, g, half, cos, sin, tmp, *w):
        sh = [128, nh, g, half]
        v = lambda a: a.rearrange("p h (g w f) -> p h g w f", g=g, w=2)
        bc = lambda a: a.rearrange("p (g f) -> p g f", g=g).unsqueeze(1).broadcast_to(sh)
        x1, x2 = v(src)[:, :, :, 0, :], v(src)[:, :, :, 1, :]
        d1, d2 = v(dst)[:, :, :, 0, :], v(dst)[:, :, :, 1, :]
        n = nh * g * half
        t = [tmp[:, q * n:(q + 1) * n].rearrange("p (h g f) -> p h g f", h=nh, g=g) for q in range(4)]
        c, s = bc(cos), bc(sin)
        a = self.tt(self.V, t[0], x1, c, ALU.mult, *w)
        b = self.tt(self.V, t[1], x2, s, ALU.mult, *w)
        p = self.tt(self.V, d1, t[0], t[1], ALU.subtract, a, b, *w)
        a = self.tt(self.G, t[2], x2, c, ALU.mult, *w)
        b = self.tt(self.G, t[3], x1, s, ALU.mult, *w)
        return [p, self.tt(self.G, d2, t[2], t[3], ALU.add, a, b, *w)]

    def head_norm(self, src, nh, hd, gains, sq, col, *w):
        ss = self.st[:, 64 + col:64 + col + nh]
        a = self.act(sq, src, ACT.Square, *w)
        v = src.rearrange("p (h d) -> p h d", h=nh)
        b = self.V(lambda e: e.tensor_reduce(ss, sq.rearrange("p (h d) -> p h d", h=nh), AX.X, ALU.add), a, *w)
        g = self.rstd(ss, ss, 1.0 / hd, RMS_EPS, b)
        c = self.tt(self.V, v, v, ss.unsqueeze(2).broadcast_to([128, nh, hd]), ALU.mult, g, b)
        out = []
        for h0, n, gain in gains:
            out.append(self.tt(self.G, v[:, h0:h0 + n, :], v[:, h0:h0 + n, :],
                               gain.unsqueeze(1).broadcast_to([128, n, hd]), ALU.mult, c, *w))
        return out

    def attend(self, heads, dv, qk, keys, val, scale, ready, hold, pbuf, ptbuf, obuf, put, mask=None, sink=None,
               wide=512):
        per = 512 // dv
        nh = len(heads)
        items = [(t, q) for t in range(NT) for q in range(nh)]
        n = len(items)
        NP = 3
        nm, sm = self.st[:, 128:160], self.st[:, 160:192]
        e8 = self.st[:, 192:200]
        p_free, pt_free, o_free = [hold] * NP, [hold] * 2, [hold] * 2
        P, PT, O = {}, {}, {}
        no = 0
        later = []
        for i in range(n + 4):
            if i < n:
                t, q0 = items[i]
                k0, k1 = keys(t)
                w = (k1 - k0) * 128
                b, bk, bt = self.bank()
                prs = qk(heads[q0], t, k0, k1)
                for q, (lw, rw) in enumerate(prs):
                    s = self.mm(bk[:, 0:w], lw, rw, q == 0, q == len(prs) - 1, ready, bt, sig=(q == len(prs) - 1))
                pb = pbuf[:, (i % NP) * wide:(i % NP) * wide + w]
                ci = i % 32
                m_, s_ = nm[:, ci:ci + 1], sm[:, ci:ci + 1]
                if mask is not None:
                    mk = mask(t, k0, k1)
                    init = sink[:, q0:q0 + 1] if sink is not None else -3.0e38
                    a = self.V(lambda e, pb=pb, bk=bk, w=w, mk=mk, m_=m_, init=init: e.tensor_tensor_reduce(
                        pb, bk[:, 0:w], mk, scale, init, ALU.add, ALU.max, m_), s, p_free[i % NP], ready)
                    self.give(b, a)
                    a = self.ts(self.V, m_, m_, -1.0, None, ALU.mult, None, a)
                    e_ = self.act(pb, pb, ACT.Exp, a, bias=m_, acc=s_)
                else:
                    a = self.V(lambda e, bk=bk, w=w, m_=m_: e.tensor_reduce(m_, bk[:, 0:w], AX.X, ALU.max), s, hold)
                    a = self.ts(self.V, m_, m_, -scale, None, ALU.mult, None, a)
                    e_ = self.act(pb, bk[:, 0:w], ACT.Exp, a, p_free[i % NP], bias=m_, scale=scale, acc=s_)
                    self.give(b, e_)
                P[i] = (e_, pb, k0, k1)
            if 2 <= i <= n + 1:
                j = i - 2
                e_, pb, k0, k1 = P.pop(j)
                w = (k1 - k0) * 128
                b, bk, bt = self.bank()
                for q in range(k1 - k0):
                    tk = self.tr(bk[:, q * 128:q * 128 + 128], pb[:, q * 128:q * 128 + 128], e_, bt, self.t_cst,
                                 sig=(q == k1 - k0 - 1))
                p_free[j % NP] = [tk]
                pt = ptbuf[:, (j % 2) * wide:(j % 2) * wide + w]
                c = self.cp(self.A if j % 2 else self.V, pt, bk[:, 0:w], tk, pt_free[j % 2])
                self.give(b, c)
                PT[j] = (c, pt, k0, k1, e_)
            for f in later:
                f()
            later = []
            if 3 <= i <= n + 2:
                j = i - 3
                t, q0 = items[j]
                c, pt, k0, k1, e_ = PT.pop(j)
                if q0 % per == 0:
                    O[t, q0 // per] = self.bank() + ([],)
                b, bk, bt, es = O[t, q0 // per]
                es.append(e_)
                col = (q0 % per) * dv
                for q in range(k1 - k0):
                    tk = self.mm(bk[:, col:col + dv], pt[:, q * 128:q * 128 + 128], val(heads[q0], k0 + q), q == 0,
                                 q == k1 - k0 - 1, c, bt, ready, sig=(q == k1 - k0 - 1))
                pt_free[j % 2] = [tk]
                if q0 % per == per - 1:
                    c0 = (j - per + 1) % 32
                    sv = sm[:, c0:c0 + per]
                    w2 = es
                    if sink is not None:
                        a = self.tt(self.V, e8, sink, nm[:, c0:c0 + per], ALU.add, es, ready)
                        a = self.act(e8, e8, ACT.Exp, a)
                        w2 = [self.tt(self.V, sv, sv, e8, ALU.add, a, es)]
                    a = self.V(lambda e, sv=sv: e.reciprocal(sv, sv), w2)
                    ob = obuf[:, (no % 2) * 512:(no % 2) * 512 + 512]
                    r = self.tt(self.V, ob.rearrange("p (h d) -> p h d", h=per),
                                bk[:, :].rearrange("p (h d) -> p h d", h=per),
                                sv.unsqueeze(2).broadcast_to([128, per, dv]), ALU.mult, a, tk, o_free[no % 2])
                    self.give(b, r)

                    def fin(t=t, c=heads[q0] // per, ob=ob, r=r, k=no % 2):
                        put(t, c, ob, [r])
                        o_free[k] = [self.T.last()]
                    later.append(fin)
                    no += 1
            yield

    def build(self):
        ins, V, A, G, T = self.ins, self.V, self.A, self.G, self.T
        self.t_xn = [None, None]
        self.t_ln, self.t_rms, self.t_pre = [None] * NT, [None] * NT, [None] * NT
        xt = {}
        keep = []
        for q in range(4):
            raw = self.u(q * 1024, 1024)
            xt[q] = (raw, self.load(raw, ins["xT"][:, q * 1024:(q + 1) * 1024]))
            if q == 0:
                self._w_load(1)
        self.t_par = self.load(self.par[:, :], ins["par"])
        self.t_cst = self.load(self.cst[:, :], ins["cst"])
        for q in range(4):
            raw, tok = xt[q]
            keep += self.split(self.xh[:, q * 2:q * 2 + 2, :], self.xl[:, q * 2:q * 2 + 2, :],
                               raw.rearrange("p (k s) -> p k s", k=2), tok)
            if q == 0:
                self.w_prefetch(0)
        self.t_xT = {t: keep for t in range(NT)}
        self.t_x = [[] for _ in range(NT)]
        self.t_xr = None
        self.free_ar = self.snap()
        for l in range(DEPTH):
            self.mark('mixer1')
            self.mixer1(l)
            if self.stage == f"mix{l}":
                return self.finish()
            self.mark('cross1')
            self.cross1(l)
            if self.stage == f"cross{l}":
                return self.finish()
            self.mark('ffn1')
            self.ffn1(l)
            if self.stage == f"ffn{l}":
                return self.finish()
        for l in range(DEPTH):
            if l == 0:
                self.mark('mixer2')
                self.mixer2()
            else:
                self.mark('convmod')
                self.convmod()
            if self.stage == f"mix2{l}":
                return self.finish()
            self.mark('cross2')
            self.cross2(l)
            if self.stage == f"cross2{l}":
                return self.finish()
            self.mark('ffn2')
            self.ffn2(l)
            if self.stage == f"ffn2{l}":
                return self.finish()
        return self.finish()

    def finish(self):
        self.flush()
        for t in range(NT):
            self.stores.append(self.load(self.out[t * 128:(t + 1) * 128, :], self.x[:, t, :], self.t_x[t]))
        self.Y(None if False else (lambda e: e.nop()), self.stores, sig=False)

    def cols(self, name, idx, a, b):
        return ((name, idx, a, b),)

    def load_gb(self, g, b, l, *w):
        a = self.load(self.gb[:, 0, :], self.ins[g][l:l + 1, :].broadcast_to([128, D]), *w)
        return [a, self.load(self.gb[:, 1, :], self.ins[b][l:l + 1, :].broadcast_to([128, D]), *w)]

    def mixer1(self, l):
        V, A, G, T = self.V, self.A, self.G, self.T
        ins = self.ins
        xa = (self.xh, self.xl, 0)
        vA, vB = self.u(0, 512), self.u(512, 512)
        qkA, qkB = self.u(10368, 2560), self.u(1024, 2560)
        qT, kT = self.u(3584, 2048), self.u(5632, 1024)
        pb, ptb, ob = self.u(6656, 1536), self.u(8192, 1024), self.u(9216, 1024)
        ro, tmp, kd = self.u(6656, 640), self.u(7296, 1280), self.u(8576, 256)
        gq, gk = self.u(10240, 64), self.u(10304, 64)
        sink = self.st[:, 200:208]
        hold = self.free_ar
        tgain = [self.load(gq, ins["b_q_gain"][l:l + 1, :].broadcast_to([128, 64]), hold),
                 self.load(gk, ins["b_k_gain"][l:l + 1, :].broadcast_to([128, 64]), hold)]
        tsink = self.load(sink, ins["a_sink"][l:l + 1, :].broadcast_to([128, 8]), hold)
        t3 = lambda a: a.rearrange("p (t c) -> p t c", t=NT)
        qk3 = {"A": t3(qkA), "B": t3(qkB)}
        v3 = {"A": t3(vA), "B": t3(vB)}
        got = {"A": [], "B": []}

        def proj(br, c0):
            def e1(t, i, ap, tok):
                r = self.cp(A if t % 2 else V, qk3[br][:, t, 0:512], ap, tok, hold)
                self.give(i, r)
                got[br].append(r)

            def e2(t, i, ap, tok):
                ln = A if t % 2 else V
                r = self.cp(ln, qk3[br][:, t, 512:640], ap[:, 0:128], tok, hold)
                r2 = self.cp(ln, v3[br][:, t, :], ap[:, 128:256], tok, hold)
                self.give(i, r, r2)
                got[br].extend([r, r2])
            yield from self.gemm(8, self.cols("w_in", l, c0, c0 + 512), xa, self.t_xT, "T", 4, e1,
                                 pair=br == "A" and l > 0)
            yield from self.gemm(8, self.cols("w_in", l, c0 + 512, c0 + 768), xa, self.t_xT, "T", 4, e2)

        qT3, kT3 = qT.rearrange("p (j s) -> p j s", j=4), kT.rearrange("p (j s) -> p j s", j=2)
        qkT = {}

        def prologue(br, free_q):
            out, prev = [], hold
            for t in range(NT):
                src = qk3[br][:, t, :]
                w = [got[br]]
                if br == "B":
                    w = self.head_norm(src, 10, 64, [(0, 8, gq), (8, 2, gk)], ob[:, 0:640], t * 10, got[br], tgain,
                                       free_q, prev)
                cos, sin = self.c("cos" + br)[:, t * 32:t * 32 + 32], self.c("sin" + br)[:, t * 32:t * 32 + 32]
                r = self.rope(src.rearrange("p (h d) -> p h d", h=10), ro.rearrange("p (h d) -> p h d", h=10), 10,
                              1 if br == "A" else 2, 32 if br == "A" else 16, cos, sin, tmp, w, prev, self.t_cst)
                kv = ro[:, 512:640].rearrange("p (k d) -> p k d", k=2)
                k2 = self.cp(G, kd.rearrange("p (k w d) -> p k w d", k=2, w=2),
                             kv.unsqueeze(2).broadcast_to([128, 2, 2, 64]), r, prev)

                def put(dst3):
                    def f(j, m, i, v, tok):
                        c = self.cp(A if t % 2 else V, dst3[:, j:j + m, t * 128:t * 128 + 128], v, tok, free_q)
                        self.give(i, c)
                        out.append(c)
                    return f
                self.turn(ro[:, 0:512], 4, r, put(qT3))
                self.turn(kd, 2, [k2], put(kT3))
                prev = [T.last()]
                yield
            qkT[br] = out

        def branch(br, free_q):
            n = 0 if br == "A" else 1
            keep = {t: [] for t in range(NT)}

            def qk(h, t, k0, k1):
                a = slice((h % 2) * 64, (h % 2) * 64 + 64)
                return [(qT3[a, h // 2, t * 128:t * 128 + 128], kT3[a, h // 4, k0 * 128:k1 * 128])]

            def val(h, k):
                return v3[br][:, k, (h // 4) * 64:(h // 4) * 64 + 64]

            def put(t, c, o, toks):
                self.turn_split(o, 4, toks, self.ah, self.al, 4 * n, t, keep[t], self.a_free)
            if br == "A":
                keys = lambda t: (max(0, t - 1), min(NT, t + 2))
                mask = lambda t, k0, k1: self.c("band")[:, (k0 - t + 1) * 128:(k1 - t + 1) * 128]
                sk = sink
            else:
                keys = lambda t: (0, NT)
                mask = sk = None
            ready = [qkT[br], got[br], tsink, self.t_cst]
            yield from self.attend(range(8), 64, qk, keys, val, 0.125, ready, free_q, pb, ptb, ob, put, mask, sk)
            self.t_br[n] = keep

        self.t_br = [None] * 3
        drive((proj("A", 0), 1))
        if l > 0:
            park = [self.load(self.park[t * 128:(t + 1) * 128, :], self.x[:, t, :], self.t_x[t]) for t in range(NT)]
            self.stores += park
            back = self.park
        else:
            park, back = [], ins["x"]
        xfree0 = [park, self.t_xr]
        mg = self.x[:, :, :].rearrange("p t (h s) -> p (t h) s", h=2)
        uT = self.u(10368, 2048).rearrange("p (k s) -> p k s", k=4)
        vc = self.u(12416, 2048).rearrange("p (t c) -> p t c", t=NT)
        t_u, t_v, cz = [], [], {}

        def eu(o, i, ap, tok):
            r = self.act(uT[:, o, :], ap, ACT.Gelu, tok, cz["free"])
            self.give(i, r)
            t_u.append(r)

        def ev(t, i, ap, tok):
            r = self.act(vc[:, t, :], ap, ACT.Gelu, tok, cz["free"])
            self.give(i, r)
            t_v.append(r)

        def branchA():
            yield from prologue("A", hold)
            cz["free"] = self.snap()
            yield from branch("A", cz["free"])

        def projBu():
            yield from proj("B", 768)
            yield from self.gemm(8, self.cols("w_in", l, 1536, 2048), xa, self.t_xT, "F", 4, eu)

        self.mark(" A|B,u")
        drive((branchA(), 3), (projBu(), 1))
        freeA = self.snap()
        self.mark(" proB|v")
        drive((self.gemm(8, self.cols("w_in", l, 2048, 2560), xa, self.t_xT, "T", 4, ev), 1),
              (prologue("B", freeA), 1))
        freeB0 = self.snap()
        sgs = [self.u(1024 + 512 * q, 512) for q in range(4)]
        tms = [self.u(6656, 512), self.u(7168, 512)]
        hb = self.st[:, 208:232]
        thb = self.ts(V, hb, self.p("b_gate", l * 24, 24), 0.5, None, ALU.mult, None, self.t_par, freeB0)
        sg_free, tm_free = [freeB0] * 4, [None] * 2
        t_mg = [xfree0] * 8
        nt = [0]

        def gates(n):
            for mgp in range(2):
                t_sg = [None] * 4

                def eg(o, i, ap, tok):
                    m = mgp * 4 + o
                    r = self.act(sgs[o], ap, ACT.Tanh, tok, thb, sg_free[o], bias=hb[:, n * 8 + m:n * 8 + m + 1],
                                 scale=0.5)
                    self.give(i, r)
                    t_sg[o] = r

                def eb(o, i, ap, tok):
                    m = mgp * 4 + o
                    if n == 0:
                        r = self.stt(mg[:, m, :], sgs[o], 1.0, ap, ALU.add, ALU.mult, tok, t_sg[o], t_mg[m])
                        self.give(i, r)
                        sg_free[o] = [r]
                    else:
                        q = nt[0] % 2
                        nt[0] += 1
                        r = self.stt(tms[q], sgs[o], 1.0, ap, ALU.add, ALU.mult, tok, t_sg[o], tm_free[q])
                        self.give(i, r)
                        sg_free[o] = [r]
                        r = self.tt(G, mg[:, m, :], mg[:, m, :], tms[q], ALU.add, r, t_mg[m])
                        tm_free[q] = [r]
                    t_mg[m] = [r]
                c0 = 2560 + n * 1024 + mgp * 512
                yield from self.gemm(8, self.cols("w_in", l, c0, c0 + 512), xa, self.t_xT, "F", 4, eg)
                yield from self.gemm(4, self.cols("w_branch", (l, n), mgp * 512, mgp * 512 + 512),
                                     (self.ah, self.al, 4 * n), self.t_br[n], "F", 4, eb)

        self.mark(" B|gates0")
        drive((branch("B", freeB0), 3), (gates(0), 1))
        freeB = self.snap()
        tm_free = [freeB] * 2
        tg = self.load_gb("ln1_g", "ln1_b", l, self.gb_free())
        lg, lb, bs = self.u(3584, 512), self.u(4096, 512), self.u(4608, 512)
        wsT = self.u(5120, 512)
        tp = [self.load(lg, ins["c_ln_g"][l:l + 1, :].broadcast_to([128, 512]), freeB),
              self.load(lb, ins["c_ln_b"][l:l + 1, :].broadcast_to([128, 512]), freeB),
              self.load(bs, ins["c_bs"][l:l + 1, :].broadcast_to([128, 512]), freeB),
              self.load(wsT, ins["wsT"][l, :, :], freeB)]

        def chunks():
            vn = []
            for t in range(NT):
                st, mv, rs = (self.st[:, 64 + t * 16 + a:64 + t * 16 + b] for a, b in ((0, 6), (6, 8), (8, 9)))
                x = vc[:, t, :]
                a = V(lambda e, st=st, x=x: e.bn_stats(st, x), t_v, freeB)
                a = V(lambda e, st=st, mv=mv: e.bn_aggr(mv, st), a)
                g = self.rstd(rs, mv[:, 1:2], 1.0, LN_EPS, a)
                c = self.stt(x, x, mv[:, 0:1], lg, ALU.subtract, ALU.mult, a, tp)
                vn.append(self.stt(x, x, rs, lb, ALU.mult, ALU.add, c, g, tp))
                yield
            keep = []
            mt = [self.u(7680, 512), self.u(8192, 512)]
            mt_free = [freeB, freeB]
            for g in range(4):
                i, bk, bt = self.bank()
                for n in range(NT):
                    tok = self.mm(bk[:, n * 128:n * 128 + 128], vc[:, n, g * 128:g * 128 + 128],
                                  wsT[:, g * 128:g * 128 + 128], True, True, vn, tp, bt, sig=(n == 3))
                m = mt[g % 2]
                r = self.tt(V, m.rearrange("p (n i) -> p n i", n=4), bk[:, :].rearrange("p (n i) -> p n i", n=4),
                            bs[:, g * 128:g * 128 + 128].unsqueeze(1).broadcast_to([128, 4, 128]), ALU.add, tok, tp,
                            mt_free[g % 2])
                self.give(i, r)
                r = self.tt(V, m, m, uT[:, g, :], ALU.mult, r, t_u)
                s = self.split(self.ah[:, 8 + g, :], self.al[:, 8 + g, :], m, r, self.a_free)
                mt_free[g % 2] = s
                keep += s
                yield
            self.t_br[2] = keep
        self.mark(" C,gates12")
        drive((gates(1), 1), (chunks(), 1))
        drive((gates(2), 1))
        self.a_free = [T.last()]
        xfree = [T.last()]
        tm_ = {}
        for m in range(8):
            tm_[m] = self.split(self.xh[:, m, :], self.xl[:, m, :], mg[:, m, :], t_mg[m], xfree,
                                scale=self.c("pw")[:, 15:16])
        tm_ = [tm_[m] for m in range(8)]
        self.free_ar = self.snap()
        self.t_x = [[self.load(self.x[:, t, :], back[t * 128:(t + 1) * 128, :], tm_)] for t in range(NT)]
        self.t_xr = None
        self.mark(" mixout")
        gen = self.residual(8, lambda hf: self.cols("w_mix_out", l, hf * 512, hf * 512 + 512), xa, tm_,
                            self.ln_turn(tg), self.ln_pre, scale=True)
        drive((gen, 1))

    def chain(self, *fs):
        for f in fs:
            yield from f()

    def gb_free(self):
        return [list(self.t_x), self.t_xn[0], self.t_xn[1]]

    def mem_operand(self, name, at, *w):
        raw = self.u(at, 2048)
        tok = self.load(raw, self.ins[name], *w)
        return self.split(self.ah[:, 0:8, 0:256], self.al[:, 0:8, 0:256],
                          raw.rearrange("p (k s) -> p k s", k=8), tok, self.a_free)

    def cross1(self, l):
        V, A, T = self.V, self.A, self.T
        hold = self.free_ar
        tg = self.load_gb("ln2_g", "ln2_b", l, self.gb_free())
        kT = self.u(2048, 1024).rearrange("p (h s) -> p h s", h=4)
        vm = self.u(3072, 1024).rearrange("p (t c) -> p t c", t=2)
        qT = self.u(4096, 2048).rearrange("p (h s) -> p h s", h=4)
        pb, ptb, ob = self.u(6144, 1024), self.u(7168, 1024), self.u(8192, 1024)
        tm = self.mem_operand("memT", 0, hold)
        ma = (self.ah, self.al, 0)
        t_k, t_v, t_q = [], [], []

        def ek(o, i, ap, tok):
            r = self.cp(A if o % 2 else V, kT[:, o, :], ap, tok, hold)
            self.give(i, r)
            t_k.append(r)

        def ev(t, i, ap, tok):
            r = self.cp(A if t % 2 else V, vm[:, t, :], ap, tok, hold)
            self.give(i, r)
            t_v.append(r)

        def eq(o, i, ap, tok):
            r = self.cp(A if o % 2 else V, qT[:, o, :], ap, tok, hold)
            self.give(i, r)
            t_q.append(r)
        drive((self.gemm(8, self.cols("x_wkv", l, 0, 512), ma, tm, "F", 4, ek, width=256), 1))
        self.flush()
        drive((self.gemm(8, self.cols("x_wkv", l, 512, 1024), ma, tm, "T", 2, ev), 1))
        self.a_free = [T.last()]
        self.mark(' q')
        drive((self.gemm(8, self.cols("x_wq", l, 0, 512), (self.xh, self.xl, 0), self.t_xT, "F", 4, eq), 1))
        keep = {t: [] for t in range(NT)}

        def put(t, c, o, toks):
            self.turn_split(o, 4, toks, self.ah, self.al, 0, t, keep[t], self.a_free)
        self.mark(' att')
        drive((self.attend(
            range(4), 128, lambda h, t, k0, k1: [(qT[:, h, t * 128:t * 128 + 128], kT[:, h, :])], lambda t: (0, 2),
            lambda h, k: vm[:, k, h * 128:h * 128 + 128], 128 ** -0.5, [t_k, t_v, t_q], hold, pb, ptb, ob, put,
            wide=256), 1))
        self.free_ar = self.snap()
        self.mark(' wo')
        drive((self.residual(4, lambda hf: self.cols("x_wo", l, hf * 512, hf * 512 + 512), (self.ah, self.al, 0),
                             keep, self.ln_turn(tg), self.ln_pre, scale=True), 1))
        self.a_free = [T.last()]

    def ffn1(self, l):
        V, A, G, T = self.V, self.A, self.G, self.T
        hold = self.free_ar
        tg = self.load_gb("ln3_g", "ln3_b", l, self.gb_free())
        xa = (self.xh, self.xl, 0)
        FT = 22
        ck = lambda j, m: self.p("conv_k", l * 132 + j * 44 + m, 1)
        cb = lambda m: self.p("conv_b", l * 44 + m, 1)
        bufs = [self.u(q * 512, 512) for q in range(8)]
        b_free = [hold] * 8
        nb = 0
        last = l == DEPTH - 1
        keep = [[], []]

        def up(m):
            if True:
                res = {}
                half = int(m >= 10)

                def ev(o, i, ap, tok):
                    nonlocal nb
                    f = m + o % 2 + (FT if o >= 2 else 0)
                    s = nb % 8
                    nb += 1
                    b = bufs[s]
                    r = self.act(b, ap, ACT.Identity, tok, b_free[s], self.t_par, bias=cb(f), scale=ck(1, f))
                    r = self.stt(b[:, 1:512], ap[:, 0:511], ck(0, f), b[:, 1:512], ALU.mult, ALU.add, r)
                    r = self.stt(b[:, 0:511], ap[:, 1:512], ck(2, f), b[:, 0:511], ALU.mult, ALU.add, r)
                    self.give(i, r)
                    if o < 2:
                        r = self.act(b, b, ACT.Gelu, r)
                        res[o] = (r, b, s)
                    else:
                        ra, ba, sa = res[o - 2]
                        r = self.tt(V, ba, ba, b, ALU.mult, ra, r)
                        b_free[s] = [r]
                        k = (m + o - 2) if m < 12 else m - 12 + o - 2
                        w = self.split(self.ah[:, k, :], self.al[:, k, :], ba, r, self.a_free)
                        b_free[sa] = w
                        keep[half].extend(w)
                pieces = (("f_w_up", l, m * 128, m * 128 + 256), ("f_w_up", l, (m + FT) * 128, (m + FT) * 128 + 256))
                return self.gemm(8, pieces, xa, self.t_xT, "F", 4, ev, pair=m == 0)

        if last:
            slots = [self.u(12288, 1024), self.u(13312, 1024)]
            self.t_xn = [hold, hold]
            norm = self.rms_turn(slots, tg)
        else:
            norm = self.ln_turn(tg)
        self.ffn_order(up, "f_w_down", l, keep, norm, self.ln_pre, True)

    def ffn_order(self, up, name, l, keep, norm, pre, scale):
        T = self.T
        hid = lambda m: (lambda hf: ((name, (l, m), hf * 512, hf * 512 + 512),))
        for m in range(0, 12, 2):
            drive((up(m), 1))
        drive((self.residual(10, hid(0), (self.ah, self.al, 0), keep[0], scale=scale), 1))
        self.a_free = [T.last()]
        for m in range(12, 22, 2):
            drive((up(m), 1))
        self.free_ar = self.snap()
        drive((self.residual(12, hid(10), (self.ah, self.al, [10, 11] + list(range(10))), keep[1], norm, pre), 1))
        self.a_free = [T.last()]

    def mixer2(self):
        V, A, G, T = self.V, self.A, self.G, self.T
        ins = self.ins
        xa = (self.xh, self.xl, 0)
        hold = self.free_ar
        gain = ("n_mix", 0)
        iqT = self.u(0, 4096).rearrange("p (j s) -> p j s", j=8)
        ikT = self.u(4096, 512)
        iqs = [self.u(q, 2048).rearrange("p (t c) -> p t c", t=NT) for q in (4608, 12288)]
        sc = self.u(6656, 2048).rearrange("p (t s) -> p t s", t=NT)
        iw = self.u(8704, 64).rearrange("p (t c) -> p t c", t=NT)
        ik = self.u(8768, 256).rearrange("p (t c) -> p t c", t=NT)
        ikd = self.u(9024, 128)
        tmp = self.u(9152, 512)
        rl = [self.u(9664 + 512 * q, 512) for q in range(3)]
        t_ik, t_iw = [], []

        def ei(t, i, ap, tok):
            r = self.ts(V, iw[:, t, :], ap[:, 0:16], 1.0 / 32.0, None, ALU.mult, None, tok, hold)
            r2 = self.cp(V, ik[:, t, :], ap[:, 16:80], tok, hold)
            self.give(i, r2)
            t_iw.append(r)
            t_ik.append(r2)

        def rope_in_place(src, nh, half, cs, t, prev, toks):
            cos = self.c("cos" + cs)[:, t * half:t * half + half]
            sin = self.c("sin" + cs)[:, t * half:t * half + half]
            v = src.rearrange("p (h d) -> p h d", h=nh)
            x1, x2 = v[:, :, 0:half], v[:, :, half:2 * half]
            n = nh * half
            q = [tmp[:, a * n:(a + 1) * n].rearrange("p (h f) -> p h f", h=nh) for a in range(4)]
            c = cos.unsqueeze(1).broadcast_to([128, nh, half])
            s = sin.unsqueeze(1).broadcast_to([128, nh, half])
            a0 = self.tt(V, q[0], x1, c, ALU.mult, toks, prev, self.t_cst)
            a1 = self.tt(V, q[1], x2, s, ALU.mult, toks, prev, self.t_cst)
            a2 = self.tt(V, q[2], x2, c, ALU.mult, toks, prev, self.t_cst)
            a3 = self.tt(V, q[3], x1, s, ALU.mult, toks, prev, self.t_cst)
            r1 = self.tt(V, x1, q[0], q[1], ALU.subtract, a0, a1, a3)
            r2 = self.tt(V, x2, q[2], q[3], ALU.add, a2, a3, r1)
            return [r1, r2]

        t_ikT, t_iqT = [], []
        t_iq = [{}, {}]

        def index_proj(cg):
            def eq(t, i, ap, tok):
                r = self.cp(A, iqs[cg][:, t, :], ap, tok, hold, self.t_xn if cg else None)
                self.give(i, r)
                t_iq[cg][t] = r
            return self.gemm(8, self.cols("w_in_ab_2", 0, 2048 + cg * 512, 2560 + cg * 512), xa, self.t_xT, "T", 4,
                             eq, gain=gain, pair=cg == 0)

        def index_rope():
            prev = hold
            for t in range(NT):
                r = rope_in_place(iqs[0][:, t, :], 8, 8, "i", t, prev, t_iq[0][t])
                prev = r
                self.turn(iqs[0][:, t, :], 4, r, iq_dst(0, t))
                yield
            while len(t_ik) < NT:
                yield
            prev = [prev, T.last()]
            for t in range(NT):
                r = rope_in_place(ik[:, t, :], 1, 8, "i", t, prev, t_ik)
                d = self.cp(V, ikd.rearrange("p (w d) -> p w d", w=2),
                            ik[:, t, :].unsqueeze(1).broadcast_to([128, 2, 64]), r, prev)

                def dst(j, m, i, v, tok, t=t):
                    c = self.cp(A, ikT[:, t * 128:t * 128 + 128], v[:, 0, :], tok, hold)
                    self.give(i, c)
                    t_ikT.append(c)
                self.turn(ikd, 1, [d], dst)
                prev = [d, T.last()]
                yield
            while len(t_iq[1]) < NT:
                yield
            for t in range(NT):
                r = rope_in_place(iqs[1][:, t, :], 8, 8, "i", t, prev, t_iq[1][t])
                prev = r
                self.turn(iqs[1][:, t, :], 4, r, iq_dst(1, t))
                yield

        def iq_dst(cg, t):
            def dst(j, m, i, v, tok):
                c = self.cp(A if t % 2 else V, iqT[:, cg * 4 + j:cg * 4 + j + m, t * 128:t * 128 + 128], v, tok, hold)
                self.give(i, c)
                t_iqT.append(c)
            return dst
        drive((index_proj(0), 1))
        ikg = self.gemm(8, self.cols("w_in_ab_2", 0, 3072, 3152), xa, self.t_xT, "T", 4, ei, gain=gain, per=8)
        drive((self.chain(lambda: ikg, lambda: index_proj(1)), 1), (index_rope(), 1))
        hold = self.snap()
        t_sc = {}
        top = self.st[:, 232:240]

        def index_scores():
            n = 0
            rf = [hold] * 3
            for t in range(NT):
                w = (t + 1) * 128
                prev = None
                for h in range(16):
                    a = slice((h % 2) * 64, (h % 2) * 64 + 64)
                    i, bk, bt = self.bank()
                    tok = self.mm(bk[:, 0:w], iqT[a, h // 2, t * 128:t * 128 + 128], ikT[a, 0:w], True, True,
                                  t_iqT, t_ikT, bt, sig=True)
                    r = rl[n % 3][:, 0:w]
                    c = self.act(r, bk[:, 0:w], ACT.Relu, tok, rf[n % 3])
                    self.give(i, c)
                    s = sc[:, t, 0:w]
                    wv = iw[:, t, h:h + 1]
                    if h == 0:
                        prev = self.ts(V, s, r, wv, None, ALU.mult, None, c, t_iw, hold)
                    else:
                        prev = self.stt(s, r, wv, s, ALU.mult, ALU.add, c, prev)
                    rf[n % 3] = [prev]
                    n += 1
                    if h % 2:
                        yield
                d = sc[:, t, t * 128:w]
                prev = self.tt(V, d, d, self.c("causal"), ALU.add, prev, self.t_cst)
                t_sc[t] = prev
                yield

        def choose():
            prev = None
            for t in range(1, NT):
                w = (t + 1) * 128
                s = sc[:, t, 0:w]
                prev = [prev, t_sc[t]]
                for _ in range(16):
                    a = V(lambda e, s=s: e.max(top, s), prev)
                    prev = V(lambda e, s=s: e.match_replace(s, top, s, GONE), a)
                    yield
                t_sc[t] = self.ts(V, s, s, -2.0e38, BIG, ALU.is_gt, ALU.mult, prev)
                yield
        self.mark(' idx')
        drive((index_scores(), 1))
        freeI = self.snap()
        qT = self.u(0, 2048).rearrange("p (h s) -> p h s", h=4)
        kT = self.u(2048, 2048).rearrange("p (h s) -> p h s", h=4)
        vt = self.u(4096, 2048).rearrange("p (t c) -> p t c", t=NT)
        raws = [self.u(q, 2048).rearrange("p (t c) -> p t c", t=NT) for q in (8704, 12032)]
        sq = self.u(10752, 512)
        tmp = self.u(11264, 512)
        gq = [self.u(11776, 128), self.u(11904, 128)]
        pbf, ptb, obf = self.u(8704, 1536), self.u(10240, 1024), self.u(12032, 1024)
        tgain = [self.load(gq[0], ins["a_q_norm_2"].broadcast_to([128, 128]), freeI),
                 self.load(gq[1], ins["a_k_norm_2"].broadcast_to([128, 128]), freeI)]
        t_qk = []
        t_vt = []

        t_r = [{}, {}]
        pro = {}

        def project():
            for which in range(2):
                def er(t, i, ap, tok, which=which):
                    r = self.cp(A, raws[which][:, t, :], ap, tok, freeI)
                    self.give(i, r)
                    t_r[which][t] = r
                yield from self.gemm(8, self.cols("w_in_ab_2", 0, which * 512, which * 512 + 512), xa, self.t_xT,
                                     "T", 4, er, gain=gain)

            def ev(t, i, ap, tok):
                r = self.cp(A, vt[:, t, :], ap, tok, freeI)
                self.give(i, r)
                t_vt.append(r)
            yield from self.gemm(8, self.cols("w_in_ab_2", 0, 1024, 1536), xa, self.t_xT, "T", 4, ev, gain=gain)
            yield from pool_branch()

        def prologue():
            pv = None
            for which in range(2):
                while len(t_r[which]) < NT:
                    yield
                for t in range(NT):
                    raw = raws[which]
                    w = self.head_norm(raw[:, t, :], 4, 128, [(0, 4, gq[which])], sq, t * 4, t_r[which][t], tgain,
                                       freeI, pv)
                    w = rope_in_place(raw[:, t, :], 4, 16, "q", t, freeI, w)
                    pv = w
                    dd = qT if which == 0 else kT

                    def dst(j, m, i, v, tok, t=t):
                        c = self.cp(A, dd[:, j:j + m, t * 128:t * 128 + 128], v, tok, freeI)
                        self.give(i, c)
                        t_qk.append(c)
                    self.turn(raw[:, t, :], 4, w, dst)
                    yield
                pro[which] = self.snap()

        def pool_branch():
            uT = [self.u(12032, 528), self.u(12560, 528)]
            pw = self.u(13088, 128)
            ub = self.u(13216, 512)
            t_u = []
            uall = raws[0]
            while 1 not in pro:
                yield

            def eu(o, i, ap, tok):
                r = self.cp(A, uall[:, o, :], ap, tok, pro[0])
                self.give(i, r)
                t_u.append(r)
            yield from self.gemm(8, self.cols("w_in_ab_2", 0, 1536, 2048), xa, self.t_xT, "F", 4, eu, gain=gain)
            keep = []
            prev = pro[1]
            z0 = V(lambda e: e.memset(uT[0][:, 0:16], 0.0), prev)
            z1 = V(lambda e: e.memset(uT[1][:, 0:16], 0.0), prev)
            zz = [z0, z1]
            tp = prev
            for g, win in enumerate(POOL_W):
                tw = self.load(pw, ins["pool_w_2"][g, :, :], tp)
                u = uall[:, g, :]
                cur = self.cp(V, uT[0][:, 16:528], u, t_u, zz, prev)
                src, k, sh = 0, 0, 1
                while sh < win:
                    s_, d_ = uT[k % 2], uT[(k + 1) % 2]
                    cur = self.tt(V, d_[:, 16:528], s_[:, 16:528], s_[:, 16 - sh:528 - sh], ALU.add, cur)
                    sh *= 2
                    k += 1
                s_ = uT[k % 2]
                po = ub
                r = self.tt(V, s_[:, 16:32], s_[:, 16:32], self.c("invc")[:, g * 16:g * 16 + 16], ALU.mult, cur,
                            self.t_cst)
                r1 = self.tt(V, po[:, 0:16], s_[:, 16:32], u[:, 0:16], ALU.subtract, r, prev)
                r2 = self.stt(po[:, 16:512], s_[:, 32:528], 1.0 / win, u[:, 16:512], ALU.mult, ALU.subtract, cur,
                              prev)
                i, bk, bt = self.bank()
                tok = self.mm(bk[:, :], pw, po, True, True, r1, r2, tw, bt, sig=True)
                prev = [tok, r1, r2]
                tp = [tok]
                rr = self.ts(V, uT[(k + 1) % 2][:, 16:528], bk[:, :], self.p("pool_scale", g, 1), None, ALU.mult,
                             None, tok, self.t_par)
                self.give(i, rr)
                sp = self.split(self.ah[:, 4 + g, :], self.al[:, 4 + g, :], uT[(k + 1) % 2][:, 16:528], rr,
                                self.a_free)
                prev = prev + sp
                keep += sp
                yield
            self.t_pool = keep
        self.mark(' qkvpool')
        drive((project(), 1), (prologue(), 1), (choose(), 2))
        if self.stage == "dsa":
            self.dump("sc", self.u(6656, 2048), self.snap())
            self.dump("qT", self.u(0, 4096), self.snap())
        self.mark(' dsaatt')
        freeP = self.snap()
        keep = {t: [] for t in range(NT)}

        def put(t, c, o, toks):
            self.turn_split(o, 4, toks, self.ah, self.al, 0, t, keep[t], self.a_free)

        def mask(t, k0, k1):
            return self.c("causal") if t == 0 else sc[:, t, 0:(t + 1) * 128]
        drive((self.attend(
            range(4), 128, lambda h, t, k0, k1: [(qT[:, h, t * 128:t * 128 + 128], kT[:, h, 0:k1 * 128])],
            lambda t: (0, t + 1), lambda h, k: vt[:, k, h * 128:h * 128 + 128], 128 ** -0.5,
            [t_qk, t_vt, list(t_sc.values())], freeP, pbf, ptb, obf, put, mask), 1))
        self.free_ar = self.snap()
        self.resid2(8, lambda hf: self.cols("w_out_ab_2", 0, hf * 512, hf * 512 + 512), (self.ah, self.al, 0),
                    {t: [keep[t], self.t_pool] for t in range(NT)})

    def resid2(self, nk, pieces, act, toks):
        drive((self.residual(nk, pieces, act, toks, self.rms_turn(self.xn_slots())), 1))
        self.a_free = [self.T.last()]

    def convmod(self):
        V, A, G, T = self.V, self.A, self.G, self.T
        xa = (self.xh, self.xl, 0)
        hold = self.free_ar
        hT = self.u(0, 8 * 542).rearrange("p (k s) -> p k s", k=8)
        y = self.u(4336, 4096).rearrange("p (k s) -> p k s", k=8)
        th = [self.u(8432 + 512 * q, 512) for q in range(4)]
        gain = ("n_mix", 8)
        hb = self.st[:, 64:72]
        thb = self.ts(V, hb, self.p("cv_bin", 8, 8), 0.5, None, ALU.mult, None, self.t_par, hold)
        z = V(lambda e: e.memset(hT[:, :, 0:30], 0.0), hold)
        th_free = [hold] * 4
        t_h = {}
        res = {}
        n = [0]
        t_y = {}
        PEC = (6, 7)

        def conv(m):
            r = self.ts(V, y[:, m, :], hT[:, m, 30:542], self.p("dw_w", m * 31 + 30, 1), self.p("dw_b", m, 1),
                        ALU.mult, ALU.add, t_h[m], z, hold)
            for j in range(30):
                r = self.stt(y[:, m, :], hT[:, m, j:j + 512], self.p("dw_w", m * 31 + j, 1), y[:, m, :], ALU.mult,
                             ALU.add, r)
                if j % 4 == 3:
                    yield
            t_y[m] = r

        def conv_pe(m, q):
            flat = lambda t: t[:, 0:8, :].rearrange("p k s -> p (k s)")[:, q * 542:q * 542 + 542]
            oh, ol = flat(self.ah), flat(self.al)
            s = self.split(oh, ol, hT[:, m, :], t_h[m], z, self.a_free)
            i, bk, bt = self.bank()
            for j in range(31):
                d = j % 8
                a = slice((d % 4) * 128, (d % 4) * 128 + 128)
                dh, dl = self.ah[:, 8 + d // 4, a], self.al[:, 8 + d // 4, a]
                g = self.split(dh, dl, self.c("ident"), self.t_cst, self.t_par, d_free[d],
                               scale=self.p("dw_w", m * 31 + j, 1))
                for e, (lw, rw) in enumerate(((dh, oh), (dh, ol), (dl, oh))):
                    tok = self.mm(bk[:, :], lw, rw[:, j:j + 512], j == 0 and e == 0, j == 30 and e == 2, s, g, bt,
                                  sig=(e == 2))
                d_free[d] = [tok]
                if j % 4 == 3:
                    yield
            t_y[m] = self.act(y[:, m, :], bk[:, :], ACT.Identity, tok, hold, self.t_par, bias=self.p("dw_b", m, 1))
            self.give(i, t_y[m])
        d_free = [self.a_free] * 8

        def proj():
            for m in (0, 6, 2, 4):
                def ev(o, i, ap, tok, m=m):
                    if o < 2:
                        s = n[0] % 4
                        n[0] += 1
                        r = self.act(th[s], ap, ACT.Tanh, tok, thb, th_free[s], bias=hb[:, m + o:m + o + 1],
                                     scale=0.5)
                        self.give(i, r)
                        r = self.ts(V, th[s], th[s], 0.5, 0.5, ALU.mult, ALU.add, r)
                        res[o] = (r, s)
                    else:
                        r0, s = res[o - 2]
                        f = m + o - 2
                        r = self.stt(hT[:, f, 30:542], ap, self.p("cv_bin", f, 1), th[s], ALU.add, ALU.mult, tok, r0,
                                     hold)
                        self.give(i, r)
                        th_free[s] = [r]
                        t_h[f] = r
                pieces = (("conv_w_in_2", 0, 1024 + m * 128, 1024 + m * 128 + 256),
                          ("conv_w_in_2", 0, m * 128, m * 128 + 256))
                yield from self.gemm(8, pieces, xa, self.t_xT, "F", 4, ev, gain=gain, pair=m == 0)
            for q, m in enumerate(PEC):
                yield from conv_pe(m, q)

        def convs():
            for m in range(8):
                if m in PEC:
                    continue
                while m not in t_h:
                    yield
                yield from conv(m)
        drive((proj(), 1), (convs(), 2))
        self.mark(' cln')
        ones = self.c("ones")
        ib, mb, bt = self.bank()
        order = [0, 1, 2, 3, 6, 7, 4, 5]
        for q, m in enumerate(order):
            tok = self.mm(mb[:, :], ones, y[:, m, :], q == 0, q == 7, t_y[m], bt, self.t_cst, sig=(q == 7))
        mu = self.u(8432, 512)
        hold2 = self.snap()
        a = self.ts(V, mu, mb[:, :], 1.0 / D, None, ALU.mult, None, tok, hold2)
        self.give(ib, a)
        iv, vb, bt = self.bank()
        sq = [self.u(9456, 512), self.u(9968, 512), self.u(10480, 512)]
        sf = [hold2] * 3
        t_d = {}
        tot = self.st[:, 72:80]
        for m in range(8):
            d = self.tt(V, y[:, m, :], y[:, m, :], mu, ALU.subtract, a, t_y[m], tok)
            t_d[m] = d
            q = self.act(sq[m % 3], y[:, m, :], ACT.Square, d, sf[m % 3])
            tok2 = self.mm(vb[:, :], ones, sq[m % 3], m == 0, m == 7, q, bt, sig=True)
            sf[m % 3] = [tok2]
        var = self.u(10992, 512)
        r = self.ts(V, var, vb[:, :], 1.0 / D, RMS_EPS, ALU.mult, ALU.add, tok2, hold2)
        self.give(iv, r)
        i2, b2, bt = self.bank()
        for t in range(NT):
            tok = self.tr(b2[:, t * 128:t * 128 + 128], var[:, t * 128:t * 128 + 128], r, bt, sig=(t == 3))
        col = self.cp(V, tot[:, 0:4], b2[:, :].rearrange("p (t c) -> p t c", t=4)[:, :, 0], tok, hold2)
        self.give(i2, col)
        q = self.tt(G, tot[:, 0:4], tot[:, 0:4], self.c("pw")[:, 0:4], ALU.pow, col, self.t_cst)
        q = self.cp(V, var.rearrange("p (t c) -> p t c", t=4),
                    tot[:, 0:4].unsqueeze(2).broadcast_to([128, 4, 128]), q, tok)
        i2, rb, bt = self.bank()
        for t in range(NT):
            tok = self.tr(rb[:, t * 128:t * 128 + 128], var[:, t * 128:t * 128 + 128], q, bt, sig=(t == 3))
        rs = self.u(8944, 512)
        q = self.cp(V, rs, rb[:, :], tok, hold2)
        self.give(i2, q)
        keep = []
        for m in range(8):
            ym = y[:, m, :]
            d = self.tt(V, ym, ym, rs, ALU.mult, q, t_d[m], tok2)
            e = self.act(ym, ym, ACT.Silu, d, self.t_par, bias=self.p("cln_b", m, 1), scale=self.p("cln_g", m, 1))
            keep += self.split(self.ah[:, m, :], self.al[:, m, :], ym, e, self.a_free)
        self.free_ar = self.snap()
        self.mark(' cout')
        self.resid2(8, lambda hf: self.cols("conv_w_out_2", 0, hf * 512, hf * 512 + 512), (self.ah, self.al, 0), keep)

    def cross2(self, l):
        V, A, G, T = self.V, self.A, self.G, self.T
        ins = self.ins
        hold = self.free_ar
        qT = self.u(0, 4096).rearrange("p (j s) -> p j s", j=8)
        kT = self.u(4096, 2048).rearrange("p (j s) -> p j s", j=8)
        vm = self.u(6144, 2048).rearrange("p (t c) -> p t c", t=2)
        raws = [self.u(q, 2048).rearrange("p (t c) -> p t c", t=4) for q in (8192, 10240)]
        sq = self.u(12288, 512)
        gq = [self.u(12800, 256), self.u(13056, 256)]
        mrow = self.u(13312, 1024)
        pb, ptb, ob = self.u(8192, 768), self.u(8960, 512), self.u(13312, 1024)
        tgain = [self.load(gq[0], ins["cross_q_norm_2"][l:l + 1, :].broadcast_to([128, 256]), hold),
                 self.load(gq[1], ins["cross_k_norm_2"][l:l + 1, :].broadcast_to([128, 256]), hold)]
        tm = self.mem_operand("mem_2T", 8192, hold)
        rs = self.st[:, 64:66]
        fr = hold
        w = []
        for t in range(2):
            k = self.load(mrow, ins["mem_2"][t * 128:t * 128 + 128, :], fr)
            s = self.act(mrow, mrow, ACT.Square, k, hold, acc=rs[:, t:t + 1])
            fr = [s]
            w.append(s)
        t_rs = self.rstd(rs, rs, 1.0 / D, RMS_EPS, w)
        ma = (self.ah, self.al, 0)
        xa = (self.xh, self.xl, 0)
        t_k, t_v, t_q = [], [], [[], []]
        t_r = [{} for _ in range(4)]
        done = [tm, None, None, None]

        def proj(j, name, cg, act, toks, n, gain):
            def er(t, i, ap, tok):
                w = [tok, hold, done[j - 2] if j >= 2 else tm]
                if j < 2:
                    r = self.ts(V, raws[j % 2][:, t, :], ap, rs[:, t:t + 1], None, ALU.mult, None, w, t_rs)
                else:
                    r = self.cp(A, raws[j % 2][:, t, :], ap, w)
                self.give(i, r)
                t_r[j][t] = r
            return self.gemm(8, self.cols(name, l, cg * 512, cg * 512 + 512), act, toks, "T", n, er, gain=gain)

        def prologue(j, n, dd, cg, out):
            pv = None
            raw = raws[j % 2]
            for t in range(n):
                while t not in t_r[j]:
                    yield
                wv = self.head_norm(raw[:, t, :], 2, 256, [(0, 2, gq[1 if j < 2 else 0])], sq, 2 + 2 * (4 * j + t),
                                    t_r[j][t], tgain, hold, pv, self.sq_free)
                pv = wv

                def dst(q, m, i, v, tok, t=t):
                    c = self.cp(A, dd[:, cg * 4 + q:cg * 4 + q + m, t * 128:t * 128 + 128], v, tok, hold)
                    self.give(i, c)
                    out.append(c)
                self.turn(raw[:, t, :], 4, wv, dst)
                yield
            self.sq_free = [pv]
            done[j] = [T.last()]

        def values(cg):
            def ev(t, i, ap, tok):
                r = self.ts(V, vm[:, t, cg * 512:cg * 512 + 512], ap, rs[:, t:t + 1], None, ALU.mult, None, tok,
                            t_rs, hold)
                self.give(i, r)
                t_v.append(r)
            return self.gemm(8, self.cols("cross_wv_2", l, cg * 512, cg * 512 + 512), ma, tm, "T", 2, ev,
                             gain=("n_mem", l * 8))
        self.sq_free = None
        gm, gx = ("n_mem", l * 8), ("n_cross", l * 8)
        drive((proj(0, "cross_wk_2", 0, ma, tm, 2, gm), 1))
        self.flush()
        drive((proj(1, "cross_wk_2", 1, ma, tm, 2, gm), 1), (prologue(0, 2, kT, 0, t_k), 1))
        drive((self.chain(lambda: values(0), lambda: values(1)), 2), (prologue(1, 2, kT, 1, t_k), 1))
        self.a_free = [T.last()]
        self.mark(' q2')
        drive((proj(2, "cross_wq_2", 0, xa, self.t_xT, 4, gx), 1))
        drive((proj(3, "cross_wq_2", 1, xa, self.t_xT, 4, gx), 1), (prologue(2, 4, qT, 0, t_q[0]), 1))
        keep = {t: [] for t in range(NT)}
        free0 = self.snap()

        def put(t, c, o, toks):
            self.turn_split(o, 4, toks, self.ah, self.al, 4 * c, t, keep[t], self.a_free)

        def att(c, free):
            return self.attend(
                [2 * c, 2 * c + 1], 256,
                lambda h, t, k0, k1: [(qT[:, 2 * h + q, t * 128:t * 128 + 128], kT[:, 2 * h + q, :])
                                      for q in range(2)],
                lambda t: (0, 2), lambda h, k: vm[:, k, h * 256:h * 256 + 256], 256 ** -0.5, [t_k, t_v, t_q[c]],
                free, pb, ptb, ob, put, wide=256)
        self.mark(' att2')
        drive((att(0, free0), 2), (prologue(3, 4, qT, 1, t_q[1]), 1))
        drive((att(1, self.snap()), 1))
        self.free_ar = self.snap()
        self.mark(' wo2')
        self.resid2(8, lambda hf: self.cols("cross_wo_2", l, hf * 512, hf * 512 + 512), (self.ah, self.al, 0), keep)

    def ffn2(self, l):
        V, A, G, T = self.V, self.A, self.G, self.T
        hold = self.free_ar
        xa = (self.xh, self.xl, 0)
        bufs = [self.u(q * 512, 512) for q in range(6)]
        b_free = [hold] * 6
        nb = 0
        keep = [[], []]

        def up(m):
            res = {}

            def ev(o, i, ap, tok):
                nonlocal nb
                if o < 2:
                    s = nb % 6
                    nb += 1
                    r = self.act(bufs[s], ap, ACT.Silu, tok, b_free[s])
                    self.give(i, r)
                    res[o] = (r, s)
                else:
                    r0, s = res[o - 2]
                    r = self.tt(V, bufs[s], bufs[s], ap, ALU.mult, tok, r0)
                    self.give(i, r)
                    k = (m + o - 2) if m < 12 else m - 12 + o - 2
                    w = self.split(self.ah[:, k, :], self.al[:, k, :], bufs[s], r, self.a_free)
                    b_free[s] = w
                    keep[int(m >= 10)].extend(w)
            pieces = (("ffn_w_gate_2", l, m * 128, m * 128 + 256), ("ffn_w_up_2", l, m * 128, m * 128 + 256))
            return self.gemm(8, pieces, xa, self.t_xT, "F", 4, ev, gain=("n_ffn", l * 8), pair=m == 0)
        norm = self.rms_turn(self.xn_slots()) if l < DEPTH - 1 else None
        self.ffn_order(up, "ffn_w_down_2", l, keep, norm, None, False)

    def emit(self):
        nc = self.nc
        sems = [self.ctx.enter_context(nc.semaphore(f"s{i}")) for i in range(self.nsem)]
        block = self.ctx.enter_context(nc.Block())
        for name, lane in (("tensor", self.T), ("vector", self.V), ("scalar", self.A), ("gpsimd", self.G),
                           ("sync", self.Y)):
            reg = {"tensor": block.tensor, "vector": block.vector, "scalar": block.scalar,
                   "gpsimd": block.gpsimd, "sync": block.sync}[name]
            reg(lambda eng, lane=lane: lane.play(eng, sems))
        self.ctx.close()


def new_program(nc, ins, out, plan, stage=None, dumps=None):
    p = Program(nc, ins, out, plan, stage, dumps)
    p.a_free = None
    p.x_free = None
    p.build()
    return p


def tables():
    c = np.zeros((128, NCST), np.float32)

    def put(name, a):
        at, n = CST[name]
        c[:, at:at + n] = a
    put("ident", np.eye(128))
    put("ones", 1.0)
    i, j = np.arange(128)[:, None], np.arange(384)[None, :]
    put("band", np.where((j >= i) & (j <= i + 256), 0.0, BIG))
    put("causal", np.where(np.arange(128)[None, :] <= i, 0.0, BIG))

    def angles(pos, half, theta, d):
        inv = np.float32(theta) ** (-np.arange(half, dtype=np.float32) * np.float32(2.0 / d))
        return pos.astype(np.float32)[:, None] * inv[None, :].astype(np.float32)

    def table(cn, sn, ang):
        n = ang.shape[1]
        for name, f in ((cn, np.cos), (sn, np.sin)):
            put(name, f(ang).astype(np.float32).reshape(NT, 128, n).transpose(1, 0, 2).reshape(128, NT * n))
    pos = np.arange(S)
    table("cosA", "sinA", angles(pos, 32, 10000.0, 64))
    table("cosB", "sinB", np.concatenate([angles(pos // 64, 16, 10000.0, 32), angles(pos % 64, 16, 10000.0, 32)], 1))
    table("cosq", "sinq", angles(pos, 16, 500000.0, 32))
    table("cosi", "sini", angles(pos, 8, 500000.0, 16))
    pw = np.full((128, 16), -0.5)
    pw[:, 15] = 0.5
    put("pw", pw)
    t = np.arange(16)
    put("invc", np.concatenate([1.0 / np.minimum(t + 1, w) for w in POOL_W])[None, :])
    return c


_SHAPES = {"x": (S, D), "mem_2": (256, D), "xT": (128, 8 * S), "memT": (128, 2048), "mem_2T": (128, 2048),
           "c_bs": (2, 512), "wsT": (2, 128, 512), "pool_w_2": (4, 128, 128), "par": (128, NPAR),
           "cst": (128, NCST), "a_sink": (2, 8), "b_q_gain": (2, 64), "b_k_gain": (2, 64), "c_ln_g": (2, 512),
           "c_ln_b": (2, 512), "a_q_norm_2": (1, 128), "a_k_norm_2": (1, 128), "cross_q_norm_2": (2, 256),
           "cross_k_norm_2": (2, 256), "ln1_g": (2, D), "ln1_b": (2, D), "ln2_g": (2, D), "ln2_b": (2, D),
           "ln3_g": (2, D), "ln3_b": (2, D)}


def the_plan(nc, stage=None):
    ins = {k: nc.dram_tensor("p_" + k, v, F32, kind="ExternalInput").ap() for k, v in _SHAPES.items()}
    out = nc.dram_tensor("p_out", (S, D), F32, kind="ExternalOutput").ap()
    p = new_program(nc, ins, out, None, stage)
    p.ctx.close()
    return p.units


_INS = ["ln1_g", "ln1_b", "ln2_g", "ln2_b", "ln3_g", "ln3_b", "a_sink", "b_q_gain", "b_k_gain", "c_ln_g", "c_ln_b",
        "a_q_norm_2", "a_k_norm_2", "cross_q_norm_2", "cross_k_norm_2"]


def lay_out(inputs, plan):
    g = {k: np.asarray(v) for k, v in inputs.items()}
    a = {k: np.ascontiguousarray(g[k]) for k in _INS}
    a["x"] = np.ascontiguousarray(g["x"][0])
    a["mem_2"] = np.ascontiguousarray(g["mem_2"][0])

    def feature_major(m):
        n = m.shape[0]
        return np.ascontiguousarray(m.T.reshape(8, 128, n).transpose(1, 0, 2).reshape(128, 8 * n))
    a["xT"] = feature_major(g["x"][0])
    a["memT"] = feature_major(g["mem"][0])
    a["mem_2T"] = feature_major(g["mem_2"][0])
    a["c_bs"] = np.ascontiguousarray(g["c_bs"].reshape(2, 512))
    a["wsT"] = np.ascontiguousarray(g["c_ws"].transpose(0, 3, 1, 2).reshape(2, 128, 512))
    a["pool_w_2"] = np.ascontiguousarray(g["pool_w_2"][0])
    par = np.zeros((128, NPAR), np.float32)

    def put(name, m):
        at, n = PAR[name]
        par[:, at:at + n] = m

    def cols(m):
        m = m.reshape(-1, 128)
        return m.T
    put("b_gate", cols(g["b_gate"]))
    put("conv_k", cols(g["f_conv_k"]))
    put("conv_b", cols(g["f_conv_b"]))
    put("pool_scale", cols(g["pool_scale_2"]))
    put("cv_bin", cols(g["conv_b_in_2"]))
    put("dw_w", g["conv_dw_w_2"][0].reshape(31, 8, 128).transpose(2, 1, 0).reshape(128, 248))
    put("dw_b", cols(g["conv_dw_b_2"]))
    put("cln_g", cols(g["conv_ln_g_2"]))
    put("cln_b", cols(g["conv_ln_b_2"]))
    for n, k in (("n_mix", "norm_mix_2"), ("n_cross", "norm_cross_2"), ("n_mem", "norm_mem_2"), ("n_ffn", "norm_ffn_2")):
        put(n, cols(g[k]))
    a["par"] = par
    a["cst"] = tables()
    pk = np.zeros((len(plan), 128, 1024), np.float32)
    for j, (k0, nk, pieces, _) in enumerate(plan):
        at = 0
        width = sum(p[3] - p[2] for p in pieces)
        dst = pk[j, :, 0:nk * width].reshape(128, nk, width)
        for name, idx, c0, c1 in pieces:
            w, r0 = g[name], 0
            if isinstance(idx, tuple):
                if "down" in name:
                    w, r0 = w[idx[0]], idx[1] * 128
                else:
                    w = w[idx[0]][idx[1]]
            else:
                w = w[idx]
            r = r0 + k0 * 128
            dst[:, :, at:at + c1 - c0] = w[r:r + nk * 128, c0:c1].reshape(nk, 128, c1 - c0).transpose(1, 0, 2)
            at += c1 - c0
    a["wpk"] = pk
    return a


def kernel(**inputs):
    import concourse.bacc as _bacc
    from concourse import mybir as _mybir
    from concourse.bass_utils import run_bass_kernel_spmd as _run

    plan = the_plan(_bacc.Bacc("TRN2", target_bir_lowering=False, num_devices=1))
    arrays = lay_out(inputs, plan)
    nc = _bacc.Bacc("TRN2", target_bir_lowering=False, num_devices=1)
    ins = {k: nc.dram_tensor("in_" + k, v.shape, _mybir.dt.float32, kind="ExternalInput").ap()
           for k, v in arrays.items()}
    out = nc.dram_tensor("out_0", (S, D), _mybir.dt.float32, kind="ExternalOutput").ap()
    new_program(nc, ins, out, plan).emit()
    r = _run(nc, [{"in_" + k: v for k, v in arrays.items()}], core_ids=[0])
    return r.results[0]["out_0"].reshape(1, S, D)
```

```python
from contextlib import ExitStack

import numpy as np
import concourse.bass as bass
from concourse import mybir

F32 = mybir.dt.float32
F32R = mybir.dt.float32r
ALU = mybir.AluOpType
ACT = mybir.ActivationFunctionType
AX = mybir.AxisListType

S = 512
D = 1024
NT = 4
DEPTH = 2
ALPHA = (2 * DEPTH) ** 0.25
LN_EPS = 1e-5
RMS_EPS = 1e-6
BIG = -1.0e30
GONE = -3.0e38

CST = {}
PAR = {}


def _columns(table, entries):
    at = 0
    for name, n in entries:
        table[name] = (at, n)
        at += n
    return at


NCST = _columns(CST, [
    ("ident", 128), ("band", 384), ("causal", 128), ("cosA", 128), ("sinA", 128), ("cosB", 128), ("sinB", 128),
    ("cosq", 64), ("sinq", 64), ("cosi", 32), ("sini", 32), ("ones", 128), ("pw", 16), ("invc", 64),
])
NPAR = _columns(PAR, [
    ("b_gate", 48), ("conv_k", 264), ("conv_b", 88), ("pool_scale", 4), ("cv_bin", 16), ("dw_w", 248), ("dw_b", 8),
    ("cln_g", 8), ("cln_b", 8), ("n_mix", 16), ("n_cross", 16), ("n_mem", 16), ("n_ffn", 16),
])
POOL_W = (2, 4, 8, 16)


class Lane:

    def __init__(self, sem):
        self.sem, self.n, self.seen, self.queue = sem, 0, {}, []

    def __call__(self, make, *waits, sig=True, sem=None, by=1):
        need = {}
        stack = list(waits)
        while stack:
            w = stack.pop()
            if isinstance(w, list):
                stack += w
            elif w is not None:
                need[w[0]] = max(need.get(w[0], 0), w[1])
        for s, v in need.items():
            if self.seen.get(s, 0) < v:
                self.seen[s] = v
                self.queue.append((None, s, v))
        if sem is not None:
            sem[1] += by
            self.queue.append((make, sem[0], by))
            return (sem[0], sem[1])
        if sig:
            self.n += 1
        self.queue.append((make, self.sem if sig else None, 1))
        return (self.sem, self.n) if sig else None

    def last(self):
        return (self.sem, self.n)

    def play(self, eng, sems):
        for make, s, v in self.queue:
            if make is None:
                eng.wait_ge(sems[s], v)
            else:
                i = make(eng)
                if s is not None:
                    i.then_inc(sems[s], v)


def drive(*gens):
    live = [[g, r] for g, r in gens]
    while live:
        for item in list(live):
            for _ in range(item[1]):
                try:
                    next(item[0])
                except StopIteration:
                    live.remove(item)
                    break


def together(*gens):
    live = list(gens)
    while live:
        for g in list(live):
            try:
                next(g)
            except StopIteration:
                live.remove(g)
        yield


def beside(main, *others):
    for _ in main:
        for g, r in others:
            for _ in range(r):
                next(g, None)


def unit_shape(desc):
    nk, pieces = desc[1], desc[2]
    return nk, sum(p[3] - p[2] for p in pieces)


class Program:
    def __init__(self, nc, ins, out, plan):
        self.nc, self.ins, self.out, self.plan = nc, ins, out, plan
        self.park = nc.dram_tensor("park", (S, D), F32, kind="Internal").ap()
        self.units = []
        self.nsem = 0
        self.T, self.V, self.A, self.G, self.Y = (Lane(self.newsem()) for _ in range(5))
        self.ctx = ExitStack()
        sb = lambda n, s, d=F32: self.ctx.enter_context(nc.sbuf_tensor(n, s, d))
        self.x = sb("x", [128, NT, D])
        self.xh, self.xl = sb("xh", [128, 8, S], F32R), sb("xl", [128, 8, S], F32R)
        self.ah, self.al = sb("ah", [128, 12, S], F32R), sb("al", [128, 12, S], F32R)
        self.NR = 3
        self.wr = sb("wr", [128, self.NR, 1024])
        self.wh, self.wl = sb("wh", [128, self.NR, 1024], F32R), sb("wl", [128, self.NR, 1024], F32R)
        self.gb = sb("gb", [128, 2, D])
        self.cst, self.par = sb("cst", [128, NCST]), sb("par", [128, NPAR])
        self.st = sb("st", [128, 320])
        self.NU = 14700
        self.ar = sb("ar", [128, self.NU])
        self.bk = [self.ctx.enter_context(nc.psum_tensor(f"bk{i}", [128, 512], F32)) for i in range(8)]
        self.free = [(i, None) for i in range(8)]
        self.wr_sem = [[self.newsem(), 0] for _ in range(self.NR)]
        self.wr_free = [None] * self.NR
        self.w_free = [None] * self.NR
        self.w_ready = {}
        self.w_dma = self.w_split = 0
        self.nuse = self.w_rel = 0
        self.look = 2
        self.pending = []
        self.io = [self.newsem(), 0]
        self.stores = []

    def newsem(self):
        self.nsem += 1
        return self.nsem - 1

    def c(self, name):
        a, n = CST[name]
        return self.cst[:, a:a + n]

    def p(self, name, i=0, n=None):
        a, m = PAR[name]
        return self.par[:, a + i:a + (m if n is None else i + n)]

    def u(self, a, n):
        assert a + n <= self.NU, (a, n)
        return self.ar[:, a:a + n]

    def snap(self):
        return [x.last() for x in (self.T, self.V, self.A, self.G)]

    def bank(self):
        i, toks = self.free.pop(0)
        return i, self.bk[i], toks

    def give(self, i, *toks):
        self.free.append((i, list(toks)))

    def load(self, dst, src, *waits, eng=None):
        s = [self.newsem(), 0]
        return (eng or self.Y)(lambda e: e.dma_start(dst, src), *waits, sem=s, by=16)

    def tt(self, lane, out, a, b, op, *w):
        return lane(lambda e: e.tensor_tensor(out, a, b, op), *w)

    def ts(self, lane, out, a, s1, s2, o1, o2, *w):
        if s2 is None:
            return lane(lambda e: e.tensor_scalar(out, a, s1, None, o1), *w)
        return lane(lambda e: e.tensor_scalar(out, a, s1, s2, o1, o2), *w)

    def stt(self, out, a, s, b, o1, o2, *w):
        return self.V(lambda e: e.scalar_tensor_tensor(out, a, s, b, o1, o2), *w)

    def cp(self, lane, out, a, *w):
        if lane is self.A:
            return lane(lambda e: e.activation(out, a, ACT.Copy), *w)
        return lane(lambda e: e.tensor_copy(out, a), *w)

    def act(self, out, a, f, *w, bias=0.0, scale=1.0, acc=None):
        if acc is not None:
            return self.A(lambda e: e.activation(out, a, f, bias=bias, scale=scale, accum_out=acc), *w)
        return self.A(lambda e: e.activation(out, a, f, bias=bias, scale=scale), *w)

    def acopy(self, out, a, scale, *w):
        return self.A(lambda e: e.activation(out, a, ACT.Copy, scale=scale), *w)

    def mm(self, out, l, r, start, stop, *w, sig=False):
        return self.T(lambda e: e.matmul(out, l, r, start=start, stop=stop), *w, sig=sig)

    def tr(self, out, a, *w, sig=False):
        ident = self.c("ident")
        return self.T(lambda e: e.transpose(out, a, ident), *w, sig=sig)

    def split(self, h, l, src, *w, scale=None):
        hf = h.bitcast(F32)
        if scale is None:
            a = self.cp(self.A, h, src, *w)
            return [a, self.tt(self.V, l, src, hf, ALU.subtract, a, *w)]
        a = self.acopy(h, src, scale, *w)
        return [a, self.stt(l, src, scale, hf, ALU.mult, ALU.subtract, a, *w)]

    def w_prefetch(self, i):
        plan = self.plan if self.plan is not None else self.units
        n = len(plan)
        while self.w_split < min(i + 1 + self.look, self.w_rel + self.NR, n):
            self._w_load(min(self.w_split + 1, n))
            j, r = self.w_split, self.w_split % self.NR
            nk, cols = unit_shape(plan[j])
            gain = plan[j][3]
            got = (self.wr_sem[r][0], 16 * (j // self.NR + 1))
            if gain is None:
                m = nk * cols
                toks = self.split(self.wh[:, r, 0:m], self.wl[:, r, 0:m], self.wr[:, r, 0:m], got, self.w_free[r])
            else:
                toks = []
                for k in range(nk):
                    g = self.p(gain[0], gain[1] + k, 1)
                    a = k * cols
                    toks += self.split(self.wh[:, r, a:a + cols], self.wl[:, r, a:a + cols],
                                       self.wr[:, r, a:a + cols], got, self.w_free[r], self.t_par, scale=g)
            self.w_ready[j] = toks
            self.wr_free[r] = toks
            self.w_split += 1
        self._w_load(min(self.w_split + self.NR, n))

    def _w_load(self, upto):
        upto = min(upto, len(self.plan or self.units))
        while self.w_dma < upto:
            j, r = self.w_dma, self.w_dma % self.NR
            if j >= self.w_split + self.NR:
                break
            nk, cols = unit_shape((self.plan or self.units)[j])
            m = nk * cols
            dst = self.wr[:, r, 0:m]
            src = None if self.plan is None else self.ins["wpk"][j, :, 0:m]
            self.Y(lambda e, dst=dst, src=src: e.dma_start(dst, src), self.wr_free[r], sem=self.wr_sem[r], by=16)
            self.w_dma += 1

    def w_use(self, desc):
        i = self.nuse
        self.nuse += 1
        if self.plan is None:
            self.units.append(desc)
        else:
            assert self.plan[i] == desc
        self.w_prefetch(i)
        r = i % self.NR
        nk, cols = unit_shape(desc)
        view = lambda t: t[:, r, 0:nk * cols].rearrange("p (k c) -> p k c", k=nk)
        return view(self.wh), view(self.wl), self.w_ready[i], i

    def w_done(self, i, tok):
        assert i == self.w_rel
        self.w_rel += 1
        self.w_free[i % self.NR] = tok

    def gemm(self, nk, pieces, act, toks, orient, nout, evac, gain=None, per=None, width=None, pair=False,
             hooks=None):
        ah, al, base = act
        cols = sum(p[3] - p[2] for p in pieces)
        per = per or max(1, 1024 // cols)
        width = width or S
        nu = -(-nk // per)
        banks = [self.bank() for _ in range(nout)]
        outs = list(range(nout))
        steps, q = [], min(self.NR, nu)
        if pair:
            for half in range(2):
                for u in range(q):
                    steps.append((u, outs, half) if orient == "F" else (u, outs[2 * half:2 * half + 2], None))
                if half == 0:
                    steps.append(None)
            steps += [(u, outs, None) for u in range(q, nu)]
        elif hooks is not None:
            steps += [(u, outs, None) for u in range(nu - q)]
            for half in range(2):
                for u in range(nu - q, nu):
                    steps.append((u, outs[2 * half:2 * half + 2], None))
        else:
            steps = [(u, outs, None) for u in range(nu)]
        last = {}
        for j, s in enumerate(steps):
            if s is not None:
                last[s[0]] = j
        first, units = set(), {}
        for j, s in enumerate(steps):
            if s is None:
                self.flush()
                continue
            u, os_, half = s
            k0 = u * per
            n = min(per, nk - k0)
            if u not in units:
                units[u] = self.w_use((k0, n, tuple(pieces), None if gain is None else (gain[0], gain[1] + k0)))
            h, l, wt, ui = units[u]
            c0, c1 = (0, width) if half is None else (half * 256, half * 256 + 256)
            for o in os_:
                i, bk, bt = banks[o]
                at = toks
                if isinstance(toks, dict):
                    tiles = [o] if orient == "T" else range(c0 // 128, c1 // 128)
                    at = [toks[t] for t in tiles]
                for kk in range(n):
                    k = k0 + kk
                    if isinstance(toks, tuple):
                        at = toks[0][k]
                    kb = base[k] if isinstance(base, list) else base + k
                    a = slice(o * 128, o * 128 + 128)
                    if orient == "F":
                        xh, xl = ah[:, kb, c0:c1], al[:, kb, c0:c1]
                        seq = [(h[:, kk, a], xh), (h[:, kk, a], xl), (l[:, kk, a], xh)]
                        ap, whole = bk[:, c0:c1], bk[:, 0:width]
                    else:
                        xh, xl = ah[:, kb, a], al[:, kb, a]
                        seq = [(xh, h[:, kk, :]), (xh, l[:, kk, :]), (xl, h[:, kk, :])]
                        ap = whole = bk[:, 0:cols]
                    for q, (lw, rw) in enumerate(seq):
                        st = o not in first
                        first.add(o)
                        end = k == nk - 1 and q == 2 and half != 0
                        sig = (kk == n - 1 and q == 2) and (end or o == os_[-1])
                        t = self.mm(ap, lw, rw, st, end, wt, at, bt if st else None, sig=sig)
                if k0 + n == nk and half != 0:
                    evac(o, i, whole, t)
            if last[u] == j:
                self.w_done(ui, t)
                self.w_prefetch(ui)
            if hooks is not None:
                f = hooks.get(j - len(steps))
                if f is not None:
                    f()
            yield

    def turn(self, src, n, toks, dst):
        for j in range(0, n, 4):
            m = min(4, n - j)
            i, bk, bt = self.bank()
            for q in range(m):
                t = self.tr(bk[:, q * 128:q * 128 + 128], src[:, (j + q) * 128:(j + q + 1) * 128],
                            toks, bt, self.t_cst, sig=(q == m - 1))
            dst(j, m, i, bk[:, 0:m * 128].rearrange("p (j c) -> p j c", j=m), t)

    def turn_split(self, src, n, toks, hi, lo, base, t, keep, *w):
        def dst(j, m, i, v, tok):
            a = slice(t * 128, t * 128 + 128)
            got = self.split(hi[:, base + j:base + j + m, a], lo[:, base + j:base + j + m, a], v, tok, *w)
            self.give(i, got[1])
            keep.extend(got)
        self.turn(src, n, toks, dst)

    def rstd(self, out, var, scale, eps, *w):
        g = self.ts(self.G, out, var, scale, eps, ALU.mult, ALU.add, *w)
        n = out.shape[-1]
        pw = self.c("pw")[:, 0:n]
        return self.tt(self.G, out, out, pw, ALU.pow, g, self.t_cst)

    def residual(self, nk, pieces, act, toks, norm=None, pre=None, scale=False):
        def turn(t, got):
            def f():
                self.turn_split(got[t][0], 8, got[t][1], self.xh, self.xl, 0, t, keep[t])
                if got[t][2] is not None:
                    self.t_xn[got[t][2]] = [self.T.last()]
                self.t_xr = [self.T.last()]
            return f
        keep = {t: [] for t in range(NT)}
        got, tok_r = {}, {}
        for hf in range(2):
            def evac(t, i, ap, tok, hf=hf):
                xs = self.x[:, t, hf * 512:hf * 512 + 512]
                w = [tok, self.t_x[t], self.t_xr]
                if scale:
                    r = self.stt(xs, xs, ALPHA, ap, ALU.mult, ALU.add, *w)
                else:
                    r = self.tt(self.V, xs, xs, ap, ALU.add, *w)
                self.give(i, r)
                tok_r.setdefault(t, []).append(r)
                if hf == 0:
                    if pre is not None:
                        pre(t, r)
                    return
                self.t_x[t] = list(tok_r[t])
                if norm is not None and t < 2:
                    got[t] = norm(t, self.t_x[t])
            hooks = None
            if norm is not None and hf == 1:
                hooks = {-2: lambda: turn(0, got)()}
            yield from self.gemm(nk, pieces(hf), act, toks, "T", 4, evac, hooks=hooks)
        if norm is not None:
            turn(1, got)()
            got[2] = norm(2, self.t_x[2])
            got[3] = norm(3, self.t_x[3])
            self.t_xT = keep
            self.pending += [turn(2, got), turn(3, got)]

    def flush(self):
        for f in self.pending:
            f()
        self.pending = []

    def ln_pre(self, t, r):
        st = self.st[:, t * 16:t * 16 + 12]
        x = self.x[:, t, :]
        self.t_pre[t] = self.V(lambda e: e.bn_stats(st[:, 0:6], x[:, 0:512]), r, self.t_ln[t])

    def ln_turn(self, tg):
        def norm(t, r):
            d = self.ln_chain(t, r, tg)
            return self.x[:, t, :], [d], None
        return norm

    def rms_turn(self, slots, tg=None):
        def norm(t, r):
            if tg is not None:
                r = [self.ln_chain(t, r, tg)]
            s, x = slots[t % 2], self.x[:, t, :]
            ss, rs = self.st[:, 240 + t:241 + t], self.st[:, 244 + t:245 + t]
            a = self.act(s, x, ACT.Square, r, self.t_xn[t % 2], self.t_rms[t], acc=ss)
            g = self.rstd(rs, ss, 1.0 / D, RMS_EPS, a)
            b = self.acopy(s, x, rs, g, a)
            self.t_rms[t] = [b, g]
            self.t_x[t] = [self.t_x[t], b]
            return s, [b], t % 2
        return norm

    def xn_slots(self):
        return [self.gb[:, 0, :], self.gb[:, 1, :]]

    def ln_chain(self, t, r, tg):
        x = self.x[:, t, :]
        st = self.st[:, t * 16:t * 16 + 12]
        mv = self.st[:, t * 16 + 12:t * 16 + 14]
        rs = self.st[:, t * 16 + 14:t * 16 + 15]
        a = self.t_pre[t]
        b = self.V(lambda e: e.bn_stats(st[:, 6:12], x[:, 512:1024]), r)
        m = self.V(lambda e: e.bn_aggr(mv, st), a, b, self.t_ln[t])
        g = self.rstd(rs, mv[:, 1:2], 1.0, LN_EPS, m)
        c = self.stt(x, x, mv[:, 0:1], self.gb[:, 0, :], ALU.subtract, ALU.mult, m, tg)
        d = self.stt(x, x, rs, self.gb[:, 1, :], ALU.mult, ALU.add, c, g, tg)
        self.t_x[t] = [d]
        self.t_ln[t] = [d, g]
        return d

    def rope(self, src, dst, nh, g, half, cos, sin, tmp, *w):
        sh = [128, nh, g, half]
        v = lambda a: a.rearrange("p h (g w f) -> p h g w f", g=g, w=2)
        bc = lambda a: a.rearrange("p (g f) -> p g f", g=g).unsqueeze(1).broadcast_to(sh)
        x1, x2 = v(src)[:, :, :, 0, :], v(src)[:, :, :, 1, :]
        d1, d2 = v(dst)[:, :, :, 0, :], v(dst)[:, :, :, 1, :]
        n = nh * g * half
        t = [tmp[:, q * n:(q + 1) * n].rearrange("p (h g f) -> p h g f", h=nh, g=g) for q in range(4)]
        c, s = bc(cos), bc(sin)
        a = self.tt(self.V, t[0], x1, c, ALU.mult, *w)
        b = self.tt(self.V, t[1], x2, s, ALU.mult, *w)
        p = self.tt(self.V, d1, t[0], t[1], ALU.subtract, a, b, *w)
        a = self.tt(self.G, t[2], x2, c, ALU.mult, *w)
        b = self.tt(self.G, t[3], x1, s, ALU.mult, *w)
        return [p, self.tt(self.G, d2, t[2], t[3], ALU.add, a, b, *w)]

    def head_norm(self, src, nh, hd, gains, sq, col, *w):
        ss = self.st[:, 64 + col:64 + col + nh]
        a = self.act(sq, src, ACT.Square, *w)
        v = src.rearrange("p (h d) -> p h d", h=nh)
        b = self.V(lambda e: e.tensor_reduce(ss, sq.rearrange("p (h d) -> p h d", h=nh), AX.X, ALU.add), a, *w)
        g = self.rstd(ss, ss, 1.0 / hd, RMS_EPS, b)
        c = self.tt(self.V, v, v, ss.unsqueeze(2).broadcast_to([128, nh, hd]), ALU.mult, g, b)
        out = []
        for h0, n, gain in gains:
            out.append(self.tt(self.G, v[:, h0:h0 + n, :], v[:, h0:h0 + n, :],
                               gain.unsqueeze(1).broadcast_to([128, n, hd]), ALU.mult, c, *w))
        return out

    def attend(self, heads, dv, qk, keys, val, scale, ready, hold, pbuf, ptbuf, obuf, put, mask=None, sink=None,
               wide=512):
        per = 512 // dv
        nh = len(heads)
        items = [(t, q) for t in range(NT) for q in range(nh)]
        n = len(items)
        NP = 3
        nm, sm = self.st[:, 128:160], self.st[:, 160:192]
        e8 = self.st[:, 192:200]
        p_free, pt_free, o_free = [hold] * NP, [hold] * 2, [hold] * 2
        P, PT, O = {}, {}, {}
        no = 0
        later = []
        for i in range(n + 4):
            if i < n:
                t, q0 = items[i]
                k0, k1 = keys(t)
                w = (k1 - k0) * 128
                b, bk, bt = self.bank()
                prs = qk(heads[q0], t, k0, k1)
                for q, (lw, rw) in enumerate(prs):
                    s = self.mm(bk[:, 0:w], lw, rw, q == 0, q == len(prs) - 1, ready, bt, sig=(q == len(prs) - 1))
                pb = pbuf[:, (i % NP) * wide:(i % NP) * wide + w]
                ci = i % 32
                m_, s_ = nm[:, ci:ci + 1], sm[:, ci:ci + 1]
                if mask is not None:
                    mk = mask(t, k0, k1)
                    init = sink[:, q0:q0 + 1] if sink is not None else -3.0e38
                    a = self.V(lambda e, pb=pb, bk=bk, w=w, mk=mk, m_=m_, init=init: e.tensor_tensor_reduce(
                        pb, bk[:, 0:w], mk, scale, init, ALU.add, ALU.max, m_), s, p_free[i % NP], ready)
                    self.give(b, a)
                    a = self.ts(self.V, m_, m_, -1.0, None, ALU.mult, None, a)
                    e_ = self.act(pb, pb, ACT.Exp, a, bias=m_, acc=s_)
                else:
                    a = self.V(lambda e, bk=bk, w=w, m_=m_: e.tensor_reduce(m_, bk[:, 0:w], AX.X, ALU.max), s, hold)
                    a = self.ts(self.V, m_, m_, -scale, None, ALU.mult, None, a)
                    e_ = self.act(pb, bk[:, 0:w], ACT.Exp, a, p_free[i % NP], bias=m_, scale=scale, acc=s_)
                    self.give(b, e_)
                P[i] = (e_, pb, k0, k1)
            if 2 <= i <= n + 1:
                j = i - 2
                e_, pb, k0, k1 = P.pop(j)
                w = (k1 - k0) * 128
                b, bk, bt = self.bank()
                for q in range(k1 - k0):
                    tk = self.tr(bk[:, q * 128:q * 128 + 128], pb[:, q * 128:q * 128 + 128], e_, bt, self.t_cst,
                                 sig=(q == k1 - k0 - 1))
                p_free[j % NP] = [tk]
                pt = ptbuf[:, (j % 2) * wide:(j % 2) * wide + w]
                c = self.cp(self.A if j % 2 else self.V, pt, bk[:, 0:w], tk, pt_free[j % 2])
                self.give(b, c)
                PT[j] = (c, pt, k0, k1, e_)
            for f in later:
                f()
            later = []
            if 3 <= i <= n + 2:
                j = i - 3
                t, q0 = items[j]
                c, pt, k0, k1, e_ = PT.pop(j)
                if q0 % per == 0:
                    O[t, q0 // per] = self.bank() + ([],)
                b, bk, bt, es = O[t, q0 // per]
                es.append(e_)
                col = (q0 % per) * dv
                for q in range(k1 - k0):
                    tk = self.mm(bk[:, col:col + dv], pt[:, q * 128:q * 128 + 128], val(heads[q0], k0 + q), q == 0,
                                 q == k1 - k0 - 1, c, bt, ready, sig=(q == k1 - k0 - 1))
                pt_free[j % 2] = [tk]
                if q0 % per == per - 1:
                    c0 = (j - per + 1) % 32
                    sv = sm[:, c0:c0 + per]
                    w2 = es
                    if sink is not None:
                        a = self.tt(self.V, e8, sink, nm[:, c0:c0 + per], ALU.add, es, ready)
                        a = self.act(e8, e8, ACT.Exp, a)
                        w2 = [self.tt(self.V, sv, sv, e8, ALU.add, a, es)]
                    a = self.V(lambda e, sv=sv: e.reciprocal(sv, sv), w2)
                    ob = obuf[:, (no % 2) * 512:(no % 2) * 512 + 512]
                    r = self.tt(self.V, ob.rearrange("p (h d) -> p h d", h=per),
                                bk[:, :].rearrange("p (h d) -> p h d", h=per),
                                sv.unsqueeze(2).broadcast_to([128, per, dv]), ALU.mult, a, tk, o_free[no % 2])
                    self.give(b, r)

                    def fin(t=t, c=heads[q0] // per, ob=ob, r=r, k=no % 2):
                        put(t, c, ob, [r])
                        o_free[k] = [self.T.last()]
                    later.append(fin)
                    no += 1
            yield

    def build(self):
        ins, V, A, G, T = self.ins, self.V, self.A, self.G, self.T
        self.t_xn = [None, None]
        self.t_ln, self.t_rms, self.t_pre = [None] * NT, [None] * NT, [None] * NT
        xt = {}
        keep = {}
        for q in range(4):
            raw = self.u(q * 1024, 1024)
            xt[q] = (raw, self.load(raw, ins["xT"][:, q * 1024:(q + 1) * 1024]))
            if q == 0:
                self._w_load(1)
        self.t_par = self.load(self.par[:, :], ins["par"])
        self.t_cst = self.load(self.cst[:, :], ins["cst"])
        for q in range(4):
            raw, tok = xt[q]
            keep[2 * q] = keep[2 * q + 1] = self.split(
                self.xh[:, q * 2:q * 2 + 2, :], self.xl[:, q * 2:q * 2 + 2, :],
                raw.rearrange("p (k s) -> p k s", k=2), tok)
            if q == 0:
                self.w_prefetch(0)
        self.t_xT = (keep,)
        self.t_x = [[] for _ in range(NT)]
        self.t_xr = None
        self.free_ar = self.snap()
        for l in range(DEPTH):
            self.mixer1(l)
            self.cross1(l)
            self.ffn1(l)
        for l in range(DEPTH):
            if l == 0:
                self.mixer2()
            else:
                self.convmod()
            self.cross2(l)
            self.ffn2(l)
        return self.finish()

    def finish(self):
        self.flush()
        for t in range(NT):
            self.stores.append(self.load(self.out[t * 128:(t + 1) * 128, :], self.x[:, t, :], self.t_x[t]))
        self.Y(lambda e: e.nop(), self.stores, sig=False)

    def cols(self, name, idx, a, b):
        return ((name, idx, a, b),)

    def load_gb(self, g, b, l, *w):
        a = self.load(self.gb[:, 0, :], self.ins[g][l:l + 1, :].broadcast_to([128, D]), *w)
        return [a, self.load(self.gb[:, 1, :], self.ins[b][l:l + 1, :].broadcast_to([128, D]), *w)]

    def mixer1(self, l):
        V, A, G, T = self.V, self.A, self.G, self.T
        ins = self.ins
        xa = (self.xh, self.xl, 0)
        vA, vB = self.u(0, 512), self.u(512, 512)
        qkA, qkB = self.u(10368, 2560), self.u(1024, 2560)
        flat = self.x[:, :, :].rearrange("p t d -> p (t d)")
        qT = {"A": flat[:, 0:2048], "B": self.u(3584, 2048)}
        kT = {"A": flat[:, 2048:3072], "B": self.u(5632, 1024)}
        pb, ob = self.u(6656, 1536), self.u(9216, 1024)
        gbf = self.gb[:, :, :].rearrange("p a b -> p (a b)")
        work = {"A": ([self.u(6656, 640), self.u(7296, 640)], self.u(7936, 1280),
                      [self.u(9216, 256), self.u(9472, 256)]),
                "B": ([gbf[:, 0:640], self.u(8576, 640)], gbf[:, 640:1920], [flat[:, 3072:3328], flat[:, 3328:3584]])}
        gq, gk = self.u(10240, 64), self.u(10304, 64)
        sink = self.st[:, 200:208]
        hold = self.free_ar
        tgain = [self.load(gq, ins["b_q_gain"][l:l + 1, :].broadcast_to([128, 64]), hold),
                 self.load(gk, ins["b_k_gain"][l:l + 1, :].broadcast_to([128, 64]), hold)]
        tsink = self.load(sink, ins["a_sink"][l:l + 1, :].broadcast_to([128, 8]), hold)
        t3 = lambda a: a.rearrange("p (t c) -> p t c", t=NT)
        qk3 = {"A": t3(qkA), "B": t3(qkB)}
        v3 = {"A": t3(vA), "B": t3(vB)}
        got = {"A": [], "B": []}

        def proj(br, c0):
            def e1(t, i, ap, tok):
                r = self.cp(A if t % 2 else V, qk3[br][:, t, 0:512], ap, tok, hold)
                self.give(i, r)
                got[br].append(r)

            def e2(t, i, ap, tok):
                ln = A if t % 2 else V
                r = self.cp(ln, qk3[br][:, t, 512:640], ap[:, 0:128], tok, hold)
                r2 = self.cp(ln, v3[br][:, t, :], ap[:, 128:256], tok, hold)
                self.give(i, r, r2)
                got[br].extend([r, r2])
            yield from self.gemm(8, self.cols("w_in", l, c0, c0 + 512), xa, self.t_xT, "T", 4, e1,
                                 pair=br == "A" and l > 0)
            yield from self.gemm(8, self.cols("w_in", l, c0 + 512, c0 + 768), xa, self.t_xT, "T", 4, e2)

        qT3 = {b: v.rearrange("p (j s) -> p j s", j=4) for b, v in qT.items()}
        kT3 = {b: v.rearrange("p (j s) -> p j s", j=2) for b, v in kT.items()}
        qkT = {}

        def prologue(br, free_q):
            out, prev, turned = [], free_q, [free_q, free_q]
            ros, tmp, kds = work[br]
            for t in range(NT):
                src = qk3[br][:, t, :]
                w = [got[br]]
                ro, kd = ros[t % 2], kds[t % 2]
                if br == "B":
                    w = self.head_norm(src, 10, 64, [(0, 8, gq), (8, 2, gk)], tmp[:, 0:640], t * 10, got[br], tgain,
                                       free_q, prev)
                cos, sin = self.c("cos" + br)[:, t * 32:t * 32 + 32], self.c("sin" + br)[:, t * 32:t * 32 + 32]
                r = self.rope(src.rearrange("p (h d) -> p h d", h=10), ro.rearrange("p (h d) -> p h d", h=10), 10,
                              1 if br == "A" else 2, 32 if br == "A" else 16, cos, sin, tmp, w, prev, turned[t % 2],
                              self.t_cst)
                kv = ro[:, 512:640].rearrange("p (k d) -> p k d", k=2)
                k2 = self.cp(G, kd.rearrange("p (k w d) -> p k w d", k=2, w=2),
                             kv.unsqueeze(2).broadcast_to([128, 2, 2, 64]), r, turned[t % 2])
                prev = r

                for _ in range(2 if br == "B" else 1):
                    yield

                def put(dst3, t=t):
                    def f(j, m, i, v, tok):
                        c = self.cp(A if t % 2 else V, dst3[:, j:j + m, t * 128:t * 128 + 128], v, tok, free_q)
                        self.give(i, c)
                        out.append(c)
                    return f
                self.turn(ro[:, 0:512], 4, r, put(qT3[br]))
                self.turn(kd, 2, [k2], put(kT3[br]))
                turned[t % 2] = [T.last()]
            qkT[br] = out

        def branch(br, free_q):
            n = 0 if br == "A" else 1
            keep = {t: [] for t in range(NT)}

            def qk(h, t, k0, k1):
                a = slice((h % 2) * 64, (h % 2) * 64 + 64)
                return [(qT3[br][a, h // 2, t * 128:t * 128 + 128], kT3[br][a, h // 4, k0 * 128:k1 * 128])]

            def val(h, k):
                return v3[br][:, k, (h // 4) * 64:(h // 4) * 64 + 64]

            def put(t, c, o, toks):
                self.turn_split(o, 4, toks, self.ah, self.al, 4 * n, t, keep[t], self.a_free)
            if br == "A":
                keys = lambda t: (max(0, t - 1), min(NT, t + 2))
                mask = lambda t, k0, k1: self.c("band")[:, (k0 - t + 1) * 128:(k1 - t + 1) * 128]
                sk = sink
            else:
                keys = lambda t: (0, NT)
                mask = sk = None
            ready = [qkT[br], got[br], tsink, self.t_cst]
            n1 = 384 if br == "A" else 512
            yield from self.attend(range(8), 64, qk, keys, val, 0.125, ready, free_q, pb,
                                   self.u(6656 + 3 * n1, 2 * n1), ob, put, mask, sk, wide=n1)
            self.t_br[n] = keep

        self.t_br = [None] * 3
        drive((proj("A", 0), 1))
        if l > 0:
            park = [self.load(self.park[t * 128:(t + 1) * 128, :], self.x[:, t, :], self.t_x[t]) for t in range(NT)]
            self.stores += park
            back = self.park
        else:
            park, back = [], ins["x"]
        xfree0 = [park, self.t_xr]
        mg = self.x[:, :, :].rearrange("p t (h s) -> p (t h) s", h=2)
        uT = self.u(10368, 2048).rearrange("p (k s) -> p k s", k=4)
        vc = self.u(12416, 2048).rearrange("p (t c) -> p t c", t=NT)
        t_u, t_v, cz = [], [], {}

        def eu(o, i, ap, tok):
            r = self.act(uT[:, o, :], ap, ACT.Gelu, tok, cz["free"])
            self.give(i, r)
            t_u.append(r)

        def ev(t, i, ap, tok):
            r = self.act(vc[:, t, :], ap, ACT.Gelu, tok, cz["free"])
            self.give(i, r)
            t_v.append(r)

        free = {}

        def projB():
            yield from proj("B", 768)
            while "u" not in free:
                yield
            cz["free"] = free["u"]
            yield from self.gemm(8, self.cols("w_in", l, 1536, 2048), xa, self.t_xT, "F", 4, eu)
            yield from self.gemm(8, self.cols("w_in", l, 2048, 2560), xa, self.t_xT, "T", 4, ev)
            while "sg" not in free:
                yield
            for o in range(4):
                sg_free[o] = free["sg"]
            yield from gates(0)

        def proB():
            while len(got["B"]) < 12 or "u" not in free:
                yield
            yield from prologue("B", [free["u"], xfree0, self.gb_free()])
            free["sg"] = self.snap()

        sgs = [self.u(1024 + 512 * q, 512) for q in range(4)]
        tms = [self.u(6656, 512), self.u(7168, 512)]
        hb = self.st[:, 208:232]
        thb = self.ts(V, hb, self.p("b_gate", l * 24, 24), 0.5, None, ALU.mult, None, self.t_par, hold)
        sg_free, tm_free, t_mg = [None] * 4, [None] * 2, [None] * 8
        nt = [0]

        def gates(n):
            for mgp in range(2):
                t_sg = [None] * 4

                def eg(o, i, ap, tok):
                    m = mgp * 4 + o
                    r = self.act(sgs[o], ap, ACT.Tanh, tok, thb, sg_free[o], bias=hb[:, n * 8 + m:n * 8 + m + 1],
                                 scale=0.5)
                    self.give(i, r)
                    t_sg[o] = r

                def eb(o, i, ap, tok):
                    m = mgp * 4 + o
                    if n == 0:
                        r = self.stt(mg[:, m, :], sgs[o], 1.0, ap, ALU.add, ALU.mult, tok, t_sg[o], t_mg[m])
                        self.give(i, r)
                        sg_free[o] = [r]
                    else:
                        q = nt[0] % 2
                        nt[0] += 1
                        r = self.stt(tms[q], sgs[o], 1.0, ap, ALU.add, ALU.mult, tok, t_sg[o], tm_free[q])
                        self.give(i, r)
                        sg_free[o] = [r]
                        r = self.tt(G, mg[:, m, :], mg[:, m, :], tms[q], ALU.add, r, t_mg[m])
                        tm_free[q] = [r]
                    t_mg[m] = [r]
                c0 = 2560 + n * 1024 + mgp * 512
                yield from self.gemm(8, self.cols("w_in", l, c0, c0 + 512), xa, self.t_xT, "F", 4, eg)
                while "mg" not in free:
                    yield
                yield from self.gemm(4, self.cols("w_branch", (l, n), mgp * 512, mgp * 512 + 512),
                                     (self.ah, self.al, 4 * n), self.t_br[n], "F", 4, eb)

        pb_ = projB()
        beside(prologue("A", [hold, xfree0]), (pb_, 1))
        free["u"] = self.snap()
        beside(together(branch("A", free["u"]), proB()), (pb_, 1))
        freeB0 = self.snap()
        free["mg"] = freeB0
        for m in range(8):
            t_mg[m] = [xfree0, freeB0]
        drive((branch("B", freeB0), 2), (pb_, 1))
        freeB = self.snap()
        tm_free = [freeB] * 2
        tg = self.load_gb("ln1_g", "ln1_b", l, self.gb_free(), freeB)
        lg, lb, bs = self.u(3584, 512), self.u(4096, 512), self.u(4608, 512)
        wsT = self.u(5120, 512)
        tp = [self.load(lg, ins["c_ln_g"][l:l + 1, :].broadcast_to([128, 512]), freeB),
              self.load(lb, ins["c_ln_b"][l:l + 1, :].broadcast_to([128, 512]), freeB),
              self.load(bs, ins["c_bs"][l:l + 1, :].broadcast_to([128, 512]), freeB),
              self.load(wsT, ins["wsT"][l, :, :], freeB)]

        def chunks():
            vn = []
            for t in range(NT):
                st, mv, rs = (self.st[:, 64 + t * 16 + a:64 + t * 16 + b] for a, b in ((0, 6), (6, 8), (8, 9)))
                x = vc[:, t, :]
                a = V(lambda e, st=st, x=x: e.bn_stats(st, x), t_v, freeB)
                a = V(lambda e, st=st, mv=mv: e.bn_aggr(mv, st), a)
                g = self.rstd(rs, mv[:, 1:2], 1.0, LN_EPS, a)
                c = self.stt(x, x, mv[:, 0:1], lg, ALU.subtract, ALU.mult, a, tp)
                vn.append(self.stt(x, x, rs, lb, ALU.mult, ALU.add, c, g, tp))
                yield
            keep = {}
            mt = [self.u(7680, 512), self.u(8192, 512)]
            mt_free = [freeB, freeB]
            for g in range(4):
                i, bk, bt = self.bank()
                for n in range(NT):
                    tok = self.mm(bk[:, n * 128:n * 128 + 128], vc[:, n, g * 128:g * 128 + 128],
                                  wsT[:, g * 128:g * 128 + 128], True, True, vn, tp, bt, sig=(n == 3))
                m = mt[g % 2]
                r = self.tt(V, m.rearrange("p (n i) -> p n i", n=4), bk[:, :].rearrange("p (n i) -> p n i", n=4),
                            bs[:, g * 128:g * 128 + 128].unsqueeze(1).broadcast_to([128, 4, 128]), ALU.add, tok, tp,
                            mt_free[g % 2])
                self.give(i, r)
                r = self.tt(V, m, m, uT[:, g, :], ALU.mult, r, t_u)
                s = self.split(self.ah[:, 8 + g, :], self.al[:, 8 + g, :], m, r, self.a_free, freeB)
                mt_free[g % 2] = s
                keep[g] = s
                yield
            self.t_br[2] = (keep,)
        drive((gates(1), 1), (chunks(), 1))
        drive((gates(2), 1))
        self.a_free = [T.last()]
        xfree = [T.last()]
        tm_ = {}
        for m in range(8):
            tm_[m] = self.split(self.xh[:, m, :], self.xl[:, m, :], mg[:, m, :], t_mg[m], xfree,
                                scale=self.c("pw")[:, 15:16])
        self.free_ar = self.snap()
        self.mem_operand('memT', 0, self.free_ar)
        self.t_x = [[self.load(self.x[:, t, :], back[t * 128:(t + 1) * 128, :], list(tm_.values()))] for t in range(NT)]
        self.t_xr = None
        gen = self.residual(8, lambda hf: self.cols("w_mix_out", l, hf * 512, hf * 512 + 512), xa, (tm_,),
                            self.ln_turn(tg), self.ln_pre, scale=True)
        drive((gen, 1))

    def chain(self, *fs):
        for f in fs:
            yield from f()

    def gb_free(self):
        return [list(self.t_x), self.t_xn[0], self.t_xn[1]]

    def mem_operand(self, name, at, *w):
        raw = self.u(at, 2048)
        self.mem_split(raw, self.load(raw, self.ins[name], *w))

    def mem_split(self, raw, tok):
        view = lambda t: t[:, 8:12, :].rearrange("p a (b s) -> p (a b) s", b=2)
        self.mem = (view(self.ah), view(self.al), 0)
        self.t_mem = self.split(self.mem[0], self.mem[1], raw.rearrange("p (k s) -> p k s", k=8), tok, self.a_free)

    def mem_second(self):
        hold = self.free_ar
        raw = self.u(0, 2048)
        tok = self.load(raw, self.ins["mem_2T"], hold)
        rows = [self.u(2048 + 1024 * t, 1024) for t in range(2)]
        tr = [self.load(rows[t], self.ins["mem_2"][t * 128:t * 128 + 128, :], hold) for t in range(2)]
        yield
        self.mem_split(raw, tok)
        rs = self.st[:, 248:250]
        w = [self.act(rows[t], rows[t], ACT.Square, tr[t], hold, acc=rs[:, t:t + 1]) for t in range(2)]
        self.t_mrs = self.rstd(rs, rs, 1.0 / D, RMS_EPS, w)

    def cross1(self, l):
        V, A, T = self.V, self.A, self.T
        hold = [self.free_ar, self.t_mem]
        tg = self.load_gb("ln2_g", "ln2_b", l, self.gb_free())
        kT = self.u(2048, 1024).rearrange("p (h s) -> p h s", h=4)
        vm = self.u(3072, 1024).rearrange("p (t c) -> p t c", t=2)
        qT = self.u(4096, 2048).rearrange("p (h s) -> p h s", h=4)
        pb, ptb, ob = self.u(6144, 1024), self.u(7168, 1024), self.u(8192, 1024)
        tm, ma = self.t_mem, self.mem
        t_k, t_v, t_q = [], [], []

        def ek(o, i, ap, tok):
            r = self.cp(A if o % 2 else V, kT[:, o, :], ap, tok, hold)
            self.give(i, r)
            t_k.append(r)

        def ev(t, i, ap, tok):
            r = self.cp(A if t % 2 else V, vm[:, t, :], ap, tok, hold)
            self.give(i, r)
            t_v.append(r)

        def eq(o, i, ap, tok):
            r = self.cp(A if o % 2 else V, qT[:, o, :], ap, tok, hold)
            self.give(i, r)
            t_q.append(r)
        drive((self.gemm(8, self.cols("x_wkv", l, 0, 512), ma, tm, "F", 4, ek, width=256), 1))
        drive((self.gemm(8, self.cols("x_wkv", l, 512, 1024), ma, tm, "T", 2, ev), 1))
        drive((self.gemm(8, self.cols("x_wq", l, 0, 512), (self.xh, self.xl, 0), self.t_xT, "F", 4, eq, pair=True), 1))
        keep = {t: [] for t in range(NT)}

        def put(t, c, o, toks):
            self.turn_split(o, 4, toks, self.ah, self.al, 0, t, keep[t], self.a_free)
        drive((self.attend(
            range(4), 128, lambda h, t, k0, k1: [(qT[:, h, t * 128:t * 128 + 128], kT[:, h, :])], lambda t: (0, 2),
            lambda h, k: vm[:, k, h * 128:h * 128 + 128], 128 ** -0.5, [t_k, t_v, t_q], hold, pb, ptb, ob, put,
            wide=256), 1))
        self.free_ar = self.snap()
        drive((self.residual(4, lambda hf: self.cols("x_wo", l, hf * 512, hf * 512 + 512), (self.ah, self.al, 0),
                             keep, self.ln_turn(tg), self.ln_pre, scale=True), 1))
        self.a_free = [T.last()]

    def ffn1(self, l):
        V, A, G, T = self.V, self.A, self.G, self.T
        hold = self.free_ar
        tg = self.load_gb("ln3_g", "ln3_b", l, self.gb_free())
        xa = (self.xh, self.xl, 0)
        FT = 22
        ck = lambda j, m: self.p("conv_k", l * 132 + j * 44 + m, 1)
        cb = lambda m: self.p("conv_b", l * 44 + m, 1)
        bufs = [self.u(q * 512, 512) for q in range(8)]
        b_free = [hold] * 8
        nb = 0
        last = l == DEPTH - 1
        keep = [{}, {}]

        def up(m):
            if True:
                res, gl, prods = {}, {}, []
                half = int(m >= 10)

                def ev(o, i, ap, tok):
                    nonlocal nb
                    f = m + o % 2 + (FT if o >= 2 else 0)
                    s = nb % 8
                    nb += 1
                    b = bufs[s]
                    r = self.act(b, ap, ACT.Identity, tok, b_free[s], self.t_par, bias=cb(f), scale=ck(1, f))
                    if o > 0 and o - 1 in res:
                        res[o - 1]()
                    r = self.stt(b[:, 1:512], ap[:, 0:511], ck(0, f), b[:, 1:512], ALU.mult, ALU.add, r)
                    r = self.stt(b[:, 0:511], ap[:, 1:512], ck(2, f), b[:, 0:511], ALU.mult, ALU.add, r)
                    self.give(i, r)
                    if o < 2:
                        def gelu():
                            gl[o] = (self.act(b, b, ACT.Gelu, r), b, s)
                        res[o] = gelu
                    else:
                        prods.append((o - 2, b, s, r))
                    if o == 3:
                        rs_ = []
                        for p, b2, s2, r2 in prods:
                            ra, ba, sa = gl[p]
                            r3 = self.tt(V, ba, ba, b2, ALU.mult, ra, r2)
                            b_free[s2] = [r3]
                            rs_.append((p, ba, sa, r3))
                        for p, ba, sa, r3 in rs_:
                            k = (m + p) if m < 12 else m - 12 + p
                            w = self.split(self.ah[:, k, :], self.al[:, k, :], ba, r3, self.a_free)
                            b_free[sa] = w
                            keep[half][m + p - 10 * half] = w
                pieces = (("f_w_up", l, m * 128, m * 128 + 256), ("f_w_up", l, (m + FT) * 128, (m + FT) * 128 + 256))
                return self.gemm(8, pieces, xa, self.t_xT, "F", 4, ev, pair=m == 0)

        if last:
            slots = [self.u(12288, 1024), self.u(13312, 1024)]
            self.t_xn = [hold, hold]
            norm = self.rms_turn(slots, tg)
        else:
            norm = self.ln_turn(tg)
        self.ffn_order(up, "f_w_down", l, keep, norm, self.ln_pre, True)

    def ffn_order(self, up, name, l, keep, norm, pre, scale):
        T = self.T
        hid = lambda m: (lambda hf: ((name, (l, m), hf * 512, hf * 512 + 512),))
        for m in range(0, 12, 2):
            drive((up(m), 1))
        drive((self.residual(10, hid(0), (self.ah, self.al, 0), (keep[0],), scale=scale), 1))
        self.a_free = [T.last()]
        for m in range(12, 22, 2):
            drive((up(m), 1))
        self.free_ar = self.snap()
        drive((self.residual(12, hid(10), (self.ah, self.al, [10, 11] + list(range(10))), (keep[1],), norm, pre), 1))
        self.a_free = [T.last()]

    def mixer2(self):
        V, A, G, T = self.V, self.A, self.G, self.T
        ins = self.ins
        xa = (self.xh, self.xl, 0)
        hold = self.free_ar
        gain = ("n_mix", 0)
        iqT = self.u(0, 4096).rearrange("p (j s) -> p j s", j=8)
        ikT = self.u(4096, 512)
        iqs = [self.u(q, 2048).rearrange("p (t c) -> p t c", t=NT) for q in (4608, 12288)]
        sc = self.u(6656, 2048).rearrange("p (t s) -> p t s", t=NT)
        iw = self.u(8704, 64).rearrange("p (t c) -> p t c", t=NT)
        ik = self.u(8768, 256).rearrange("p (t c) -> p t c", t=NT)
        ikd = self.u(9024, 128)
        tmp = self.u(9152, 512)
        rl = [self.u(9664 + 512 * q, 512) for q in range(3)]
        t_ik, t_iw = [], []

        def ei(t, i, ap, tok):
            r = self.ts(V, iw[:, t, :], ap[:, 0:16], 1.0 / 32.0, None, ALU.mult, None, tok, hold)
            r2 = self.cp(V, ik[:, t, :], ap[:, 16:80], tok, hold)
            self.give(i, r2)
            t_iw.append(r)
            t_ik.append(r2)

        def rope_in_place(src, nh, half, cs, t, prev, toks):
            cos = self.c("cos" + cs)[:, t * half:t * half + half]
            sin = self.c("sin" + cs)[:, t * half:t * half + half]
            v = src.rearrange("p (h d) -> p h d", h=nh)
            x1, x2 = v[:, :, 0:half], v[:, :, half:2 * half]
            n = nh * half
            q = [tmp[:, a * n:(a + 1) * n].rearrange("p (h f) -> p h f", h=nh) for a in range(4)]
            c = cos.unsqueeze(1).broadcast_to([128, nh, half])
            s = sin.unsqueeze(1).broadcast_to([128, nh, half])
            a0 = self.tt(V, q[0], x1, c, ALU.mult, toks, prev, self.t_cst)
            a1 = self.tt(V, q[1], x2, s, ALU.mult, toks, prev, self.t_cst)
            a2 = self.tt(V, q[2], x2, c, ALU.mult, toks, prev, self.t_cst)
            a3 = self.tt(V, q[3], x1, s, ALU.mult, toks, prev, self.t_cst)
            r1 = self.tt(V, x1, q[0], q[1], ALU.subtract, a0, a1, a3)
            r2 = self.tt(V, x2, q[2], q[3], ALU.add, a2, a3, r1)
            return [r1, r2]

        t_ikT, t_iqT = [], {t: [] for t in range(NT)}
        t_iq = [{}, {}]

        def index_proj(cg):
            def eq(t, i, ap, tok):
                r = self.cp(A, iqs[cg][:, t, :], ap, tok, hold, self.t_xn if cg else None)
                self.give(i, r)
                t_iq[cg][t] = r
            return self.gemm(8, self.cols("w_in_ab_2", 0, 2048 + cg * 512, 2560 + cg * 512), xa, self.t_xT, "T", 4,
                             eq, gain=gain, pair=cg == 0)

        def index_rope():
            prev = hold
            for t in range(NT):
                r = rope_in_place(iqs[0][:, t, :], 8, 8, "i", t, prev, t_iq[0][t])
                prev = r
                yield
                self.turn(iqs[0][:, t, :], 4, r, iq_dst(0, t))
            while len(t_ik) < NT:
                yield
            prev = [prev, T.last()]
            for t in range(NT):
                r = rope_in_place(ik[:, t, :], 1, 8, "i", t, prev, t_ik)
                d = self.cp(V, ikd.rearrange("p (w d) -> p w d", w=2),
                            ik[:, t, :].unsqueeze(1).broadcast_to([128, 2, 64]), r, prev)

                def dst(j, m, i, v, tok, t=t):
                    c = self.cp(A, ikT[:, t * 128:t * 128 + 128], v[:, 0, :], tok, hold)
                    self.give(i, c)
                    t_ikT.append(c)
                self.turn(ikd, 1, [d], dst)
                prev = [d, T.last()]
                yield
            while len(t_iq[1]) < NT:
                yield
            for t in range(NT):
                r = rope_in_place(iqs[1][:, t, :], 8, 8, "i", t, prev, t_iq[1][t])
                prev = r
                yield
                self.turn(iqs[1][:, t, :], 4, r, iq_dst(1, t))

        def iq_dst(cg, t):
            def dst(j, m, i, v, tok):
                c = self.cp(A if t % 2 else V, iqT[:, cg * 4 + j:cg * 4 + j + m, t * 128:t * 128 + 128], v, tok, hold)
                self.give(i, c)
                t_iqT[t].append(c)
            return dst
        t_sc = {}
        top = self.st[:, 232:240]

        def index_scores():
            n = 0
            rf = [hold] * 3
            for t in range(NT):
                w = (t + 1) * 128
                prev = None
                while len(t_iqT[t]) < 2:
                    yield
                for h in range(16):
                    a = slice((h % 2) * 64, (h % 2) * 64 + 64)
                    i, bk, bt = self.bank()
                    tok = self.mm(bk[:, 0:w], iqT[a, h // 2, t * 128:t * 128 + 128], ikT[a, 0:w], True, True,
                                  t_iqT[t], t_ikT[:t + 1], bt, sig=True)
                    r = rl[n % 3][:, 0:w]
                    c = self.act(r, bk[:, 0:w], ACT.Relu, tok, rf[n % 3])
                    self.give(i, c)
                    s = sc[:, t, 0:w]
                    wv = iw[:, t, h:h + 1]
                    if h == 0:
                        prev = self.ts(V, s, r, wv, None, ALU.mult, None, c, t_iw, hold)
                    else:
                        prev = self.stt(s, r, wv, s, ALU.mult, ALU.add, c, prev)
                    rf[n % 3] = [prev]
                    n += 1
                    if h % 2:
                        yield
                d = sc[:, t, t * 128:w]
                prev = self.tt(V, d, d, self.c("causal"), ALU.add, prev, self.t_cst)
                t_sc[t] = prev
                yield

        def choose():
            prev = None
            for t in range(1, NT):
                w = (t + 1) * 128
                s = sc[:, t, 0:w]
                while t not in t_sc:
                    yield
                prev = [prev, t_sc[t]]
                for _ in range(16):
                    a = V(lambda e, s=s: e.max(top, s), prev)
                    prev = V(lambda e, s=s: e.match_replace(s, top, s, GONE), a)
                    yield
                t_sc[t] = self.ts(V, s, s, -2.0e38, BIG, ALU.is_gt, ALU.mult, prev)
                yield
        chooser = choose()

        def scoring():
            for _ in index_scores():
                if 1 in t_sc:
                    next(chooser)
                yield

        drive((index_proj(0), 1))
        ikg = self.gemm(8, self.cols("w_in_ab_2", 0, 3072, 3152), xa, self.t_xT, "T", 4, ei, gain=gain, per=8)
        drive((self.chain(lambda: ikg, lambda: index_proj(1)), 1), (index_rope(), 1), (scoring(), 1))
        freeI = self.snap()
        qT = self.u(0, 2048).rearrange("p (h s) -> p h s", h=4)
        kT = self.u(2048, 2048).rearrange("p (h s) -> p h s", h=4)
        vt = self.u(4096, 2048).rearrange("p (t c) -> p t c", t=NT)
        raws = [self.u(q, 2048).rearrange("p (t c) -> p t c", t=NT) for q in (8704, 12032)]
        sq = self.u(10752, 512)
        tmp = self.u(11264, 512)
        gq = [self.u(11776, 128), self.u(11904, 128)]
        gbf = self.gb[:, :, :].rearrange("p a b -> p (a b)")
        pbf, ptb, obf = gbf[:, 0:1536], self.u(11936, 1024), self.u(12960, 1024)
        tgain = [self.load(gq[0], ins["a_q_norm_2"].broadcast_to([128, 128]), freeI),
                 self.load(gq[1], ins["a_k_norm_2"].broadcast_to([128, 128]), freeI)]
        t_qk = []
        t_vt = []

        t_r = [{}, {}]
        pro = {}

        def project():
            for which in range(2):
                def er(t, i, ap, tok, which=which):
                    r = self.cp(A, raws[which][:, t, :], ap, tok, freeI)
                    self.give(i, r)
                    t_r[which][t] = r
                yield from self.gemm(8, self.cols("w_in_ab_2", 0, which * 512, which * 512 + 512), xa, self.t_xT,
                                     "T", 4, er, gain=gain)

            def ev(t, i, ap, tok):
                r = self.cp(A, vt[:, t, :], ap, tok, freeI)
                self.give(i, r)
                t_vt.append(r)
            yield from self.gemm(8, self.cols("w_in_ab_2", 0, 1024, 1536), xa, self.t_xT, "T", 4, ev, gain=gain)
            while 0 not in pro:
                yield
            yield from self.gemm(8, self.cols("w_in_ab_2", 0, 1536, 2048), xa, self.t_xT, "F", 4, eu, gain=gain)

        t_u = []
        uall = raws[0]

        def eu(o, i, ap, tok):
            r = self.cp(A, uall[:, o, :], ap, tok, pro[0])
            self.give(i, r)
            t_u.append(r)

        def prologue():
            pv = None
            for which in range(2):
                while len(t_r[which]) < NT:
                    yield
                for t in range(NT):
                    raw = raws[which]
                    w = self.head_norm(raw[:, t, :], 4, 128, [(0, 4, gq[which])], sq, t * 4, t_r[which][t], tgain,
                                       freeI, pv)
                    w = rope_in_place(raw[:, t, :], 4, 16, "q", t, freeI, w)
                    pv = w
                    yield
                    dd = qT if which == 0 else kT

                    def dst(j, m, i, v, tok, t=t):
                        c = self.cp(A, dd[:, j:j + m, t * 128:t * 128 + 128], v, tok, freeI)
                        self.give(i, c)
                        t_qk.append(c)
                    self.turn(raw[:, t, :], 4, w, dst)
                pro[which] = self.snap()

        def pool_branch():
            uT = [self.u(10752, 528), self.u(11280, 528)]
            pw = self.u(11808, 128)
            ub = gbf[:, 1536:2048]
            keep = []
            prev = [freeP, self.gb_free()]
            z0 = V(lambda e: e.memset(uT[0][:, 0:16], 0.0), prev)
            z1 = V(lambda e: e.memset(uT[1][:, 0:16], 0.0), prev)
            zz = [z0, z1]
            tp = prev
            for g, win in enumerate(POOL_W):
                tw = self.load(pw, ins["pool_w_2"][g, :, :], tp)
                u = uall[:, g, :]
                cur = self.cp(V, uT[0][:, 16:528], u, t_u, zz, prev)
                src, k, sh = 0, 0, 1
                while sh < win:
                    s_, d_ = uT[k % 2], uT[(k + 1) % 2]
                    cur = self.tt(V, d_[:, 16:528], s_[:, 16:528], s_[:, 16 - sh:528 - sh], ALU.add, cur)
                    sh *= 2
                    k += 1
                    yield
                s_ = uT[k % 2]
                po = ub
                r = self.tt(V, s_[:, 16:32], s_[:, 16:32], self.c("invc")[:, g * 16:g * 16 + 16], ALU.mult, cur,
                            self.t_cst)
                r1 = self.tt(V, po[:, 0:16], s_[:, 16:32], u[:, 0:16], ALU.subtract, r, prev)
                r2 = self.stt(po[:, 16:512], s_[:, 32:528], 1.0 / win, u[:, 16:512], ALU.mult, ALU.subtract, cur,
                              prev)
                yield
                i, bk, bt = self.bank()
                tok = self.mm(bk[:, :], pw, po, True, True, r1, r2, tw, bt, sig=True)
                prev = [tok, r1, r2]
                tp = [tok]
                yield
                rr = self.ts(V, uT[(k + 1) % 2][:, 16:528], bk[:, :], self.p("pool_scale", g, 1), None, ALU.mult,
                             None, tok, self.t_par)
                self.give(i, rr)
                sp = self.split(self.ah[:, 4 + g, :], self.al[:, 4 + g, :], uT[(k + 1) % 2][:, 16:528], rr,
                                self.a_free)
                prev = prev + sp
                keep += sp
                yield
            self.t_pool = keep
        drive((project(), 1), (prologue(), 1), (chooser, 2))
        freeP = self.snap()
        keep = {t: [] for t in range(NT)}

        def put(t, c, o, toks):
            self.turn_split(o, 4, toks, self.ah, self.al, 0, t, keep[t], self.a_free)

        def mask(t, k0, k1):
            return self.c("causal") if t == 0 else sc[:, t, 0:(t + 1) * 128]
        att = self.attend(
            range(4), 128, lambda h, t, k0, k1: [(qT[:, h, t * 128:t * 128 + 128], kT[:, h, 0:k1 * 128])],
            lambda t: (0, t + 1), lambda h, k: vt[:, k, h * 128:h * 128 + 128], 128 ** -0.5,
            [t_qk, t_vt, list(t_sc.values())], [freeP, self.gb_free()], pbf, ptb, obf, put, mask)
        drive((att, 1), (pool_branch(), 1))
        self.free_ar = self.snap()
        self.t_xn = [self.free_ar, self.free_ar]
        self.resid2(8, lambda hf: self.cols("w_out_ab_2", 0, hf * 512, hf * 512 + 512), (self.ah, self.al, 0),
                    {t: [keep[t], self.t_pool] for t in range(NT)}, self.mem_second())

    def resid2(self, nk, pieces, act, toks, mem=None):
        for n, _ in enumerate(self.residual(nk, pieces, act, toks, self.rms_turn(self.xn_slots()))):
            if mem is not None and n in (0, 4):
                next(mem, None)
        self.a_free = [self.T.last()]

    def convmod(self):
        V, A, G, T = self.V, self.A, self.G, self.T
        xa = (self.xh, self.xl, 0)
        hold = self.free_ar
        hT = self.u(0, 8 * 542).rearrange("p (k s) -> p k s", k=8)
        y = self.u(4336, 4096).rearrange("p (k s) -> p k s", k=8)
        th = [self.u(8432 + 512 * q, 512) for q in range(4)]
        gain = ("n_mix", 8)
        hb = self.st[:, 64:72]
        thb = self.ts(V, hb, self.p("cv_bin", 8, 8), 0.5, None, ALU.mult, None, self.t_par, hold)
        z = V(lambda e: e.memset(hT[:, :, 0:30], 0.0), hold)
        th_free = [hold] * 4
        t_h = {}
        res = {}
        n = [0]
        t_y = {}
        PEC = (6, 7)
        PLC = (1, 3)

        def conv(m):
            r = self.ts(V, y[:, m, :], hT[:, m, 30:542], self.p("dw_w", m * 31 + 30, 1), self.p("dw_b", m, 1),
                        ALU.mult, ALU.add, t_h[m], z, hold)
            for j in range(30):
                r = self.stt(y[:, m, :], hT[:, m, j:j + 512], self.p("dw_w", m * 31 + j, 1), y[:, m, :], ALU.mult,
                             ALU.add, r)
                if j % 4 == 3:
                    yield
            t_y[m] = r

        def conv_pe(m, q):
            flat = lambda t: t[:, 0:8, :].rearrange("p k s -> p (k s)")[:, q * 542:q * 542 + 542]
            oh, ol = flat(self.ah), flat(self.al)
            s = self.split(oh, ol, hT[:, m, :], t_h[m], z, self.a_free)
            i, bk, bt = self.bank()
            for j in range(31):
                d = j % 8
                a = slice((d % 4) * 128, (d % 4) * 128 + 128)
                dh, dl = self.ah[:, 8 + d // 4, a], self.al[:, 8 + d // 4, a]
                g = self.split(dh, dl, self.c("ident"), self.t_cst, self.t_par, d_free[d],
                               scale=self.p("dw_w", m * 31 + j, 1))
                for e, (lw, rw) in enumerate(((dh, oh), (dh, ol), (dl, oh))):
                    tok = self.mm(bk[:, :], lw, rw[:, j:j + 512], j == 0 and e == 0, j == 30 and e == 2, s, g, bt,
                                  sig=(e == 2))
                d_free[d] = [tok]
                if j % 4 == 3:
                    yield
            t_y[m] = self.act(y[:, m, :], bk[:, :], ACT.Identity, tok, hold, self.t_par, bias=self.p("dw_b", m, 1))
            self.give(i, t_y[m])
        d_free = [self.a_free] * 8

        def proj():
            for m in (0, 2, 4, 6):
                def ev(o, i, ap, tok, m=m):
                    if o < 2:
                        s = n[0] % 4
                        n[0] += 1
                        r = self.act(th[s], ap, ACT.Tanh, tok, thb, th_free[s], bias=hb[:, m + o:m + o + 1],
                                     scale=0.5)
                        self.give(i, r)
                        r = self.ts(V, th[s], th[s], 0.5, 0.5, ALU.mult, ALU.add, r)
                        res[o] = (r, s)
                    else:
                        r0, s = res[o - 2]
                        f = m + o - 2
                        r = self.stt(hT[:, f, 30:542], ap, self.p("cv_bin", f, 1), th[s], ALU.add, ALU.mult, tok, r0,
                                     hold)
                        self.give(i, r)
                        th_free[s] = [r]
                        t_h[f] = r
                pieces = (("conv_w_in_2", 0, 1024 + m * 128, 1024 + m * 128 + 256),
                          ("conv_w_in_2", 0, m * 128, m * 128 + 256))
                yield from self.gemm(8, pieces, xa, self.t_xT, "F", 4, ev, gain=gain, pair=m == 0)
            for q, m in enumerate(PEC):
                yield from conv_pe(m, q)

        tp = [self.u(11504 + 512 * q, 512) for q in range(3)]
        tf = [hold] * 3

        def conv_pool(m):
            while m not in t_h:
                yield
            r = self.act(y[:, m, :], hT[:, m, 30:542], ACT.Identity, t_h[m], z, hold, self.t_par,
                         bias=self.p("dw_b", m, 1), scale=self.p("dw_w", m * 31 + 30, 1))
            for j in range(30):
                q = self.acopy(tp[j % 3], hT[:, m, j:j + 512], self.p("dw_w", m * 31 + j, 1), tf[j % 3])
                r = self.tt(G, y[:, m, :], y[:, m, :], tp[j % 3], ALU.add, q, r)
                tf[j % 3] = [r]
                yield
            t_y[m] = r

        def convs():
            for m in range(8):
                if m in PLC or m in PEC:
                    continue
                while m not in t_h:
                    yield
                yield from conv(m)
        drive((proj(), 1), (convs(), 1), (self.chain(*[lambda m=m: conv_pool(m) for m in PLC]), 3))
        self.free_pe = [T.last()]
        ones = self.c("ones")
        ib, mb, bt = self.bank()
        order = [0, 1, 2, 6, 4, 5, 7, 3]
        for q, m in enumerate(order):
            tok = self.mm(mb[:, :], ones, y[:, m, :], q == 0, q == 7, t_y[m], bt, self.t_cst, sig=(q == 7))
        mu = self.u(8432, 512)
        hold2 = self.snap()
        a = self.ts(V, mu, mb[:, :], 1.0 / D, None, ALU.mult, None, tok, hold2)
        self.give(ib, a)
        iv, vb, bt = self.bank()
        sq = [self.u(9456, 512), self.u(9968, 512), self.u(10480, 512)]
        sf = [hold2] * 3
        t_d = {}
        tot = self.st[:, 72:80]
        for m in range(8):
            d = self.tt(V, y[:, m, :], y[:, m, :], mu, ALU.subtract, a, t_y[m], tok)
            t_d[m] = d
            q = self.act(sq[m % 3], y[:, m, :], ACT.Square, d, sf[m % 3])
            tok2 = self.mm(vb[:, :], ones, sq[m % 3], m == 0, m == 7, q, bt, sig=True)
            sf[m % 3] = [tok2]
        var = self.u(10992, 512)
        r = self.ts(V, var, vb[:, :], 1.0 / D, RMS_EPS, ALU.mult, ALU.add, tok2, hold2)
        self.give(iv, r)
        i2, b2, bt = self.bank()
        for t in range(NT):
            tok = self.tr(b2[:, t * 128:t * 128 + 128], var[:, t * 128:t * 128 + 128], r, bt, sig=(t == 3))
        col = self.cp(V, tot[:, 0:4], b2[:, :].rearrange("p (t c) -> p t c", t=4)[:, :, 0], tok, hold2)
        self.give(i2, col)
        q = self.tt(G, tot[:, 0:4], tot[:, 0:4], self.c("pw")[:, 0:4], ALU.pow, col, self.t_cst)
        q = self.cp(V, var.rearrange("p (t c) -> p t c", t=4),
                    tot[:, 0:4].unsqueeze(2).broadcast_to([128, 4, 128]), q, tok)
        i2, rb, bt = self.bank()
        for t in range(NT):
            tok = self.tr(rb[:, t * 128:t * 128 + 128], var[:, t * 128:t * 128 + 128], q, bt, sig=(t == 3))
        rs = self.u(8944, 512)
        q = self.cp(V, rs, rb[:, :], tok, hold2)
        self.give(i2, q)
        keep = {}
        for m in range(8):
            ym = y[:, m, :]
            d = self.tt(V, ym, ym, rs, ALU.mult, q, t_d[m], tok2)
            e = self.act(ym, ym, ACT.Silu, d, self.t_par, bias=self.p("cln_b", m, 1), scale=self.p("cln_g", m, 1))
            keep[m] = self.split(self.ah[:, m, :], self.al[:, m, :], ym, e, self.a_free, self.free_pe)
        self.free_ar = self.snap()
        self.resid2(8, lambda hf: self.cols("conv_w_out_2", 0, hf * 512, hf * 512 + 512), (self.ah, self.al, 0),
                    (keep,), self.mem_second())

    def cross2(self, l):
        V, A, G, T = self.V, self.A, self.G, self.T
        ins = self.ins
        hold = [self.free_ar, self.t_mem, self.t_mrs]
        qT = self.u(0, 4096).rearrange("p (j s) -> p j s", j=8)
        kT = self.u(4096, 2048).rearrange("p (j s) -> p j s", j=8)
        vm = self.u(6144, 2048).rearrange("p (t c) -> p t c", t=2)
        raws = [self.u(q, 2048).rearrange("p (t c) -> p t c", t=4) for q in (8192, 10240)]
        sq = self.u(12288, 512)
        gq = [self.u(12800, 256), self.u(13056, 256)]
        pb, ptb, ob = self.u(8192, 768), self.u(8960, 512), self.u(13312, 1024)
        tgain = [self.load(gq[0], ins["cross_q_norm_2"][l:l + 1, :].broadcast_to([128, 256]), hold),
                 self.load(gq[1], ins["cross_k_norm_2"][l:l + 1, :].broadcast_to([128, 256]), hold)]
        tm, ma, t_rs = self.t_mem, self.mem, self.t_mrs
        rs = self.st[:, 248:250]
        xa = (self.xh, self.xl, 0)
        t_k, t_v, t_q = [], [], [[], []]
        t_r = [{} for _ in range(4)]
        done = [tm, None, None, None]

        def proj(j, name, cg, act, toks, n, gain):
            def er(t, i, ap, tok):
                w = [tok, hold, done[j - 2] if j >= 2 else tm]
                if j < 2:
                    r = self.ts(V, raws[j % 2][:, t, :], ap, rs[:, t:t + 1], None, ALU.mult, None, w, t_rs)
                else:
                    r = self.cp(A, raws[j % 2][:, t, :], ap, w)
                self.give(i, r)
                t_r[j][t] = r
            return self.gemm(8, self.cols(name, l, cg * 512, cg * 512 + 512), act, toks, "T", n, er, gain=gain)

        def prologue(j, n, dd, cg, out):
            pv = None
            raw = raws[j % 2]
            for t in range(n):
                while t not in t_r[j]:
                    yield
                wv = self.head_norm(raw[:, t, :], 2, 256, [(0, 2, gq[1 if j < 2 else 0])], sq, 2 + 2 * (4 * j + t),
                                    t_r[j][t], tgain, hold, pv, self.sq_free)
                pv = wv
                yield

                def dst(q, m, i, v, tok, t=t):
                    c = self.cp(A if t % 2 else V, dd[:, cg * 4 + q:cg * 4 + q + m, t * 128:t * 128 + 128], v, tok, hold)
                    self.give(i, c)
                    out.append(c)
                self.turn(raw[:, t, :], 4, wv, dst)
            self.sq_free = [pv]
            done[j] = [T.last()]

        def values(cg):
            def ev(t, i, ap, tok):
                r = self.ts(V, vm[:, t, cg * 512:cg * 512 + 512], ap, rs[:, t:t + 1], None, ALU.mult, None, tok,
                            t_rs, hold)
                self.give(i, r)
                t_v.append(r)
            return self.gemm(8, self.cols("cross_wv_2", l, cg * 512, cg * 512 + 512), ma, tm, "T", 2, ev,
                             gain=("n_mem", l * 8))
        self.sq_free = None
        gm, gx = ("n_mem", l * 8), ("n_cross", l * 8)
        drive((proj(0, "cross_wk_2", 0, ma, tm, 2, gm), 1))
        drive((proj(1, "cross_wk_2", 1, ma, tm, 2, gm), 1), (prologue(0, 2, kT, 0, t_k), 1))
        self.flush()
        drive((proj(2, "cross_wq_2", 0, xa, self.t_xT, 4, gx), 1), (prologue(1, 2, kT, 1, t_k), 1))
        drive((proj(3, "cross_wq_2", 1, xa, self.t_xT, 4, gx), 1), (prologue(2, 4, qT, 0, t_q[0]), 1))
        drive((self.chain(lambda: values(0), lambda: values(1)), 2), (prologue(3, 4, qT, 1, t_q[1]), 1))
        keep = {t: [] for t in range(NT)}
        free0 = self.snap()

        def put(t, c, o, toks):
            self.turn_split(o, 4, toks, self.ah, self.al, 4 * c, t, keep[t], self.a_free)

        drive((self.attend(
            range(4), 256,
            lambda h, t, k0, k1: [(qT[:, 2 * h + q, t * 128:t * 128 + 128], kT[:, 2 * h + q, :]) for q in range(2)],
            lambda t: (0, 2), lambda h, k: vm[:, k, h * 256:h * 256 + 256], 256 ** -0.5, [t_k, t_v, t_q], free0,
            pb, ptb, ob, put, wide=256), 1))
        self.free_ar = self.snap()
        self.resid2(8, lambda hf: self.cols("cross_wo_2", l, hf * 512, hf * 512 + 512), (self.ah, self.al, 0), keep)

    def ffn2(self, l):
        V, A, G, T = self.V, self.A, self.G, self.T
        hold = self.free_ar
        xa = (self.xh, self.xl, 0)
        bufs = [self.u(q * 512, 512) for q in range(6)]
        b_free = [hold] * 6
        nb = 0
        keep = [{}, {}]

        def up(m):
            res = {}
            half = int(m >= 10)

            def ev(o, i, ap, tok):
                nonlocal nb
                if o < 2:
                    s = nb % 6
                    nb += 1
                    r = self.act(bufs[s], ap, ACT.Silu, tok, b_free[s])
                    self.give(i, r)
                    res[o] = (r, s)
                else:
                    r0, s = res[o - 2]
                    r = self.tt(V, bufs[s], bufs[s], ap, ALU.mult, tok, r0)
                    self.give(i, r)
                    k = (m + o - 2) if m < 12 else m - 12 + o - 2
                    w = self.split(self.ah[:, k, :], self.al[:, k, :], bufs[s], r, self.a_free)
                    b_free[s] = w
                    keep[half][m + o - 2 - 10 * half] = w
            pieces = (("ffn_w_gate_2", l, m * 128, m * 128 + 256), ("ffn_w_up_2", l, m * 128, m * 128 + 256))
            return self.gemm(8, pieces, xa, self.t_xT, "F", 4, ev, gain=("n_ffn", l * 8), pair=m == 0)
        norm = self.rms_turn(self.xn_slots()) if l < DEPTH - 1 else None
        self.ffn_order(up, "ffn_w_down_2", l, keep, norm, None, False)

    def emit(self):
        nc = self.nc
        sems = [self.ctx.enter_context(nc.semaphore(f"s{i}")) for i in range(self.nsem)]
        block = self.ctx.enter_context(nc.Block())
        for name, lane in (("tensor", self.T), ("vector", self.V), ("scalar", self.A), ("gpsimd", self.G),
                           ("sync", self.Y)):
            reg = {"tensor": block.tensor, "vector": block.vector, "scalar": block.scalar,
                   "gpsimd": block.gpsimd, "sync": block.sync}[name]
            reg(lambda eng, lane=lane: lane.play(eng, sems))
        self.ctx.close()


def new_program(nc, ins, out, plan):
    p = Program(nc, ins, out, plan)
    p.a_free = None
    p.x_free = None
    p.build()
    return p


def tables():
    c = np.zeros((128, NCST), np.float32)

    def put(name, a):
        at, n = CST[name]
        c[:, at:at + n] = a
    put("ident", np.eye(128))
    put("ones", 1.0)
    i, j = np.arange(128)[:, None], np.arange(384)[None, :]
    put("band", np.where((j >= i) & (j <= i + 256), 0.0, BIG))
    put("causal", np.where(np.arange(128)[None, :] <= i, 0.0, BIG))

    def angles(pos, half, theta, d):
        inv = np.float32(theta) ** (-np.arange(half, dtype=np.float32) * np.float32(2.0 / d))
        return pos.astype(np.float32)[:, None] * inv[None, :].astype(np.float32)

    def table(cn, sn, ang):
        n = ang.shape[1]
        for name, f in ((cn, np.cos), (sn, np.sin)):
            put(name, f(ang).astype(np.float32).reshape(NT, 128, n).transpose(1, 0, 2).reshape(128, NT * n))
    pos = np.arange(S)
    table("cosA", "sinA", angles(pos, 32, 10000.0, 64))
    table("cosB", "sinB", np.concatenate([angles(pos // 64, 16, 10000.0, 32), angles(pos % 64, 16, 10000.0, 32)], 1))
    table("cosq", "sinq", angles(pos, 16, 500000.0, 32))
    table("cosi", "sini", angles(pos, 8, 500000.0, 16))
    pw = np.full((128, 16), -0.5)
    pw[:, 15] = 0.5
    put("pw", pw)
    t = np.arange(16)
    put("invc", np.concatenate([1.0 / np.minimum(t + 1, w) for w in POOL_W])[None, :])
    return c


_SHAPES = {"x": (S, D), "mem_2": (256, D), "xT": (128, 8 * S), "memT": (128, 2048), "mem_2T": (128, 2048),
           "c_bs": (2, 512), "wsT": (2, 128, 512), "pool_w_2": (4, 128, 128), "par": (128, NPAR),
           "cst": (128, NCST), "a_sink": (2, 8), "b_q_gain": (2, 64), "b_k_gain": (2, 64), "c_ln_g": (2, 512),
           "c_ln_b": (2, 512), "a_q_norm_2": (1, 128), "a_k_norm_2": (1, 128), "cross_q_norm_2": (2, 256),
           "cross_k_norm_2": (2, 256), "ln1_g": (2, D), "ln1_b": (2, D), "ln2_g": (2, D), "ln2_b": (2, D),
           "ln3_g": (2, D), "ln3_b": (2, D)}


def the_plan(nc):
    ins = {k: nc.dram_tensor("p_" + k, v, F32, kind="ExternalInput").ap() for k, v in _SHAPES.items()}
    out = nc.dram_tensor("p_out", (S, D), F32, kind="ExternalOutput").ap()
    p = new_program(nc, ins, out, None)
    p.ctx.close()
    return p.units


_INS = ["ln1_g", "ln1_b", "ln2_g", "ln2_b", "ln3_g", "ln3_b", "a_sink", "b_q_gain", "b_k_gain", "c_ln_g", "c_ln_b",
        "a_q_norm_2", "a_k_norm_2", "cross_q_norm_2", "cross_k_norm_2"]


def lay_out(inputs, plan):
    g = {k: np.asarray(v) for k, v in inputs.items()}
    a = {k: np.ascontiguousarray(g[k]) for k in _INS}
    a["x"] = np.ascontiguousarray(g["x"][0])
    a["mem_2"] = np.ascontiguousarray(g["mem_2"][0])

    def feature_major(m):
        n = m.shape[0]
        return np.ascontiguousarray(m.T.reshape(8, 128, n).transpose(1, 0, 2).reshape(128, 8 * n))
    a["xT"] = feature_major(g["x"][0])
    a["memT"] = feature_major(g["mem"][0])
    a["mem_2T"] = feature_major(g["mem_2"][0])
    a["c_bs"] = np.ascontiguousarray(g["c_bs"].reshape(2, 512))
    a["wsT"] = np.ascontiguousarray(g["c_ws"].transpose(0, 3, 1, 2).reshape(2, 128, 512))
    a["pool_w_2"] = np.ascontiguousarray(g["pool_w_2"][0])
    par = np.zeros((128, NPAR), np.float32)

    def put(name, m):
        at, n = PAR[name]
        par[:, at:at + n] = m

    def cols(m):
        m = m.reshape(-1, 128)
        return m.T
    put("b_gate", cols(g["b_gate"]))
    put("conv_k", cols(g["f_conv_k"]))
    put("conv_b", cols(g["f_conv_b"]))
    put("pool_scale", cols(g["pool_scale_2"]))
    put("cv_bin", cols(g["conv_b_in_2"]))
    put("dw_w", g["conv_dw_w_2"][0].reshape(31, 8, 128).transpose(2, 1, 0).reshape(128, 248))
    put("dw_b", cols(g["conv_dw_b_2"]))
    put("cln_g", cols(g["conv_ln_g_2"]))
    put("cln_b", cols(g["conv_ln_b_2"]))
    for n, k in (("n_mix", "norm_mix_2"), ("n_cross", "norm_cross_2"), ("n_mem", "norm_mem_2"), ("n_ffn", "norm_ffn_2")):
        put(n, cols(g[k]))
    a["par"] = par
    a["cst"] = tables()
    pk = np.zeros((len(plan), 128, 1024), np.float32)
    for j, (k0, nk, pieces, _) in enumerate(plan):
        at = 0
        width = sum(p[3] - p[2] for p in pieces)
        dst = pk[j, :, 0:nk * width].reshape(128, nk, width)
        for name, idx, c0, c1 in pieces:
            w, r0 = g[name], 0
            if isinstance(idx, tuple):
                if "down" in name:
                    w, r0 = w[idx[0]], idx[1] * 128
                else:
                    w = w[idx[0]][idx[1]]
            else:
                w = w[idx]
            r = r0 + k0 * 128
            dst[:, :, at:at + c1 - c0] = w[r:r + nk * 128, c0:c1].reshape(nk, 128, c1 - c0).transpose(1, 0, 2)
            at += c1 - c0
    a["wpk"] = pk
    return a


def kernel(**inputs):
    import concourse.bacc as _bacc
    from concourse import mybir as _mybir
    from concourse.bass_utils import run_bass_kernel_spmd as _run

    plan = the_plan(_bacc.Bacc("TRN2", target_bir_lowering=False, num_devices=1))
    arrays = lay_out(inputs, plan)
    nc = _bacc.Bacc("TRN2", target_bir_lowering=False, num_devices=1)
    ins = {k: nc.dram_tensor("in_" + k, v.shape, _mybir.dt.float32, kind="ExternalInput").ap()
           for k, v in arrays.items()}
    out = nc.dram_tensor("out_0", (S, D), _mybir.dt.float32, kind="ExternalOutput").ap()
    new_program(nc, ins, out, plan).emit()
    r = _run(nc, [{"in_" + k: v for k, v in arrays.items()}], core_ids=[0])
    return r.results[0]["out_0"].reshape(1, S, D)
```
